# Optimizing a Trainium2 kernel written in Bass

```python
import math
import jax, jax.numpy as jnp
from jax import lax
import numpy as np

D_MODEL = 1024
BATCH = 1
SEQ = 1024
DEPTH = 1
DEC_BATCH = 8
DEC_SEQ = 1
PAST_LEN = 2048
PAGE_SIZE = 128

HEAD_DIM = 64
HEADS_PER_GROUP = 8
WINDOWS = (128, 512, 2048)
DILATIONS = (1, 4, 16)
N_GROUPS = 3
ATTN_WIDTH = N_GROUPS * HEADS_PER_GROUP * HEAD_DIM
ATTN_OUT = HEADS_PER_GROUP * HEAD_DIM
ROT_DIM = HEAD_DIM // 4
ROPE_THETA = 500000.0
MLSTM_HEADS = 8
MLSTM_DQK = 64
MLSTM_DV = 128
MLSTM_QK_WIDTH = MLSTM_HEADS * MLSTM_DQK
MLSTM_V_WIDTH = MLSTM_HEADS * MLSTM_DV
MLSTM_CHUNK = 64
D_FF = -(-8 * D_MODEL // (3 * 256)) * 256
NORM_EPS = 1e-6
SPLITS = (ATTN_WIDTH, ATTN_WIDTH, ATTN_WIDTH, MLSTM_QK_WIDTH, MLSTM_QK_WIDTH,
          MLSTM_V_WIDTH, MLSTM_V_WIDTH, 2 * MLSTM_HEADS, D_MODEL, D_MODEL)
D_IN = sum(SPLITS)

kernel_name = "hybrid_dilated_swa_mlstm_step"

def _rmsnorm(x, g):
    xf = x.astype(jnp.float32)
    y = xf * lax.rsqrt(jnp.mean(xf * xf, axis=-1, keepdims=True) + NORM_EPS)
    return (y * g.astype(jnp.float32)).astype(x.dtype)

def _rope_partial(x, pos):
    half = ROT_DIM // 2
    inv_freq = jnp.exp(-math.log(ROPE_THETA) * jnp.arange(0, ROT_DIM, 2, dtype=jnp.float32) / ROT_DIM)
    ang = pos[:, None] * inv_freq[None, :]
    cos = jnp.cos(ang)[None, :, None, :]
    sin = jnp.sin(ang)[None, :, None, :]
    xf = x.astype(jnp.float32)
    x1, x2, rest = xf[..., :half], xf[..., half:ROT_DIM], xf[..., ROT_DIM:]
    out = jnp.concatenate([x1 * cos - x2 * sin, x2 * cos + x1 * sin, rest], axis=-1)
    return out.astype(x.dtype)

def _project(x, pos, norm1_g, w_in, b_if, q_norm_g, k_norm_g):
    B, T, _ = x.shape
    h = _rmsnorm(x, norm1_g)
    z = jnp.einsum('btd,de->bte', h, w_in)
    offs = np.cumsum(SPLITS)[:-1].tolist()
    qa, ka, va, qm, km, vm, om, gif, ga, gb = jnp.split(z, offs, axis=-1)
    nh = N_GROUPS * HEADS_PER_GROUP
    qa = _rope_partial(_rmsnorm(qa.reshape(B, T, nh, HEAD_DIM), q_norm_g), pos)
    ka = _rope_partial(_rmsnorm(ka.reshape(B, T, nh, HEAD_DIM), k_norm_g), pos)
    va = va.reshape(B, T, nh, HEAD_DIM)
    grp = lambda a: a.reshape(B, T, N_GROUPS, HEADS_PER_GROUP, HEAD_DIM)
    qm = qm.reshape(B, T, MLSTM_HEADS, MLSTM_DQK) * (MLSTM_DQK ** -0.5)
    km = km.reshape(B, T, MLSTM_HEADS, MLSTM_DQK)
    vm = vm.reshape(B, T, MLSTM_HEADS, MLSTM_DV)
    gif = gif.astype(jnp.float32) + b_if.astype(jnp.float32)
    ig = gif[..., :MLSTM_HEADS]
    lf = jax.nn.log_sigmoid(gif[..., MLSTM_HEADS:])
    return grp(qa), grp(ka), grp(va), qm, km, vm, om, ig, lf, ga, gb

def _to_residues(a, d):
    B, S = a.shape[:2]
    rest = a.shape[2:]
    return a.reshape(B, S // d, d, *rest).swapaxes(1, 2).reshape(B * d, S // d, *rest)

def _from_residues(a, d, B):
    N, L = a.shape[:2]
    rest = a.shape[2:]
    return a.reshape(B, d, L, *rest).swapaxes(1, 2).reshape(B, L * d, *rest)

def _banded_causal_attention(q, k, v, span):
    N, L, H, Dh = q.shape
    blk = span
    nb = -(-L // blk)
    pad = nb * blk - L
    padf = lambda a: jnp.pad(a.astype(jnp.float32), ((0, 0), (0, pad), (0, 0), (0, 0))).reshape(N, nb, blk, H, Dh)
    qb, kb, vb = padf(q), padf(k), padf(v)

    def with_prev(a):
        prev = jnp.pad(a[:, :-1], ((0, 0), (1, 0), (0, 0), (0, 0), (0, 0)))
        return jnp.concatenate([prev, a], axis=2)

    kk, vv = with_prev(kb), with_prev(vb)
    s = jnp.einsum('nbqhd,nbkhd->nbhqk', qb, kk) * (Dh ** -0.5)
    qi = jnp.arange(blk)[:, None]
    ki = jnp.arange(2 * blk)[None, :]
    dist = qi + blk - ki
    band = (dist >= 0) & (dist <= span)
    not_before_start = (ki >= blk)[None] | (jnp.arange(nb)[:, None, None] > 0)
    mask = band[None] & not_before_start
    s = jnp.where(mask[None, :, None], s, -jnp.inf)
    lse = jax.nn.logsumexp(s, axis=-1)
    p = jnp.exp(s - lse[..., None])
    o = jnp.einsum('nbhqk,nbkhd->nbqhd', p, vv).reshape(N, nb * blk, H, Dh)[:, :L]
    lse = lse.transpose(0, 1, 3, 2).reshape(N, nb * blk, H)[:, :L]
    return o, lse

def _combine_groups(outs, lses):
    w = jax.nn.softmax(jnp.stack(lses, axis=0), axis=0)
    return jnp.einsum('gbth,gbthd->bthd', w, jnp.stack(outs, axis=0))

def _prompt_attention(qa, ka, va):
    B, S = qa.shape[:2]
    outs, lses, kvs = [], [], []
    for g in range(N_GROUPS):
        d = DILATIONS[g]
        span = WINDOWS[g] // d
        o, lse = _banded_causal_attention(_to_residues(qa[:, :, g], d), _to_residues(ka[:, :, g], d),
                                          _to_residues(va[:, :, g], d), span)
        outs.append(_from_residues(o, d, B))
        lses.append(_from_residues(lse, d, B))
        keep = min(WINDOWS[g], S)
        kvs.append(jnp.stack([ka[:, S - keep:, g], va[:, S - keep:, g]], axis=2))
    return _combine_groups(outs, lses), kvs

def _sample_attention(qa, ka, va, caches):
    T = qa.shape[1]
    outs, lses, kvs = [], [], []
    for g in range(N_GROUPS):
        d = DILATIONS[g]
        span = WINDOWS[g] // d
        cache = caches[g]
        wb = cache.shape[1]
        kvc = jnp.concatenate([cache, jnp.stack([ka[:, :, g], va[:, :, g]], axis=2).astype(cache.dtype)], axis=1)
        idx = wb + jnp.arange(T)[:, None] - jnp.arange(span + 1)[None, :] * d
        valid = idx >= 0
        kvg = jnp.take(kvc, jnp.clip(idx, 0, None), axis=1).astype(jnp.float32)
        s = jnp.einsum('bthd,btjhd->bthj', qa[:, :, g].astype(jnp.float32), kvg[:, :, :, 0]) * (HEAD_DIM ** -0.5)
        s = jnp.where(valid[None, :, None, :], s, -jnp.inf)
        lse = jax.nn.logsumexp(s, axis=-1)
        p = jnp.exp(s - lse[..., None])
        outs.append(jnp.einsum('bthj,btjhd->bthd', p, kvg[:, :, :, 1]))
        lses.append(lse)
        kvs.append(kvc[:, kvc.shape[1] - wb:])
    return _combine_groups(outs, lses), kvs

def _mlstm_chunk(carry, inputs):
    C, n, m = (c.astype(jnp.float32) for c in carry)
    q, k, v, ig, lf = inputs
    q, k, v = q.astype(jnp.float32), k.astype(jnp.float32), v.astype(jnp.float32)
    L = q.shape[1]
    b = jnp.cumsum(lf, axis=1)
    tri = jnp.tril(jnp.ones((L, L), dtype=bool))
    D = b[:, :, None, :] - b[:, None, :, :] + ig[:, None, :, :]
    D = jnp.where(tri[None, :, :, None], D, -jnp.inf)
    inter = b + m[:, None, :]
    m_t = jnp.maximum(inter, jnp.max(D, axis=2))
    w = jnp.exp(D - m_t[:, :, None, :])
    wqk = w * jnp.einsum('bthd,bshd->btsh', q, k)
    dec = jnp.exp(inter - m_t)
    num = dec[..., None] * jnp.einsum('bthd,bhde->bthe', q, C) + jnp.einsum('btsh,bshe->bthe', wqk, v)
    den = dec * jnp.einsum('bthd,bhd->bth', q, n) + jnp.sum(wqk, axis=2)
    h = num / jnp.maximum(jnp.abs(den), jnp.exp(-m_t))[..., None]
    m_new = m_t[:, -1]
    dstate = jnp.exp(b[:, -1] + m - m_new)
    ws = jnp.exp(b[:, -1:, :] - b + ig - m_new[:, None, :])
    C_new = dstate[..., None, None] * C + jnp.einsum('bsh,bshd,bshe->bhde', ws, k, v)
    n_new = dstate[..., None] * n + jnp.einsum('bsh,bshd->bhd', ws, k)
    return (C_new, n_new, m_new), h

def _mlstm_prompt(q, k, v, ig, lf):
    B, S = q.shape[:2]
    nc = S // MLSTM_CHUNK
    ch = lambda a: a.reshape(B, nc, MLSTM_CHUNK, *a.shape[2:]).swapaxes(0, 1)
    init = (jnp.zeros((B, MLSTM_HEADS, MLSTM_DQK, MLSTM_DV), jnp.float32),
            jnp.zeros((B, MLSTM_HEADS, MLSTM_DQK), jnp.float32),
            jnp.zeros((B, MLSTM_HEADS), jnp.float32))
    state, hs = lax.scan(_mlstm_chunk, init, (ch(q), ch(k), ch(v), ch(ig), ch(lf)))
    return state, hs.swapaxes(0, 1).reshape(B, S, MLSTM_HEADS, MLSTM_DV)

def _merge_and_ffn(x, o_att, h_m, om, ga, gb, w_att_out, w_m_out, w_o, norm2_g, w_gate, w_up, w_down):
    B, T, _ = x.shape
    ya = jnp.einsum('bte,ed->btd', o_att.reshape(B, T, ATTN_OUT).astype(x.dtype), w_att_out)
    hm = jax.nn.sigmoid(om) * h_m.reshape(B, T, MLSTM_V_WIDTH).astype(x.dtype)
    yb = jnp.einsum('bte,ed->btd', hm, w_m_out)
    mixed = jax.nn.sigmoid(ga) * ya + jax.nn.sigmoid(gb) * yb
    x = x + jnp.einsum('btd,de->bte', mixed, w_o)
    h = _rmsnorm(x, norm2_g)
    ff = jax.nn.silu(jnp.einsum('btd,df->btf', h, w_gate)) * jnp.einsum('btd,df->btf', h, w_up)
    return x + jnp.einsum('btf,fd->btd', ff, w_down)

def setup_inputs(seed: int = 0) -> dict:
    key = jax.random.key(seed)
    ks = jax.random.split(key, 24)
    f = jnp.float32
    nrm = jax.random.normal
    return {
        "x_prompt": nrm(ks[0], (BATCH, SEQ, D_MODEL), f),
        "x_sample": nrm(ks[1], (DEC_BATCH, DEC_SEQ, D_MODEL), f),
        "cache_kv_w128": nrm(ks[2], (DEC_BATCH, min(WINDOWS[0], PAST_LEN), 2, HEADS_PER_GROUP, HEAD_DIM), f),
        "cache_kv_w512": nrm(ks[3], (DEC_BATCH, min(WINDOWS[1], PAST_LEN), 2, HEADS_PER_GROUP, HEAD_DIM), f),
        "cache_kv_w2048": nrm(ks[4], (DEC_BATCH, min(WINDOWS[2], PAST_LEN), 2, HEADS_PER_GROUP, HEAD_DIM), f),
        "state_mlstm_C": 0.5 * nrm(ks[5], (DEC_BATCH, MLSTM_HEADS, MLSTM_DQK, MLSTM_DV), f),
        "state_mlstm_n": 0.5 * nrm(ks[6], (DEC_BATCH, MLSTM_HEADS, MLSTM_DQK), f),
        "state_mlstm_m": nrm(ks[7], (DEC_BATCH, MLSTM_HEADS), f),
        "norm1_g": 1.0 + 0.1 * nrm(ks[8], (D_MODEL,), f),
        "w_in": nrm(ks[9], (D_MODEL, D_IN), f) * D_MODEL ** -0.5,
        "b_if": jnp.concatenate([0.1 * nrm(ks[10], (MLSTM_HEADS,), f),
                                 3.0 + 0.1 * nrm(ks[11], (MLSTM_HEADS,), f)]),
        "q_norm_g": 1.0 + 0.1 * nrm(ks[12], (HEAD_DIM,), f),
        "k_norm_g": 1.0 + 0.1 * nrm(ks[13], (HEAD_DIM,), f),
        "w_att_out": nrm(ks[14], (ATTN_OUT, D_MODEL), f) * ATTN_OUT ** -0.5,
        "w_m_out": nrm(ks[15], (MLSTM_V_WIDTH, D_MODEL), f) * MLSTM_V_WIDTH ** -0.5,
        "w_o": nrm(ks[16], (D_MODEL, D_MODEL), f) * D_MODEL ** -0.5,
        "norm2_g": 1.0 + 0.1 * nrm(ks[17], (D_MODEL,), f),
        "w_gate": nrm(ks[18], (D_MODEL, D_FF), f) * D_MODEL ** -0.5,
        "w_up": nrm(ks[19], (D_MODEL, D_FF), f) * D_MODEL ** -0.5,
        "w_down": nrm(ks[20], (D_FF, D_MODEL), f) * D_FF ** -0.5,
    }

def reference(x_prompt, x_sample, cache_kv_w128, cache_kv_w512, cache_kv_w2048,
              state_mlstm_C, state_mlstm_n, state_mlstm_m,
              norm1_g, w_in, b_if, q_norm_g, k_norm_g, w_att_out, w_m_out, w_o,
              norm2_g, w_gate, w_up, w_down):
    S = x_prompt.shape[1]
    T = x_sample.shape[1]
    pos_p = jnp.arange(S, dtype=jnp.float32)
    qa, ka, va, qm, km, vm, om, ig, lf, ga, gb = _project(x_prompt, pos_p, norm1_g, w_in, b_if, q_norm_g, k_norm_g)
    o_att_p, kv_p = _prompt_attention(qa, ka, va)
    (C_p, n_p, m_p), h_p = _mlstm_prompt(qm, km, vm, ig, lf)
    y_prompt = _merge_and_ffn(x_prompt, o_att_p, h_p, om, ga, gb, w_att_out, w_m_out, w_o,
                              norm2_g, w_gate, w_up, w_down)
    pos_s = jnp.arange(T, dtype=jnp.float32) + PAST_LEN
    qa_s, ka_s, va_s, qm_s, km_s, vm_s, om_s, ig_s, lf_s, ga_s, gb_s = _project(
        x_sample, pos_s, norm1_g, w_in, b_if, q_norm_g, k_norm_g)
    o_att_s, kv_s = _sample_attention(qa_s, ka_s, va_s, (cache_kv_w128, cache_kv_w512, cache_kv_w2048))
    (C_s, n_s, m_s), h_s = _mlstm_chunk((state_mlstm_C, state_mlstm_n, state_mlstm_m),
                                        (qm_s, km_s, vm_s, ig_s, lf_s))
    y_sample = _merge_and_ffn(x_sample, o_att_s, h_s, om_s, ga_s, gb_s, w_att_out, w_m_out, w_o,
                              norm2_g, w_gate, w_up, w_down)
    return (y_prompt, y_sample, kv_p[0], kv_p[1], kv_p[2], C_p, n_p, m_p,
            kv_s[0], kv_s[1], kv_s[2], C_s, n_s, m_s)


_drawn_inputs = setup_inputs


def setup_inputs(seed=0):
    import zlib

    import numpy as np

    out = dict(_drawn_inputs(seed))
    spreads = {}
    factors = {'q_norm_g': 8.0}
    for name, (base, spread) in spreads.items():
        noise = np.random.default_rng([zlib.crc32(name.encode()), seed]).standard_normal(out[name].shape)
        drawn = base * np.exp(spread * noise) if base else spread * noise
        out[name] = __import__('jax').numpy.asarray(drawn.astype(out[name].dtype))
    for name, factor in factors.items():
        out[name] = (out[name] * factor).astype(out[name].dtype)
    return out
```

```python
import math
from contextlib import ExitStack

import concourse.bass as bass
from concourse import mybir

F32 = mybir.dt.float32
F32R = mybir.dt.float32r
ALU = mybir.AluOpType
ACT = mybir.ActivationFunctionType
AX = mybir.AxisListType

P = 128
D = 1024
S = 1024
NB = 8
T = S + NB
SEG = T // 3
KD = D // P
NT = S // P
H = 8
DH = 64
DV = 128
G = 3
WINDOWS = (128, 512, 2048)
DILS = (1, 4, 16)
AW = G * H * DH
DFF = 2816
EPS = 1e-6
NEG = -1e30
SCALE = DH ** -0.5
CQM, CKM, CVM, COM = 3 * AW, 3 * AW + 512, 3 * AW + 1024, 3 * AW + 2048
CIF = COM + 1024
CGA, CGB = CIF + 16, CIF + 16 + 1024
CW = 512
RAW = 3
RING = 12
PAST = 2048


def bc(ap, shape):
    return ap.unsqueeze(len(shape) - 1).to_broadcast(shape)


STEPS = tuple(min(d, S // P) for d in DILS)


def residues(ap, g, n):
    length = S // STEPS[g]
    r, i = n * P // length, n * P % length
    if len(ap.shape) == 2:
        return ap.rearrange("p (i d) -> p d i", d=STEPS[g])[:, r, i:i + P]
    return ap.rearrange("p k (i d) -> p k d i", d=STEPS[g])[:, :, r, i:i + P]


def token_rows(ap, g, n):
    length = S // STEPS[g]
    return ap.rearrange("(i d) c -> d i c", d=STEPS[g])[n * P // length, n * P % length:n * P % length + P, :]


def has_prev(g, n):
    return n * P % (S // STEPS[g]) != 0


class Chain:

    def __init__(self, eng, sem):
        self.eng, self.sem, self.n = eng, sem, 0

    def mark(self, ins):
        self.n += 1
        ins.then_inc(self.sem, 1)
        return self.n

    def wait(self, n=None):
        self.eng.wait_ge(self.sem, self.n if n is None else n)

    def link(self, ins):
        self.mark(ins)
        self.wait()


def weight_pieces(t):
    w_in = t["w_in"]
    cols = [x * AW + g * 512 for g in range(G) for x in range(3)] + [CQM, CKM, CVM, CVM + 512]
    cols += [COM, COM + 512, CGA, CGA + 512, CGB, CGB + 512]
    out = [[(w_in[k * P:(k + 1) * P, c:c + CW], 0)] for c in cols for k in range(KD)]
    for name, nk in (("w_att_out", 4), ("w_m_out", KD), ("w_o", KD)):
        out += [[(t[name][k * P:(k + 1) * P, c:c + CW], 0)] for c in (0, CW) for k in range(nk)]
    down = []
    for j in range(DFF // 256):
        out += [[(t["w_gate"][k * P:(k + 1) * P, j * 256:(j + 1) * 256], 0),
                 (t["w_up"][k * P:(k + 1) * P, j * 256:(j + 1) * 256], 256)] for k in range(KD)]
        out += down
        down = [[(t["w_down"][(2 * j + k) * P:(2 * j + k + 1) * P, c:c + CW], 0)] for c in (0, CW) for k in range(2)]
    out += down
    return out


def cache_copies(t, o):
    out = []
    for g, w in enumerate(WINDOWS):
        cache = t[f"cache_kv_w{w}"].rearrange("b w a h c -> b (w a h c)")
        new = o[8 + g].rearrange("b w a h c -> b (w a h c)")
        row = 2 * H * DH
        for b in range(NB):
            for r in range(0, w - 1, P):
                n = min(P, w - 1 - r) * row
                src = cache[b, (r + 1) * row:(r + 1) * row + n].rearrange("(a c) -> a c", a=16)
                out.append((new[b, r * row:r * row + n].rearrange("(a c) -> a c", a=16), src))
    return out


class Core:

    def __init__(self, nc, t, o, top):
        self.nc, self.t, self.o, self.top = nc, t, o, top
        self.phase = None
        sb, sem, dram = self.sb, self.sem, self.dram
        self.ps = top.enter_context(nc.psum_tensor("ps", [P, 8, 512], F32))

        self.pieces = weight_pieces(t)
        self.raw = sb("raw", [P, RAW, CW])
        self.whi = sb("whi", [P, RING, CW], F32R)
        self.wlo = sb("wlo", [P, RING, CW], F32R)
        self.raw_in = [sem(f"raw_in{i}") for i in range(RAW)]
        self.w_hi, self.w_lo, self.w_used = sem("w_hi"), sem("w_lo"), sem("w_used")
        self.landed, at = [], [0] * RAW
        for p, parts in enumerate(self.pieces):
            at[p % RAW] += 16 * len(parts)
            self.landed.append(at[p % RAW])
        self.loaded = self.split = self.taken = 0
        self.copies = cache_copies(t, o)
        self.copied = 0
        self.cache_out = sem("cache_out")

        names = [f"b_zout{g}_{i}" for g in range(G) for i in range(4)] + [f"b_out{g}" for g in range(G)]
        names += ["g_mout", "c_out", "s_rows", "r_out", "y_out0", "y_out1"]
        self.stores = {name: sem(name) for name in names}

        self.ident = sb("ident", [P, P])
        self.mask_pair = sb("mask_pair", [P, 2 * P])
        self.mask_halves = sb("mask_halves", [P, P])
        self.mask_later = sb("mask_later", [P, P])
        self.ones = sb("ones", [P, P])
        self.gq = sb("gq", [P, DH])
        self.gk = sb("gk", [P, DH])
        self.rope = sb("rope", [P, G, NT + 1, 32])
        self.mstat = sb("mstat", [P, G, NT, 2, H])

        self.z_s = dram("z_s", (G, 3, NB, 512))
        self.m_tok = dram("m_tok", (NT, P, 3, 512))
        self.m_tr = dram("m_tr", (2, NT, P, 512))
        self.zm_s = dram("zm_s", (NB, 2048))
        self.if_s = dram("if_s", (2, H, NB))
        self.o_grp = dram("o_grp", (G, NT, P, 512))
        self.ml_nat = dram("ml_nat", (G, S, 16))
        self.cf_nat = dram("cf_nat", (G, S, 8))
        self.h_mem = dram("h_mem", (KD, P, T))
        self.gates = dram("gates", (2 * KD, P, T))
        self.att_t = dram("att_t", (4, P, T))
        self.hm_t = dram("hm_t", (KD, P, T))

        self.dve = Chain(nc.vector, sem("dve_c"))
        self.act = Chain(nc.scalar, sem("act_c"))
        self.pool = Chain(nc.gpsimd, sem("pool_c"))

    def sem(self, name):
        handle = self.nc.alloc_semaphore(name=name)
        if self.phase is not None:
            self.phase.append(handle)
        return handle

    def store_sem(self, name):
        return self.stores[name]

    def clear_phase(self):
        nc, handles = self.nc, self.phase or []
        if handles:
            with nc.Block() as block:
                @block.gpsimd
                def _(pool):
                    for h in handles:
                        pool.sem_clear(h)
        for h in handles:
            nc.release_semaphore(h)
        self.phase = []

    def sb(self, name, shape, dt=F32, ctx=None):
        return (ctx or self.top).enter_context(self.nc.sbuf_tensor(name, shape, dt))

    def dram(self, name, shape):
        return self.nc.dram_tensor(name, shape, F32, kind="Internal").ap()

    def load_weights(self, until):
        sp = self.nc.sync
        for p in range(self.loaded, min(until + RAW, len(self.pieces))):
            if p >= RAW:
                sp.wait_ge(self.w_lo, p - RAW + 1)
            for src, c in self.pieces[p]:
                sp.dma_start(self.raw[:, p % RAW, c:c + src.shape[1]], src).then_inc(self.raw_in[p % RAW], 16)
            self.loaded = p + 1
            while self.copied < len(self.copies) * (p + 1) // len(self.pieces):
                dst, src = self.copies[self.copied]
                sp.dma_start(dst, src).then_inc(self.cache_out, 16)
                self.copied += 1

    def split_weights(self, until):
        pool = self.nc.gpsimd
        for p in range(self.split, min(until, len(self.pieces))):
            pool.wait_ge(self.raw_in[p % RAW], self.landed[p])
            if p >= RING:
                pool.wait_ge(self.w_used, p - RING + 1)
            pool.tensor_copy(self.whi[:, p % RING, :], self.raw[:, p % RAW, :]).then_inc(self.w_hi, 1)
            pool.wait_ge(self.w_hi, p + 1)
            pool.tensor_tensor(self.wlo[:, p % RING, :], self.raw[:, p % RAW, :],
                               self.whi[:, p % RING, :].bitcast(F32), ALU.subtract).then_inc(self.w_lo, 1)
            self.split = p + 1

    def weight(self, p, cols):
        return self.whi[:, p % RING, cols], self.wlo[:, p % RING, cols]


def products(nc, out, lhs, rhs, start, stop):
    nc.tensor.matmul(out, lhs[0], rhs[0], start=start, stop=False)
    nc.tensor.matmul(out, lhs[0], rhs[1], start=False, stop=False)
    return nc.tensor.matmul(out, lhs[1], rhs[0], start=False, stop=stop)


def norm_input(core):
    nc, t, ps, sem, sb = core.nc, core.t, core.ps, core.sem, core.sb
    ident, hhi, hlo = core.ident, core.hhi, core.hlo
    with ExitStack() as c:
        x_sb = sb("x_sb", [P, NT + 1, D], ctx=c)
        g1 = sb("g1", [P, D], ctx=c)
        sq_a = sb("sq_a", [P, 2, D], ctx=c)
        ssq = sb("ssq", [P, NT + 1], ctx=c)
        a_in = [sem(f"a_in{n}") for n in range(NT + 1)]
        a_g, a_const, a_ssq, a_var, a_std, a_xn = (sem(x) for x in ("a_g", "a_const", "a_ssq", "a_var", "a_std", "a_xn"))
        a_tr, a_hi, a_lo = sem("a_tr"), sem("a_hi"), sem("a_lo")
        c_in = sem("c_in")
        block = c.enter_context(nc.Block())

        @block.sync
        def _(sp):
            for n in range(NT):
                sp.dma_start(x_sb[:, n, :], t["x_prompt"][0, n * P:(n + 1) * P, :]).then_inc(a_in[n], 16)
            sp.dma_start(x_sb[0:NB, NT, :], t["x_sample"].rearrange("b s d -> (b s) d")).then_inc(a_in[NT], 16)
            sp.dma_start(g1[:], t["norm1_g"].rearrange("(a d) -> a d", a=1).to_broadcast([P, D])).then_inc(a_g, 16)
            sp.dma_start(core.gq[:], t["q_norm_g"].rearrange("(a d) -> a d", a=1).to_broadcast([P, DH])).then_inc(c_in, 16)
            sp.dma_start(core.mask_halves[:], t["mask_halves"]).then_inc(c_in, 16)
            sp.dma_start(core.gk[:], t["k_norm_g"].rearrange("(a d) -> a d", a=1).to_broadcast([P, DH])).then_inc(c_in, 16)
            for g in range(G):
                for n in range(NT):
                    sp.dma_start(core.rope[:, g, n, :], token_rows(t["rope_table"][0:S, :], g, n)).then_inc(c_in, 16)
                sp.dma_start(core.rope[0:NB, g, NT, :], t["rope_table"][S:S + 1, :].to_broadcast([NB, 32])).then_inc(c_in, 16)
            core.load_weights(8)
            sp.wait_ge(c_in, 16 * (3 + G * NT + G))

        @block.gpsimd
        def _(pool):
            ch = core.pool
            ch.link(pool.memset(ident[:], 0.0))
            ch.link(pool.affine_select(out=ident[:], in_=ident[:], compare_op=ALU.not_equal, fill=1.0, base=0,
                                       pattern=[[-1, P]], channel_multiplier=1))
            pool.memset(core.ones[:], 1.0).then_inc(a_const, 1)
            for m in (core.mask_pair, core.mask_later):
                ch.mark(pool.memset(m[:], 0.0))
            ch.wait()
            ch.mark(pool.affine_select(out=core.mask_pair[:, 0:P], in_=core.mask_pair[:, 0:P], compare_op=ALU.is_ge, fill=NEG,
                                       base=0, pattern=[[1, P]], channel_multiplier=-1))
            ch.mark(pool.affine_select(out=core.mask_pair[:, P:2 * P], in_=core.mask_pair[:, P:2 * P], compare_op=ALU.is_ge,
                                       fill=NEG, base=0, pattern=[[-1, P]], channel_multiplier=1))
            ch.mark(pool.affine_select(out=core.mask_later[:], in_=core.mask_later[:], compare_op=ALU.is_ge, fill=NEG,
                                       base=0, pattern=[[1, P]], channel_multiplier=-1))
            ch.wait()
            pool.memset(core.mstat[:], 0.0).then_inc(a_const, 1)
            core.split_weights(8)

        @block.scalar
        def _(act):
            ch = core.act
            for n in range(NT + 1):
                rows = P if n < NT else NB
                act.wait_ge(a_in[n], 16)
                if n == 0:
                    act.wait_ge(a_var, 1)
                if n >= 2:
                    ch.wait(ch.n - 1)
                ch.mark(nc.scalar.activation(sq_a[0:rows, n % 2, :], x_sb[0:rows, n, :], ACT.Square,
                                             accum_out=ssq[0:rows, n:n + 1]))
            ch.wait()
            nc.scalar.activation(ssq[0:1, 0:1], ssq[0:1, 0:1], ACT.Copy).then_inc(a_ssq, 1)
            act.wait_ge(a_var, 2)
            nc.scalar.activation(ssq[:], ssq[:], ACT.Sqrt).then_inc(a_std, 1)
            for u in range(2 * (NT + 1)):
                n, kk = divmod(u, 2)
                cols = P if n < NT else NB
                act.wait_ge(a_tr, u + 1)
                nc.scalar.activation(hhi[:, 4 * kk:4 * kk + 4, n * P:n * P + cols],
                                     ps[:, u % 4, :].rearrange("p (k c) -> p k c", k=4)[:, :, 0:cols],
                                     ACT.Copy).then_inc(a_hi, 1)

        @block.vector
        def _(dve):
            ch = core.dve
            nc.vector.memset(ssq[:], 1.0).then_inc(a_var, 1)
            dve.wait_ge(a_ssq, 1)
            nc.vector.tensor_scalar(ssq[:], ssq[:], 1.0 / D, EPS, ALU.mult, ALU.add).then_inc(a_var, 1)
            dve.wait_ge(a_std, 1)
            ch.link(nc.vector.reciprocal(ssq[:], ssq[:]))
            dve.wait_ge(a_g, 16)
            for n in range(NT + 1):
                rows = P if n < NT else NB
                nc.vector.scalar_tensor_tensor(x_sb[0:rows, n, :], x_sb[0:rows, n, :], ssq[0:rows, n:n + 1],
                                               g1[0:rows, :], ALU.mult, ALU.mult).then_inc(a_xn, 1)
            for u in range(2 * (NT + 1)):
                n, kk = divmod(u, 2)
                cols = P if n < NT else NB
                dve.wait_ge(a_hi, u + 1)
                part = slice(4 * kk, 4 * kk + 4), slice(n * P, n * P + cols)
                nc.vector.tensor_tensor(hlo[:, part[0], part[1]],
                                        ps[:, u % 4, :].rearrange("p (k c) -> p k c", k=4)[:, :, 0:cols],
                                        hhi[:, part[0], part[1]].bitcast(F32), ALU.subtract).then_inc(a_lo, 1)

        @block.tensor
        def _(pe):
            pe.wait_ge(a_const, 1)
            for u in range(2 * (NT + 1)):
                n, kk = divmod(u, 2)
                rows = P if n < NT else NB
                pe.wait_ge(a_xn, n + 1)
                if u >= 4:
                    pe.wait_ge(a_lo, u - 3)
                for k in range(4):
                    last = nc.tensor.transpose(ps[:, u % 4, k * P:k * P + rows],
                                               x_sb[0:rows, n, (4 * kk + k) * P:(4 * kk + k + 1) * P],
                                               ident[0:rows, 0:rows])
                last.then_inc(a_tr, 1)



def project_attention(core, g):
    nc, o, ps, sem, sb, Z = core.nc, core.o, core.ps, core.sem, core.sb, 4
    hhi, hlo, ident, z_s, rope = core.hhi, core.hlo, core.ident, core.z_s, core.rope
    qT, kT, vv = core.qT, core.kT, core.vv
    UN = 3 * (NT + 1)
    NQ = 2 * (NT + 1)
    keep = min(WINDOWS[g], S)
    kv_out = o[2 + g][0]
    p0 = core.taken
    core.taken += 3 * KD
    with ExitStack() as c:
        zt = sb(f"zt{g}", [P, Z, 512], ctx=c)
        vs = sb(f"vs{g}", [NB, 512], ctx=c)
        sq = sb(f"sq{g}", [P, 512], ctx=c)
        st = sb(f"st{g}", [P, Z, H], ctx=c)
        rt = sb(f"rt{g}", [P, 2, H, 16], ctx=c)
        mm, ev, var, std, nrm, tr, tre = (sem(f"b_{x}{g}") for x in
                                                ("mm", "ev", "var", "std", "nrm", "tr", "tre"))
        zout = [core.store_sem(f"b_zout{g}_{i}") for i in range(Z)]
        out0 = core.store_sem(f"b_out{g}")
        block = c.enter_context(nc.Block())

        def stores(u):
            x, n = divmod(u, NT + 1)
            if n == NT:
                return [(slice(0, NB), z_s[g, x])]
            if x == 0:
                return []
            lst = []
            rows = kv_out[:, x - 1].rearrange("(i d) h c -> d i (h c)", d=STEPS[g])
            if keep == S or (n + 1) * P % (S // STEPS[g]) == 0:
                lst.append((slice(0, P), rows[n * P // (S // STEPS[g])]))
            return lst

        n_out = [0] * Z
        done_at = {}
        for u in range(NQ):
            for _ in stores(u):
                n_out[u % Z] += 16
            done_at[u] = n_out[u % Z]

        @block.sync
        def _(sp):
            core.load_weights(core.taken + 8)

        @block.gpsimd
        def _(pool):
            core.split_weights(core.taken + 8)

        @block.tensor
        def _(pe):
            def turn(u):
                pe.wait_ge(nrm, u + 1)
                if u >= 2:
                    pe.wait_ge(tre, u - 1 - (u - 1) // (NT + 1))
                for j in range(4):
                    last = nc.tensor.transpose(ps[:, 4 + u % 2, j * P:(j + 1) * P], zt[:, u % Z, j * P:(j + 1) * P],
                                               ident[:])
                last.then_inc(tr, 1)

            for u in range(UN + 2):
                if u < UN:
                    x, n = divmod(u, NT + 1)
                    rows = P if n < NT else NB
                    if n == 0:
                        pe.wait_ge(core.w_lo, p0 + (x + 1) * KD)
                    if u >= 4:
                        pe.wait_ge(ev, u - 3)
                    for k in range(KD):
                        if n < NT:
                            lhs = [residues(h[:, k, 0:S], g, n) for h in (hhi, hlo)]
                        else:
                            lhs = [h[:, k, S:T] for h in (hhi, hlo)]
                        last = products(nc, ps[0:rows, u % 4, :], lhs, core.weight(p0 + x * KD + k, slice(0, CW)),
                                        k == 0, k == KD - 1)
                        if n == NT:
                            last.then_inc(core.w_used, 1)
                    if n < NT:
                        last.then_inc(mm, 1)
                if 2 <= u and u - 2 < NQ and (u - 2) % (NT + 1) < NT:
                    turn(u - 2)

        @block.scalar
        def _(act):
            transposed = kept = 0
            for u in range(UN + 2):
                if u < UN:
                    x, n = divmod(u, NT + 1)
                    rows = P if n < NT else NB
                    if n < NT:
                        act.wait_ge(mm, u + 1 - (u + 1) // (NT + 1))
                    else:
                        act.wait_ge(core.w_used, p0 + (x + 1) * KD)
                    if x == 2:
                        dst = vv[:, n, :] if n < NT else vs[:, :]
                    else:
                        if u >= Z:
                            v = u - Z
                            act.wait_ge(tr, v + 1 - (v + 1) // (NT + 1))
                            if done_at[v]:
                                act.wait_ge(zout[v % Z], done_at[v])
                        dst = zt[0:rows, u % Z, :]
                    nc.scalar.activation(dst, ps[0:rows, u % 4, :], ACT.Copy).then_inc(ev, 1)
                if 1 <= u <= NQ:
                    v = u - 1
                    rows = P if v % (NT + 1) < NT else NB
                    act.wait_ge(var, v + 1)
                    nc.scalar.activation(st[0:rows, v % Z, :], st[0:rows, v % Z, :], ACT.Sqrt).then_inc(std, 1)
                if u >= 2:
                    v = u - 2
                    x, n = divmod(v, NT + 1)
                    if v < NQ and n < NT:
                        transposed += 1
                        act.wait_ge(tr, transposed)
                        nc.scalar.activation((qT, kT)[x][:, :, n * P:(n + 1) * P],
                                             ps[:, 4 + v % 2, :].rearrange("p (j c) -> p j c", j=4),
                                             ACT.Copy).then_inc(tre, 1)
                    for rows, dst in stores(v):
                        if v < NQ:
                            act.wait_ge(nrm, v + 1)
                            act.dma_start(dst, zt[rows, v % Z, :]).then_inc(zout[v % Z], 16)
                        else:
                            act.wait_ge(ev, v + 1)
                            act.dma_start(dst, vs[:, :] if n == NT else vv[rows, n, :]).then_inc(out0, 16)
                            kept += 16
            for i in range(Z):
                if n_out[i]:
                    act.wait_ge(zout[i], n_out[i])
            act.wait_ge(out0, kept)

        @block.vector
        def _(dve):
            ch = core.dve
            for u in range(NQ + 1):
                if u < NQ:
                    rows = P if u % (NT + 1) < NT else NB
                    z = zt[0:rows, u % Z, :]
                    dve.wait_ge(ev, u + 1)
                    ch.link(nc.vector.tensor_tensor(sq[0:rows, :], z, z, ALU.mult))
                    ch.link(nc.vector.tensor_reduce(st[0:rows, u % Z, :], sq[0:rows, :].rearrange("p (h c) -> p h c", h=H),
                                                    AX.X, ALU.add))
                    nc.vector.tensor_scalar(st[0:rows, u % Z, :], st[0:rows, u % Z, :], 1.0 / DH, EPS, ALU.mult,
                                            ALU.add).then_inc(var, 1)
                if u >= 1:
                    v = u - 1
                    x, n = divmod(v, NT + 1)
                    rows = P if n < NT else NB
                    z = zt[0:rows, v % Z, :].rearrange("p (h c) -> p h c", h=H)
                    s = st[0:rows, v % Z, :]
                    dve.wait_ge(std, v + 1)
                    ch.link(nc.vector.reciprocal(s, s))
                    ch.link(nc.vector.tensor_tensor(z, z, bc(s, [rows, H, DH]), ALU.mult))
                    gain = (core.gq, core.gk)[x][0:rows, :].unsqueeze(1).to_broadcast([rows, H, DH])
                    ch.link(nc.vector.tensor_tensor(z, z, gain, ALU.mult))
                    tab = rope[0:rows, g, n, :].unsqueeze(1).to_broadcast([rows, H, 32])
                    r = rt[0:rows]
                    ch.mark(nc.vector.tensor_tensor(r[:, 0], z[:, :, 0:16], tab[:, :, 0:16], ALU.mult))
                    ch.mark(nc.vector.tensor_tensor(r[:, 1, :, 0:8], z[:, :, 8:16], tab[:, :, 16:24], ALU.mult))
                    ch.link(nc.vector.tensor_tensor(r[:, 1, :, 8:16], z[:, :, 0:8], tab[:, :, 24:32], ALU.mult))
                    nc.vector.tensor_tensor(z[:, :, 0:16], r[:, 0], r[:, 1], ALU.add).then_inc(nrm, 1)




def attend(core, g):
    nc, ps, sem, sb = core.nc, core.ps, core.sem, core.sb
    qT, kT, vv, ident = core.qT, core.kT, core.vv, core.ident
    items = [(n, hh) for n in range(NT) for hh in range(2)]
    W = len(items)

    def span(n):
        return 2 * P if has_prev(g, n) else P

    with ExitStack() as c:
        sc = sb(f"sc{g}", [P, 2, 4, 2 * P], ctx=c)
        pt = sb(f"pt{g}", [P, 4, 2 * P], ctx=c)
        nm = sb(f"nm{g}", [P, 2, 4], ctx=c)
        ot = sb(f"ot{g}", [P, 2, 512], ctx=c)
        qk, msk, neg, prb, ptr, pte_a, pte_v, pv, oev = (sem(f"t_{x}{g}") for x in
                                                    ("qk", "msk", "neg", "prb", "ptr", "pte_a", "pte_v", "pv", "oev"))
        o_out = [sem(f"t_out{g}_{i}") for i in range(2)]
        block = c.enter_context(nc.Block())

        def heads(hh):
            return [(4 * hh + 2 * i + par, par, i) for i in range(2) for par in range(2)]

        @block.sync
        def _(sp):
            core.load_weights(core.taken + 8)

        @block.tensor
        def _(pe):
            def scores(w):
                n, hh = items[w]
                keys = slice((n + 1) * P - span(n), (n + 1) * P)
                if w >= 2:
                    pe.wait_ge(msk, w - 1)
                for h, par, i in heads(hh):
                    rows = slice(DH * par, DH * par + DH)
                    last = nc.tensor.matmul(ps[:, 2 * (w % 2) + par, i * 2 * P:i * 2 * P + span(n)],
                                            qT[rows, h // 2, n * P:(n + 1) * P], kT[rows, h // 2, keys],
                                            start=True, stop=True)
                last.then_inc(qk, 1)

            def turn(w):
                n, hh = items[w]
                pe.wait_ge(prb, w + 1)
                if w >= 1:
                    pe.wait_ge(pte_a, w)
                    pe.wait_ge(pte_v, w)
                for h, par, i in heads(hh):
                    for b in range(span(n) // P):
                        last = nc.tensor.transpose(ps[:, 4 + par, (2 * i + b) * P:(2 * i + b + 1) * P],
                                                   sc[:, w % 2, 2 * par + i, b * P:(b + 1) * P], ident[:])
                last.then_inc(ptr, 1)

            def values(w):
                n, hh = items[w]
                pe.wait_ge(pte_a, w + 1)
                pe.wait_ge(pte_v, w + 1)
                if hh == 0 and n >= 2:
                    pe.wait_ge(oev, n - 1)
                nb = span(n) // P
                for h, par, i in heads(hh):
                    for b in range(nb):
                        last = nc.tensor.matmul(ps[:, 6 + n % 2, h * DH:(h + 1) * DH],
                                                pt[:, 2 * par + i, b * P:(b + 1) * P],
                                                vv[:, n - nb + 1 + b, h * DH:(h + 1) * DH],
                                                start=(b == 0), stop=(b == nb - 1))
                last.then_inc(pv, 1)

            scores(0)
            for w in range(W):
                if w + 1 < W:
                    scores(w + 1)
                if w >= 1:
                    values(w - 1)
                turn(w)
            values(W - 1)

        @block.vector
        def _(dve):
            ch = core.dve
            for w in range(W + 2):
                if w < W:
                    n, hh = items[w]
                    mask = core.mask_halves[:] if g == 2 else core.mask_pair[:, 2 * P - span(n):]
                    dve.wait_ge(qk, w + 1)
                    if w >= 2:
                        dve.wait_ge(ptr, w - 1)
                    for h, par, i in heads(hh):
                        ins = nc.vector.tensor_tensor_reduce(
                            sc[:, w % 2, 2 * par + i, 0:span(n)],
                            ps[:, 2 * (w % 2) + par, i * 2 * P:i * 2 * P + span(n)], mask, SCALE, 3 * NEG,
                            ALU.add, ALU.max, core.mstat[:, g, n, 0, h:h + 1])
                        if (par, i) == (1, 1):
                            ins.then_inc(msk, 1)
                        else:
                            ch.mark(ins)
                    ch.wait()
                    dve.wait_ge(msk, w + 1)
                    if w >= 2:
                        dve.wait_ge(prb, w - 1)
                    nc.vector.tensor_scalar(nm[:, w % 2, :], core.mstat[:, g, n, 0, 4 * hh:4 * hh + 4], -1.0, None,
                                            ALU.mult).then_inc(neg, 1)
                if 1 <= w <= W:
                    v = w - 1
                    dve.wait_ge(ptr, v + 1)
                    if v >= 1:
                        dve.wait_ge(pv, v)
                    k = span(items[v][0])
                    nc.vector.tensor_copy(pt[:, 2:4, 0:k],
                                          ps[:, 5, :].rearrange("p (i c) -> p i c", i=2)[:, :, 0:k]).then_inc(pte_v, 1)
                if w >= 3 and (w - 2) % 2 == 1:
                    n = (w - 2) // 2
                    dve.wait_ge(pv, w - 1)
                    if n >= 2:
                        dve.wait_ge(o_out[n % 2], 16 * (n // 2))
                    nc.vector.tensor_copy(ot[:, n % 2, :], ps[:, 6 + n % 2, :]).then_inc(oev, 1)

        @block.scalar
        def _(act):
            ch = core.act
            for w in range(W + 2):
                if w < W:
                    n, hh = items[w]
                    act.wait_ge(neg, w + 1)
                    for h, par, i in heads(hh):
                        row = sc[:, w % 2, 2 * par + i, 0:span(n)]
                        j = h - 4 * hh
                        ins = nc.scalar.activation(row, row, ACT.Exp, bias=nm[:, w % 2, j:j + 1],
                                                   accum_out=core.mstat[:, g, n, 1, h:h + 1])
                        if (par, i) == (1, 1):
                            ins.then_inc(prb, 1)
                        else:
                            ch.mark(ins)
                if 1 <= w <= W:
                    v = w - 1
                    act.wait_ge(ptr, v + 1)
                    if v >= 1:
                        act.wait_ge(pv, v)
                    k = span(items[v][0])
                    nc.scalar.activation(pt[:, 0:2, 0:k], ps[:, 4, :].rearrange("p (i c) -> p i c", i=2)[:, :, 0:k],
                                         ACT.Copy).then_inc(pte_a, 1)
                if w >= 3 and (w - 2) % 2 == 1:
                    n = (w - 2) // 2
                    act.wait_ge(oev, n + 1)
                    act.dma_start(core.o_grp[g, n], ot[:, n % 2, :]).then_inc(o_out[n % 2], 16)
            for i in range(2):
                act.wait_ge(o_out[i], 16 * NT // 2)


def merge_groups(core):
    nc, ps, sem, sb = core.nc, core.ps, core.sem, core.sb
    with ExitStack() as c:
        ml = sb("ml", [P, NT, G, 2, H], ctx=c)
        mx = sb("mx", [P, NT, H], ctx=c)
        cf = sb("cf", [P, NT, G, H], ctx=c)
        cr = sb("cr", [P, G, NT, H], ctx=c)
        og = sb("og", [P, 3, 512], ctx=c)
        at = sb("at", [P, 4, S], ctx=c)
        m_out, m_in, e_sub, e_exp, c_done, c_out, c_in, scaled, tr, added, a_out = (sem(f"m_{x}") for x in
            ("out", "in", "sub", "exp", "done", "cout", "cin", "scaled", "tr", "added", "aout"))
        o_in = [sem(f"m_oin{i}") for i in range(3)]
        units = [(g, n) for g in range(G) for n in range(NT)]
        block = c.enter_context(nc.Block())

        @block.scalar
        def _(act):
            for g, n in units:
                act.dma_start(token_rows(core.ml_nat[g], g, n),
                              core.mstat[:, g, n].rearrange("p a h -> p (a h)")).then_inc(m_out, 16)
            act.wait_ge(m_out, 16 * len(units))
            for g in range(G):
                act.dma_start(ml[:, :, g].rearrange("p n a h -> p n (a h)"),
                              core.ml_nat[g].rearrange("(n p) c -> p n c", p=P)).then_inc(m_in, 16)
            act.wait_ge(e_sub, 1)
            nc.scalar.activation(cf[:], cf[:], ACT.Exp).then_inc(e_exp, 1)
            act.wait_ge(c_done, 1)
            for g in range(G):
                act.dma_start(core.cf_nat[g].rearrange("(n p) c -> p n c", p=P), cf[:, :, g, :]).then_inc(c_out, 16)
            act.wait_ge(c_out, 16 * G)
            for g, n in units:
                act.dma_start(cr[:, g, n], token_rows(core.cf_nat[g], g, n)).then_inc(c_in, 16)
            act.wait_ge(added, len(units))
            act.dma_start(core.att_t[:, :, 0:S].rearrange("k p t -> p k t"), at[:]).then_inc(a_out, 16)
            act.wait_ge(a_out, 16)

        @block.sync
        def _(sp):
            for u, (g, n) in enumerate(units):
                if u >= 3:
                    sp.wait_ge(tr, u - 2)
                sp.dma_start(og[:, u % 3, :], core.o_grp[g, n]).then_inc(o_in[u % 3], 16)
            core.load_weights(core.taken + 8)

        @block.vector
        def _(dve):
            ch = core.dve
            dve.wait_ge(m_in, 16 * G)
            m = [ml[:, :, g, 0, :] for g in range(G)]
            ch.link(nc.vector.tensor_tensor(mx[:], m[0], m[1], ALU.max))
            ch.link(nc.vector.tensor_tensor(mx[:], mx[:], m[2], ALU.max))
            for g in range(G - 1):
                ch.mark(nc.vector.tensor_tensor(cf[:, :, g, :], m[g], mx[:], ALU.subtract))
            ch.wait()
            nc.vector.tensor_tensor(cf[:, :, G - 1, :], m[G - 1], mx[:], ALU.subtract).then_inc(e_sub, 1)
            dve.wait_ge(e_exp, 1)
            for g in range(G):
                ch.link(nc.vector.tensor_tensor(ml[:, :, g, 1, :], ml[:, :, g, 1, :], cf[:, :, g, :], ALU.mult))
            ch.link(nc.vector.tensor_tensor(mx[:], ml[:, :, 0, 1, :], ml[:, :, 1, 1, :], ALU.add))
            ch.link(nc.vector.tensor_tensor(mx[:], mx[:], ml[:, :, 2, 1, :], ALU.add))
            ch.link(nc.vector.reciprocal(mx[:], mx[:]))
            for g in range(G - 1):
                ch.mark(nc.vector.tensor_tensor(cf[:, :, g, :], cf[:, :, g, :], mx[:], ALU.mult))
            ch.wait()
            nc.vector.tensor_tensor(cf[:, :, G - 1, :], cf[:, :, G - 1, :], mx[:], ALU.mult).then_inc(c_done, 1)
            dve.wait_ge(c_in, 16 * len(units))

            def scale(u):
                g, n = units[u]
                dve.wait_ge(o_in[u % 3], 16 * (u // 3 + 1))
                v = og[:, u % 3, :].rearrange("p (h c) -> p h c", h=H)
                nc.vector.tensor_tensor(v, v, bc(cr[:, g, n, :], [P, H, DH]), ALU.mult).then_inc(scaled, 1)

            scale(0)
            for u, (g, n) in enumerate(units):
                if u + 1 < len(units):
                    scale(u + 1)
                dve.wait_ge(tr, u + 1)
                dst = residues(at[:], g, n)
                src = ps[:, u % 2, :].rearrange("p (k c) -> p k c", k=4)
                if g == 0:
                    nc.vector.tensor_copy(dst, src).then_inc(added, 1)
                else:
                    if n == 0:
                        dve.wait_ge(added, u)
                    nc.vector.tensor_tensor(dst, dst, src, ALU.add).then_inc(added, 1)

        @block.tensor
        def _(pe):
            for u in range(len(units)):
                pe.wait_ge(scaled, u + 1)
                if u >= 2:
                    pe.wait_ge(added, u - 1)
                for j in range(4):
                    last = nc.tensor.transpose(ps[:, u % 2, j * P:(j + 1) * P], og[:, u % 3, j * P:(j + 1) * P],
                                               core.ident[:])
                last.then_inc(tr, 1)


def project_mlstm(core):
    nc, t, ps, sem, sb, Z = core.nc, core.t, core.ps, core.sem, core.sb, 4
    hhi, hlo, ident = core.hhi, core.hlo, core.ident
    igf, lfg = core.igf, core.lfg
    UN = 4 * (NT + 1)
    NQ = 2 * (NT + 1)
    p0 = core.taken
    core.taken += 4 * KD
    with ExitStack() as c:
        zt = sb("zm", [P, Z, 512], ctx=c)
        tt = sb("zmt", [P, 2, 512], ctx=c)
        wif = sb("wif", [P, KD, 16], ctx=c)
        wif_hi = sb("wif_hi", [P, KD, 40], F32R, c)
        wif_lo = sb("wif_lo", [P, KD, 40], F32R, c)
        bif = sb("bif", [40, 1], ctx=c)
        yy = sb("yif", [40, T], ctx=c)
        ab = sb("aif", [40, T], ctx=c)
        mm, ev, tr, tre, w_in, w_hi, w_lo, g_mm, g_ev, g_ab, g_ln, g_done, g_out = (sem(f"p_{x}") for x in
            ("mm", "ev", "tr", "tre", "win", "whi", "wlo", "gmm", "gev", "gab", "gln", "gdone", "gout"))
        zout = [sem(f"p_zout{i}") for i in range(Z)]
        tout = [sem(f"p_tout{i}") for i in range(2)]
        block = c.enter_context(nc.Block())

        def store(u):
            x, n = divmod(u, NT + 1)
            if n == NT:
                return core.zm_s[:, x * 512:(x + 1) * 512]
            return core.m_tok[n, :, x - 1, :] if x else None

        n_out, done_at = [0] * Z, {}
        for u in range(UN):
            if store(u) is not None:
                n_out[u % Z] += 16
            done_at[u] = n_out[u % Z]

        @block.sync
        def _(sp):
            sp.dma_start(wif[:], t["w_in"].rearrange("(k p) c -> p k c", p=P)[:, :, CIF:CIF + 16]).then_inc(w_in, 16)
            sp.dma_start(bif[0:8, :], t["b_if"].rearrange("(h a) -> h a", a=1)[0:8, :]).then_inc(w_in, 16)
            sp.dma_start(bif[32:40, :], t["b_if"].rearrange("(h a) -> h a", a=1)[8:16, :]).then_inc(w_in, 16)
            core.load_weights(core.taken + 8)

        @block.gpsimd
        def _(pool):
            core.split_weights(core.taken + 8)

        @block.tensor
        def _(pe):
            pe.wait_ge(w_lo, 2)
            for s in range(3):
                seg = slice(s * SEG, (s + 1) * SEG)
                for k in range(KD):
                    last = products(nc, ps[0:40, 5 + s, 0:SEG], (wif_hi[:, k, :], wif_lo[:, k, :]),
                                    (hhi[:, k, seg], hlo[:, k, seg]), k == 0, k == KD - 1)
            last.then_inc(g_mm, 1)

            turned = 0
            for u in range(UN + 2):
                if u < UN:
                    x, n = divmod(u, NT + 1)
                    rows = P if n < NT else NB
                    if n == 0:
                        pe.wait_ge(core.w_lo, p0 + (x + 1) * KD)
                    if u >= 4:
                        pe.wait_ge(ev, u - 3)
                    cols = slice(n * P, n * P + rows)
                    for k in range(KD):
                        last = products(nc, ps[0:rows, u % 4, :], (hhi[:, k, cols], hlo[:, k, cols]),
                                        core.weight(p0 + x * KD + k, slice(0, CW)), k == 0, k == KD - 1)
                        if n == NT:
                            last.then_inc(core.w_used, 1)
                    if n < NT:
                        last.then_inc(mm, 1)
                if 2 <= u < NQ + 2 and (u - 2) % (NT + 1) < NT:
                    v = u - 2
                    pe.wait_ge(ev, v + 1)
                    if turned >= 1:
                        pe.wait_ge(tre, turned)
                    turned += 1
                    for j in range(4):
                        last = nc.tensor.transpose(ps[:, 4, j * P:(j + 1) * P], zt[:, v % Z, j * P:(j + 1) * P], ident[:])
                    last.then_inc(tr, 1)

        @block.vector
        def _(dve):
            ch = core.dve
            for w in (wif_hi, wif_lo):
                ch.mark(nc.vector.memset(w[:].bitcast(F32), 0.0))
            dve.wait_ge(w_in, 48)
            ch.wait()
            for at, frm in ((0, 0), (32, 8)):
                nc.vector.tensor_copy(wif_hi[:, :, at:at + 8], wif[:, :, frm:frm + 8]).then_inc(w_hi, 1)
            dve.wait_ge(w_hi, 2)
            for at, frm in ((0, 0), (32, 8)):
                nc.vector.tensor_tensor(wif_lo[:, :, at:at + 8], wif[:, :, frm:frm + 8],
                                        wif_hi[:, :, at:at + 8].bitcast(F32), ALU.subtract).then_inc(w_lo, 1)
            dve.wait_ge(g_mm, 1)
            src = ps[:, 5:8, 0:SEG]
            seg3 = lambda a: a.rearrange("p (s c) -> p s c", s=3)
            ch.mark(nc.vector.tensor_scalar(seg3(igf[0:8, :]), src[0:8], bif[0:8, :], None, ALU.add))
            ch.link(nc.vector.tensor_scalar(seg3(yy[32:40, :]), src[32:40], bif[32:40, :], None, ALU.add))
            nc.vector.scalar_tensor_tensor(ab[32:40, :], yy[32:40, :], -1.0, yy[32:40, :], ALU.mult, ALU.max).then_inc(g_ab, 1)
            ch.link(nc.vector.tensor_scalar(yy[32:40, :], yy[32:40, :], 0.0, None, ALU.min))
            dve.wait_ge(g_ln, 2)
            nc.vector.tensor_tensor(lfg[0:8, :], yy[32:40, :], ab[32:40, :], ALU.subtract).then_inc(g_done, 1)

        @block.scalar
        def _(act):
            act.wait_ge(g_ab, 1)
            nc.scalar.activation(ab[32:40, :], ab[32:40, :], ACT.Exp, scale=-1.0).then_inc(g_ln, 1)
            act.wait_ge(g_ln, 1)
            nc.scalar.activation(ab[32:40, :], ab[32:40, :], ACT.Ln, bias=1.0).then_inc(g_ln, 1)
            act.wait_ge(g_done, 1)
            act.dma_start(core.if_s[0], igf[0:8, S:T]).then_inc(g_out, 16)
            act.dma_start(core.if_s[1], lfg[0:8, S:T]).then_inc(g_out, 16)
            turned = 0
            for u in range(UN + 2):
                if u < UN:
                    x, n = divmod(u, NT + 1)
                    rows = P if n < NT else NB
                    if n < NT:
                        act.wait_ge(mm, u + 1 - (u + 1) // (NT + 1))
                    else:
                        act.wait_ge(core.w_used, p0 + (x + 1) * KD)
                    if u >= Z:
                        v = u - Z
                        act.wait_ge(tr, min(v + 1, NQ) - min(v + 1, NQ) // (NT + 1))
                        if done_at[v]:
                            act.wait_ge(zout[v % Z], done_at[v])
                    nc.scalar.activation(zt[0:rows, u % Z, :], ps[0:rows, u % 4, :], ACT.Copy,
                                         scale=SCALE if x == 0 else 1.0).then_inc(ev, 1)
                    if store(u) is not None:
                        act.wait_ge(ev, u + 1)
                        act.dma_start(store(u), zt[0:rows, u % Z, :]).then_inc(zout[u % Z], 16)
                if 2 <= u < NQ + 2 and (u - 2) % (NT + 1) < NT:
                    x, n = divmod(u - 2, NT + 1)
                    act.wait_ge(tr, turned + 1)
                    if turned >= 2:
                        act.wait_ge(tout[turned % 2], 16 * (turned // 2))
                    nc.scalar.activation(tt[:, turned % 2, :], ps[:, 4, :], ACT.Copy).then_inc(tre, 1)
                    act.wait_ge(tre, turned + 1)
                    act.dma_start(core.m_tr[x, n], tt[:, turned % 2, :]).then_inc(tout[turned % 2], 16)
                    turned += 1
            for i in range(Z):
                act.wait_ge(zout[i], n_out[i])
            for i in range(2):
                act.wait_ge(tout[i], 16 * NT)
            act.wait_ge(g_out, 32)


def mlstm_gates(core):
    nc, sem, sb = core.nc, core.sem, core.sb
    igf, lfg, bands, neg_m = core.igf, core.lfg, core.bands, core.neg_m
    with ExitStack() as c:
        bb = sb("g_b", [8, S], ctx=c)
        mx = sb("g_m", [8, S], ctx=c)
        zero = sb("g_zero", [8, P], ctx=c)
        m_run = sb("g_run", [8, NT + 1], ctx=c)
        m_end, m_out = sem("g_end"), core.store_sem("g_mout")
        block = c.enter_context(nc.Block())

        @block.sync
        def _(sp):
            core.load_weights(core.taken + 8)
            sp.wait_ge(m_end, 1)
            sp.dma_start(core.o[7].rearrange("a h -> h a"), m_run[:, NT:NT + 1]).then_inc(m_out, 16)
            sp.wait_ge(m_out, 16)

        @block.vector
        def _(dve):
            ch = core.dve
            ch.mark(nc.vector.memset(zero[:], 0.0))
            ch.mark(nc.vector.memset(m_run[:], 0.0))
            ch.link(nc.vector.memset(bands[:], 0.0))
            for n in range(NT):
                cols = slice(n * P, (n + 1) * P)
                ch.mark(nc.vector.tensor_tensor_scan(bb[:, cols], lfg[0:8, cols], zero[:], 0.0, ALU.add, ALU.add))
            ch.wait()
            ch.link(nc.vector.tensor_tensor(bands[0:8, :], igf[0:8, 0:S], bb[:], ALU.subtract))
            for n in range(NT):
                cols = slice(n * P, (n + 1) * P)
                end = slice(n * P + P - 1, n * P + P)
                ch.link(nc.vector.tensor_tensor_scan(mx[:, cols], zero[:], bands[0:8, cols], m_run[:, n:n + 1],
                                                     ALU.add, ALU.max))
                ch.mark(nc.vector.tensor_tensor(m_run[:, n + 1:n + 2], bb[:, end], mx[:, end], ALU.add))
                ch.mark(nc.vector.tensor_scalar(bands[32:40, cols], mx[:, cols], -1.0, m_run[:, n:n + 1],
                                                ALU.mult, ALU.add))
                ch.link(nc.vector.tensor_scalar(bands[96:104, cols], bands[0:8, cols], mx[:, end], None, ALU.subtract))
            ch.mark(nc.vector.scalar_tensor_tensor(bands[64:72, :], mx[:], -1.0, bb[:], ALU.mult, ALU.subtract))
            ch.link(nc.vector.tensor_scalar(neg_m[:], mx[:], -1.0, None, ALU.mult))
            nc.vector.tensor_copy(m_run[:, 0:1], zero[:, 0:1]).then_inc(m_end, 1)


def mlstm_chunks(core):
    nc, o, ps, sem, sb, ident = core.nc, core.o, core.ps, core.sem, core.sb, core.ident
    bands, neg_m = core.bands, core.neg_m
    E = DV + 1
    with ExitStack() as c:
        qT = sb("c_q", [P, 2, 4, P], ctx=c)
        kT = sb("c_k", [P, 2, 4, P], ctx=c)
        kk = sb("c_kk", [P, 2, H, DH], ctx=c)
        vv = sb("c_v", [P, 2, H, E], ctx=c)
        st = sb("c_state", [P, 4, E], ctx=c)
        xt = sb("c_xt", [P, P], ctx=c)
        xe = sb("c_xe", [P, 3, H], ctx=c)
        ww = sb("c_w", [P, H, P], ctx=c)
        num = sb("c_num", [P, H, E], ctx=c)
        den = sb("c_den", [P, H], ctx=c)
        hb = sb("c_h", [P, H, DV], ctx=c)
        ht = sb("c_ht", [P, H, P], ctx=c)
        kw = sb("c_kw", [P, H, DH], ctx=c)
        dec = sb("c_dec", [P, 4], ctx=c)
        names = ("one", "xtp", "xts", "xex", "mb", "kq", "wm", "wex", "wqk", "inter", "nsc", "intra", "num", "dstp",
                 "kwd", "up", "std", "hbd", "htp", "hts", "hts2", "st0")
        s_ = {x: sem(f"c_{x}") for x in names}
        c_in = [sem(f"c_in{i}") for i in range(2)]
        h_out, c_out = sem("c_hout"), core.store_sem("c_out")
        block = c.enter_context(nc.Block())
        par = lambda h: h % 2
        pos = lambda h: 4 * (h % 2) + h // 2

        def inter_at(h):
            i = h // 2
            return 4 + 2 * par(h) + i // 3, slice((i % 3) * E, (i % 3 + 1) * E)

        @block.sync
        def _(sp):
            for n in range(NT):
                if n >= 2:
                    sp.wait_ge(s_["up"], n - 1)
                b = n % 2
                if n < 2:
                    sp.wait_ge(s_["one"], 1)
                for dst, src in ((qT[:, b], core.m_tr[0, n].rearrange("p (j c) -> p j c", j=4)),
                                 (kT[:, b], core.m_tr[1, n].rearrange("p (j c) -> p j c", j=4)),
                                 (kk[:, b], core.m_tok[n, :, 0, :].rearrange("p (h c) -> p h c", h=H)),
                                 (vv[:, b, :, 0:DV], core.m_tok[n, :, 1:3, :].rearrange("p x (h c) -> p (x h) c", c=DV))):
                    sp.dma_start(dst, src).then_inc(c_in[b], 16)
            sp.wait_ge(s_["std"], NT + 1)
            dst = o[5][0].rearrange("(j two) d e -> two d j e", two=2)
            dstn = o[6][0].rearrange("(j two) d -> two d j", two=2)
            with nc.allow_non_contiguous_dma(reason="the normaliser's column"):
                for two in range(2):
                    rows = slice(DH * two, DH * two + DH)
                    sp.dma_start(dst[two], st[rows, :, 0:DV]).then_inc(c_out, 16)
                    sp.dma_start(dstn[two], st[rows, :, DV]).then_inc(c_out, 16)
            sp.wait_ge(c_out, 64)

        @block.tensor
        def _(pe):
            for n in range(NT):
                b = n % 2
                cols = slice(n * P, (n + 1) * P)
                if n >= 1:
                    pe.wait_ge(s_["std"], n + 1)
                nc.tensor.transpose(ps[:, 7, 0:P], bands[:, cols], ident[:]).then_inc(s_["xtp"], 1)
                if n >= 1:
                    pe.wait_ge(s_["num"], n)
                for h in range(H):
                    last = nc.tensor.matmul(ps[:, par(h), (h // 2) * P:(h // 2 + 1) * P],
                                            ident[0:H, h:h + 1].to_broadcast([H, P]), neg_m[:, cols],
                                            start=True, stop=True)
                last.then_inc(s_["mb"], 1)
                pe.wait_ge(c_in[b], 64 * (n // 2 + 1))
                for h in range(H):
                    rows = slice(DH * par(h), DH * par(h) + DH)
                    last = nc.tensor.matmul(ps[:, 2 + par(h), (h // 2) * P:(h // 2 + 1) * P], kT[rows, b, h // 2, :],
                                            qT[rows, b, h // 2, :], start=True, stop=True)
                last.then_inc(s_["kq"], 1)
                if n == 0:
                    pe.wait_ge(s_["st0"], 1)
                if n >= 1:
                    pe.wait_ge(s_["hts"], n)
                    pe.wait_ge(s_["hts2"], n)
                pe.wait_ge(s_["xts"], n + 1)
                for h in [0, 2, 4, 6, 1, 3, 5, 7]:
                    rows = slice(DH * par(h), DH * par(h) + DH)
                    last = nc.tensor.matmul(ps[:, *inter_at(h)], qT[rows, b, h // 2, :], st[rows, h // 2, :],
                                            start=True, stop=True)
                last.then_inc(s_["inter"], 1)
                pe.wait_ge(s_["wqk"], 2 * n + 2)
                for h in range(H):
                    last = nc.tensor.matmul(ps[:, h // 3, (h % 3) * E:(h % 3 + 1) * E], ww[:, pos(h), :],
                                            vv[:, b, h, :], start=True, stop=True)
                last.then_inc(s_["intra"], 1)
                pe.wait_ge(s_["nsc"], n + 1)
                nc.tensor.matmul(ps[:, 7, 0:H], ident[:, P - 1:P].to_broadcast([P, P]), xe[:, 0, :],
                                 start=True, stop=True).then_inc(s_["dstp"], 1)
                pe.wait_ge(s_["kwd"], n + 1)
                for h in range(H):
                    rows = slice(DH * par(h), DH * par(h) + DH)
                    bank, at = (3, (h // 2) * E) if h < 6 else (7, P)
                    last = nc.tensor.matmul(ps[rows, bank, at:at + E], kw[:, h, :], vv[:, b, h, :],
                                            start=True, stop=True)
                last.then_inc(s_["up"], 1)
                pe.wait_ge(s_["hbd"], n + 1)
                for h in range(H):
                    last = nc.tensor.transpose(ps[:, 4 + h // 4, (h % 4) * P:(h % 4 + 1) * P], hb[:, h, :], ident[:])
                last.then_inc(s_["htp"], 1)

        @block.vector
        def _(dve):
            ch = core.dve
            nc.vector.memset(vv[:], 1.0).then_inc(s_["one"], 1)
            nc.vector.memset(st[:], 0.0).then_inc(s_["st0"], 1)
            dve.wait_ge(s_["st0"], 1)
            nc.vector.memset(dec[:], 0.0).then_inc(s_["std"], 1)
            for n in range(NT):
                b = n % 2
                dve.wait_ge(s_["xtp"], n + 1)
                if n >= 1:
                    dve.wait_ge(s_["wex"], n)
                nc.vector.tensor_copy(xt[:], ps[:, 7, 0:P]).then_inc(s_["xts"], 1)
                dve.wait_ge(s_["mb"], n + 1)
                if n >= 1:
                    dve.wait_ge(s_["intra"], n)
                mask = core.mask_later[:].unsqueeze(1).to_broadcast([P, 4, P])
                for q in range(2):
                    nc.vector.tensor_tensor(ww[:, 4 * q:4 * q + 4, :], ps[:, q, :].rearrange("p (i c) -> p i c", i=4),
                                            mask, ALU.add).then_inc(s_["wm"], 1)
                dve.wait_ge(s_["xex"], n + 1)
                dve.wait_ge(c_in[b], 64 * (n // 2 + 1))
                if n >= 1:
                    dve.wait_ge(s_["up"], n)
                nc.vector.tensor_tensor(kw[:], kk[:, b], bc(xe[:, 2, :], [P, H, DH]), ALU.mult).then_inc(s_["kwd"], 1)
                dve.wait_ge(s_["wex"], n + 1)
                dve.wait_ge(s_["kq"], n + 1)
                for q in range(2):
                    nc.vector.tensor_tensor(ww[:, 4 * q:4 * q + 4, :], ww[:, 4 * q:4 * q + 4, :],
                                            ps[:, 2 + q, :].rearrange("p (i c) -> p i c", i=4),
                                            ALU.mult).then_inc(s_["wqk"], 1)
                dve.wait_ge(s_["intra"], n + 1)
                dve.wait_ge(s_["nsc"], n + 1)
                for q, k in ((0, 3), (1, 3), (2, 2)):
                    part = num[:, 3 * q:3 * q + k, :]
                    ins = nc.vector.tensor_tensor(part, part, ps[:, q, 0:k * E].rearrange("p (i c) -> p i c", i=k),
                                                  ALU.add)
                    if q == 2:
                        ins.then_inc(s_["num"], 1)
                    else:
                        ch.mark(ins)
                ch.wait()
                dve.wait_ge(s_["num"], n + 1)
                ch.link(nc.vector.scalar_tensor_tensor(den[:], num[:, :, DV], -1.0, num[:, :, DV], ALU.mult, ALU.max))
                ch.link(nc.vector.tensor_tensor(den[:], den[:], xe[:, 1, :], ALU.max))
                ch.link(nc.vector.reciprocal(den[:], den[:]))
                if n >= 1:
                    dve.wait_ge(s_["htp"], n)
                nc.vector.tensor_tensor(hb[:], num[:, :, 0:DV], bc(den[:], [P, H, DV]), ALU.mult).then_inc(s_["hbd"], 1)
                dve.wait_ge(s_["dstp"], n + 1)
                dve.wait_ge(s_["up"], n + 1)
                dve.wait_ge(s_["std"], n + 1)
                ch.mark(nc.vector.tensor_copy(dec[0:DH, :], ps[0:DH, 7, 0:H:2]))
                ch.link(nc.vector.tensor_copy(dec[DH:P, :], ps[DH:P, 7, 1:H:2]))
                for i in range(4):
                    bank, at = (3, i * E) if i < 3 else (7, P)
                    ins = nc.vector.scalar_tensor_tensor(st[:, i, :], st[:, i, :], dec[:, i:i + 1],
                                                         ps[:, bank, at:at + E], ALU.mult, ALU.add)
                    if i == 3:
                        ins.then_inc(s_["std"], 1)
                    else:
                        ch.mark(ins)
                ch.wait()
                dve.wait_ge(s_["htp"], n + 1)
                if n >= 1:
                    dve.wait_ge(h_out, 16 * n)
                nc.vector.tensor_copy(ht[:, 0:4, :], ps[:, 4, :].rearrange("p (i c) -> p i c", i=4)).then_inc(s_["hts"], 1)

        @block.scalar
        def _(act):
            ch = core.act
            for n in range(NT):
                act.wait_ge(s_["xts"], n + 1)
                if n >= 1:
                    act.wait_ge(s_["dstp"], n)
                    act.wait_ge(s_["hbd"], n)
                    act.wait_ge(s_["kwd"], n)
                nc.scalar.activation(xe[:], xt[:].rearrange("p (b c) -> p b c", b=4)[:, 1:4, 0:H],
                                     ACT.Exp).then_inc(s_["xex"], 1)
                act.wait_ge(s_["wm"], 2 * n + 2)
                for h in range(H):
                    ins = nc.scalar.activation(ww[:, pos(h), :], ww[:, pos(h), :], ACT.Exp, bias=xt[:, h:h + 1])
                    if h == H - 1:
                        ch.wait()
                        ins.then_inc(s_["wex"], 1)
                    else:
                        ch.mark(ins)
                act.wait_ge(s_["inter"], n + 1)
                act.wait_ge(s_["xex"], n + 1)
                for h in range(H):
                    ins = nc.scalar.activation(num[:, h, :], ps[:, *inter_at(h)], ACT.Copy, scale=xe[:, 0, h:h + 1])
                    if h == H - 1:
                        ins.then_inc(s_["nsc"], 1)
                    else:
                        ch.mark(ins)
                act.wait_ge(s_["htp"], n + 1)
                if n >= 1:
                    act.wait_ge(h_out, 16 * n)
                nc.scalar.activation(ht[:, 4:8, :], ps[:, 5, :].rearrange("p (i c) -> p i c", i=4),
                                     ACT.Copy).then_inc(s_["hts2"], 1)
                act.wait_ge(s_["hts"], n + 1)
                act.wait_ge(s_["hts2"], n + 1)
                act.dma_start(core.h_mem[:, :, n * P:(n + 1) * P].rearrange("k p t -> p k t"), ht[:]).then_inc(h_out, 16)
            act.wait_ge(h_out, 16 * NT)


def sample_attention(core):
    nc, t, o, ps, sem, sb, ident = core.nc, core.t, core.o, core.ps, core.sem, core.sb, core.ident
    caches = [t["cache_kv_w128"], t["cache_kv_w512"], t["cache_kv_w2048"]]
    C = NB * G * H
    with ExitStack() as c:
        zs = sb("s_z", [NB, G, 3, 512], ctx=c)
        pr = sb("s_pr", [NB, G, 512], ctx=c)
        sn = sb("s_sn", [NB, G * H], ctx=c)
        dg = sb("s_dg", [NB, NB, G * H], ctx=c)
        kc = sb("s_kc", [P, 3, 512], ctx=c)
        qb = sb("s_qb", [P, 3, 512], ctx=c)
        vc = sb("s_vc", [P, 2, G, 512], ctx=c)
        ss = sb("s_ss", [P, NB, G, H], ctx=c)
        sa = sb("s_sa", [P, NB, G, H], ctx=c)
        nw = sb("s_nw", [P, NB, G, H], ctx=c)
        mx = sb("s_mx", [P, NB, H], ctx=c)
        ll = sb("s_ll", [P, NB, H], ctx=c)
        l3 = sb("s_l3", [P, NB, G, H], ctx=c)
        vt = sb("s_vt", [P, G, 4, NB], ctx=c)
        pn = sb("s_pn", [P, G, 4, NB], ctx=c)
        rl = sb("s_rl", [P, 4, NB], ctx=c)
        ot = sb("s_ot", [P, 4, NB], ctx=c)
        z_in, snd, dgd, bcp, nwd, prd, sc, amx, sub, ex, vtp, lp, pv, done, out = (sem(f"s_{x}") for x in
            ("zin", "sn", "dg", "bcp", "nw", "pr", "sc", "amx", "sub", "ex", "vtp", "lp", "pv", "done", "out"))
        rows_out = core.store_sem("s_rows")
        k_in = [sem(f"s_kin{i}") for i in range(3)]
        v_in = [sem(f"s_vin{i}") for i in range(2)]
        units = [(b, g) for b in range(NB) for g in range(G)]
        block = c.enter_context(nc.Block())

        def cached(g, b, which):
            return caches[g][b].rearrange("(j d) a h c -> d j a (h c)", d=DILS[g])[0, :, which]

        @block.sync
        def _(sp):
            sp.dma_start(zs[:], core.z_s.rearrange("g x b c -> b g x c")).then_inc(z_in, 16)
            for u, (b, g) in enumerate(units):
                if u >= 3:
                    sp.wait_ge(sc, u - 2)
                sp.dma_start(kc[:, u % 3, :], cached(g, b, 0)).then_inc(k_in[u % 3], 16)
                sp.dma_start(qb[:, u % 3, :], core.z_s[g, 0, b:b + 1, :].to_broadcast([P, 512])).then_inc(k_in[u % 3], 16)
            for g in range(G):
                sp.dma_start(o[8 + g][:, -1 + WINDOWS[g]].rearrange("b a h c -> b a (h c)"),
                             zs[:, g, 1:3, :]).then_inc(rows_out, 16)
            core.load_weights(core.taken + 8)
            sp.wait_ge(rows_out, 16 * G)

        @block.scalar
        def _(act):
            for b in range(NB):
                if b >= 2:
                    act.wait_ge(pv, b - 1)
                for g in range(G):
                    act.dma_start(vc[:, b % 2, g, :], cached(g, b, 1)).then_inc(v_in[b % 2], 16)
                if b == 1:
                    act.wait_ge(sub, 2)
                    nc.scalar.activation(ss[:], ss[:], ACT.Exp, scale=SCALE).then_inc(ex, 1)
                    nc.scalar.activation(nw[:], nw[:], ACT.Exp, scale=SCALE).then_inc(ex, 1)
            act.wait_ge(done, 1)
            act.dma_start(core.att_t[:, :, S:T].rearrange("k p b -> p k b"), ot[:]).then_inc(out, 16)
            act.wait_ge(out, 16)

        @block.gpsimd
        def _(pool):
            pool.wait_ge(sc, len(units))
            pool.partition_all_reduce(sa[:].rearrange("p b g h -> p (b g h)"), ss[:].rearrange("p b g h -> p (b g h)"),
                                      P, bass.bass_isa.ReduceOp.max).then_inc(amx, 1)

        @block.vector
        def _(dve):
            ch = core.dve
            dve.wait_ge(z_in, 16)
            ch.link(nc.vector.tensor_tensor(pr[:], zs[:, :, 0, :], zs[:, :, 1, :], ALU.mult))
            nc.vector.tensor_reduce(sn[:], pr[:].rearrange("b g (h c) -> b (g h) c", h=H), AX.X, ALU.add).then_inc(snd, 1)
            dve.wait_ge(snd, 1)
            nc.vector.tensor_tensor(dg[:], sn[:].unsqueeze(1).to_broadcast([NB, NB, G * H]),
                                    bc(ident[0:NB, 0:NB], [NB, NB, G * H]), ALU.mult).then_inc(dgd, 1)
            for u, (b, g) in enumerate(units):
                dve.wait_ge(k_in[u % 3], 32 * (u // 3 + 1))
                ch.link(nc.vector.tensor_tensor(kc[:, u % 3, :], kc[:, u % 3, :], qb[:, u % 3, :], ALU.mult))
                nc.vector.tensor_reduce(ss[:, b, g, :], kc[:, u % 3, :].rearrange("p (h c) -> p h c", h=H),
                                        AX.X, ALU.add).then_inc(sc, 1)
            dve.wait_ge(bcp, 1)
            ch.link(nc.vector.tensor_copy(nw[:].rearrange("p b g h -> p (b g h)"), ps[:, 0, 0:C]))
            dve.wait_ge(amx, 1)
            ch.link(nc.vector.tensor_tensor(sa[:], sa[:], nw[:], ALU.max))
            ch.link(nc.vector.tensor_reduce(mx[:], sa[:].rearrange("p b g h -> p b h g"), AX.X, ALU.max))
            m4 = mx[:].unsqueeze(2).to_broadcast([P, NB, G, H])
            nc.vector.tensor_tensor(ss[:], ss[:], m4, ALU.subtract).then_inc(sub, 1)
            nc.vector.tensor_tensor(nw[:], nw[:], m4, ALU.subtract).then_inc(sub, 1)
            dve.wait_ge(vtp, 1)
            ch.mark(nc.vector.tensor_copy(vt[:].rearrange("p g j b -> p (g j b)"), ps[:, 1, 0:G * 4 * NB]))
            dve.wait_ge(ex, 2)
            dve.wait_ge(lp, 1)
            ch.link(nc.vector.tensor_tensor(l3[:].rearrange("p b g h -> p (b g h)"), ps[:, 2, 0:C],
                                            nw[:].rearrange("p b g h -> p (b g h)"), ALU.add))
            ch.link(nc.vector.tensor_reduce(ll[:], l3[:].rearrange("p b g h -> p b h g"), AX.X, ALU.add))
            ch.link(nc.vector.reciprocal(ll[:], ll[:]))
            for two in range(2):
                rows = slice(DH * two, DH * two + DH)
                for g in range(G):
                    ch.mark(nc.vector.tensor_copy(pn[rows, g], nw[rows, :, g, two::2].rearrange("p b j -> p j b")))
                ch.mark(nc.vector.tensor_copy(rl[rows], ll[rows, :, two::2].rearrange("p b j -> p j b")))
            ch.wait()
            ch.link(nc.vector.tensor_tensor(vt[:], vt[:], pn[:], ALU.mult))
            ch.link(nc.vector.tensor_tensor(vt[:, 0], vt[:, 0], vt[:, 1], ALU.add))
            ch.link(nc.vector.tensor_tensor(vt[:, 0], vt[:, 0], vt[:, 2], ALU.add))
            dve.wait_ge(pv, NB)
            for two in range(2):
                rows = slice(DH * two, DH * two + DH)
                src = ps[rows, 3, 0:NB * H].rearrange("p (b j two) -> p two j b", two=2, j=4)[:, two]
                ch.mark(nc.vector.tensor_tensor(ot[rows], vt[rows, 0], src, ALU.add))
            ch.wait()
            nc.vector.tensor_tensor(ot[:], ot[:], rl[:], ALU.mult).then_inc(done, 1)

        @block.tensor
        def _(pe):
            pe.wait_ge(dgd, 1)
            nc.tensor.matmul(ps[:, 0, 0:C], core.ones[0:NB, :], dg[:].rearrange("a b c -> a (b c)"),
                             start=True, stop=True).then_inc(bcp, 1)
            for g in range(G):
                for j in range(4):
                    at = (4 * g + j) * NB
                    last = nc.tensor.transpose(ps[:, 1, at:at + NB], zs[:, g, 2, j * P:(j + 1) * P], ident[0:NB, 0:NB])
            last.then_inc(vtp, 1)
            pe.wait_ge(ex, 2)
            nc.tensor.matmul(ps[:, 2, 0:C], core.ones[:], ss[:].rearrange("p b g h -> p (b g h)"),
                             start=True, stop=True).then_inc(lp, 1)
            for b in range(NB):
                pe.wait_ge(v_in[b % 2], 48 * (b // 2 + 1))
                for j in range(4):
                    for g in range(G):
                        at = (b * 4 + j) * 2
                        last = nc.tensor.matmul(ps[:, 3, at:at + 2], vc[:, b % 2, g, j * P:(j + 1) * P],
                                                ss[:, b, g, 2 * j:2 * j + 2], start=(g == 0), stop=(g == G - 1))
                last.then_inc(pv, 1)


def sample_mlstm(core):
    nc, t, o, ps, sem, sb, ident = core.nc, core.t, core.o, core.ps, core.sem, core.sb, core.ident
    with ExitStack() as c:
        z = sb("r_z", [NB, 2048], ctx=c)
        st = sb("r_c", [P, NB, 4, DV], ctx=c)
        nn = sb("r_n", [NB, 512], ctx=c)
        gt = sb("r_g", [NB, 3, H], ctx=c)
        tmp = sb("r_t", [NB, 512], ctx=c)
        kw = sb("r_kw", [NB, 512], ctx=c)
        km = sb("r_km", [NB, NB, 512], ctx=c)
        mt = sb("r_m", [NB, H], ctx=c)
        e3 = sb("r_e", [NB, 3, H], ctx=c)
        qk = sb("r_qk", [NB, H], ctx=c)
        qn = sb("r_qn", [NB, H], ctx=c)
        co = sb("r_co", [NB, 3, H], ctx=c)
        dg = sb("r_dg", [NB, NB, 3, H], ctx=c)
        cb = sb("r_cb", [P, NB, 3, H], ctx=c)
        d2 = sb("r_d2", [P, NB, 4], ctx=c)
        qd = sb("r_qd", [P, NB, 4, 2], ctx=c)
        vt = sb("r_vt", [P, H, NB], ctx=c)
        ht = sb("r_ht", [P, H, NB], ctx=c)
        z_in, g_in, s_in, tr, qdd, gsub, gexp, dgd, cbp, cbd, kmd, up, std, hq, hd = (sem(f"r_{x}") for x in
            ("zin", "gin", "sin", "tr", "qd", "gsub", "gexp", "dg", "cbp", "cb", "km", "up", "st", "hq", "h"))
        out = core.store_sem("r_out")
        nd, md = sem("r_nd"), sem("r_md")
        block = c.enter_context(nc.Block())
        halves = [slice(0, DH), slice(DH, P)]

        @block.sync
        def _(sp):
            sp.dma_start(z[:], core.zm_s).then_inc(z_in, 16)
            with nc.allow_non_contiguous_dma(reason="64 gates"):
                sp.dma_start(gt[:, 0, :], core.if_s[0].rearrange("h b -> b h")).then_inc(g_in, 16)
                sp.dma_start(gt[:, 1, :], core.if_s[1].rearrange("h b -> b h")).then_inc(g_in, 16)
            sp.dma_start(gt[:, 2, :], t["state_mlstm_m"]).then_inc(g_in, 16)
            sp.dma_start(nn[:], t["state_mlstm_n"].rearrange("b h d -> b (h d)")).then_inc(g_in, 16)
            for b in range(NB):
                sp.dma_start(st[:, b], t["state_mlstm_C"][b].rearrange("(j two) d e -> (two d) j e", two=2)).then_inc(s_in, 16)
            core.load_weights(core.taken + 8)
            sp.wait_ge(md, 1)
            sp.dma_start(o[13], mt[:]).then_inc(out, 16)
            sp.wait_ge(nd, 1)
            sp.dma_start(o[12].rearrange("b h d -> b (h d)"), nn[:]).then_inc(out, 16)
            sp.wait_ge(hd, 1)
            sp.dma_start(core.h_mem[:, :, S:T].rearrange("k p b -> p k b"), ht[:]).then_inc(out, 16)
            for b in range(NB):
                sp.wait_ge(std, 4 * b + 4)
                sp.dma_start(o[11][b].rearrange("(j two) d e -> (two d) j e", two=2), st[:, b]).then_inc(out, 16)
            sp.wait_ge(out, 16 * (3 + NB))

        @block.tensor
        def _(pe):
            pe.wait_ge(z_in, 16)
            for j in range(4):
                nc.tensor.transpose(ps[:, 0, j * NB:(j + 1) * NB], z[:, j * P:(j + 1) * P], ident[0:NB, 0:NB])
            for h in range(H):
                last = nc.tensor.transpose(ps[:, 0, (4 + h) * NB:(5 + h) * NB], z[:, 1024 + h * P:1024 + (h + 1) * P],
                                           ident[0:NB, 0:NB])
            last.then_inc(tr, 1)
            pe.wait_ge(qdd, 2)
            pe.wait_ge(s_in, 16 * NB)
            for b in range(NB):
                for j in range(4):
                    at = (b * 4 + j) * 2
                    last = nc.tensor.matmul(ps[:, 1, at:at + 2], st[:, b, j, :], qd[:, b, j, :], start=True, stop=True)
            last.then_inc(hq, 1)
            pe.wait_ge(dgd, 1)
            nc.tensor.matmul(ps[:, 2, 0:NB * 3 * H], core.ones[0:NB, :], dg[:].rearrange("a b x h -> a (b x h)"),
                             start=True, stop=True).then_inc(cbp, 1)
            pe.wait_ge(kmd, 1)
            for b in range(NB):
                if b >= 2:
                    pe.wait_ge(std, 4 * b - 4)
                for h in range(H):
                    rows = halves[h % 2]
                    last = nc.tensor.matmul(ps[rows, 4 + b % 2, (h // 2) * DV:(h // 2 + 1) * DV],
                                            km[:, b, h * DH:(h + 1) * DH], z[:, 1024 + h * DV:1024 + (h + 1) * DV],
                                            start=True, stop=True)
                last.then_inc(up, 1)

        @block.scalar
        def _(act):
            act.wait_ge(gsub, 3)
            nc.scalar.activation(e3[:], e3[:], ACT.Exp).then_inc(gexp, 1)

        @block.vector
        def _(dve):
            ch = core.dve
            h3 = lambda a: a.rearrange("b (h c) -> b h c", h=H)
            ch.mark(nc.vector.memset(qd[:], 0.0))
            dve.wait_ge(g_in, 64)
            ch.link(nc.vector.tensor_tensor(gt[:, 1, :], gt[:, 1, :], gt[:, 2, :], ALU.add))
            nc.vector.tensor_tensor(mt[:], gt[:, 0, :], gt[:, 1, :], ALU.max).then_inc(md, 1)
            dve.wait_ge(md, 1)
            nc.vector.tensor_tensor(e3[:, 0, :], gt[:, 1, :], mt[:], ALU.subtract).then_inc(gsub, 1)
            nc.vector.tensor_tensor(e3[:, 1, :], gt[:, 0, :], mt[:], ALU.subtract).then_inc(gsub, 1)
            nc.vector.tensor_scalar(e3[:, 2, :], mt[:], -1.0, None, ALU.mult).then_inc(gsub, 1)
            dve.wait_ge(z_in, 16)
            ch.link(nc.vector.tensor_tensor(tmp[:], z[:, 0:512], z[:, 512:1024], ALU.mult))
            ch.link(nc.vector.tensor_reduce(qk[:], h3(tmp[:]), AX.X, ALU.add))
            ch.link(nc.vector.tensor_tensor(tmp[:], z[:, 0:512], nn[:], ALU.mult))
            ch.link(nc.vector.tensor_reduce(qn[:], h3(tmp[:]), AX.X, ALU.add))
            dve.wait_ge(tr, 1)
            q4 = ps[:, 0, 0:4 * NB].rearrange("p (j b) -> p b j", j=4)
            nc.vector.tensor_copy(qd[halves[0], :, :, 0], q4[halves[0]]).then_inc(qdd, 1)
            nc.vector.tensor_copy(qd[halves[1], :, :, 1], q4[halves[1]]).then_inc(qdd, 1)
            ch.link(nc.vector.tensor_copy(vt[:].rearrange("p h b -> p (h b)"), ps[:, 0, 4 * NB:12 * NB]))
            dve.wait_ge(gexp, 1)
            ch.link(nc.vector.tensor_tensor(qk[:], qk[:], e3[:, 1, :], ALU.mult))
            ch.link(nc.vector.tensor_tensor(qn[:], qn[:], e3[:, 0, :], ALU.mult))
            ch.link(nc.vector.tensor_tensor(qn[:], qn[:], qk[:], ALU.add))
            ch.link(nc.vector.scalar_tensor_tensor(qn[:], qn[:], -1.0, qn[:], ALU.mult, ALU.max))
            ch.link(nc.vector.tensor_tensor(qn[:], qn[:], e3[:, 2, :], ALU.max))
            ch.link(nc.vector.reciprocal(qn[:], qn[:]))
            ch.mark(nc.vector.tensor_copy(co[:, 0, :], e3[:, 0, :]))
            ch.mark(nc.vector.tensor_tensor(co[:, 1, :], e3[:, 0, :], qn[:], ALU.mult))
            ch.link(nc.vector.tensor_tensor(co[:, 2, :], qk[:], qn[:], ALU.mult))
            nc.vector.tensor_tensor(dg[:].rearrange("a b x h -> a b (x h)"),
                                    co[:].rearrange("a x h -> a (x h)").unsqueeze(1).to_broadcast([NB, NB, 3 * H]),
                                    bc(ident[0:NB, 0:NB], [NB, NB, 3 * H]), ALU.mult).then_inc(dgd, 1)
            ch.link(nc.vector.tensor_tensor(h3(kw[:]), h3(z[:, 512:1024]), bc(e3[:, 1, :], [NB, H, DH]), ALU.mult))
            nc.vector.tensor_tensor(km[:], kw[:].unsqueeze(1).to_broadcast([NB, NB, 512]),
                                    bc(ident[0:NB, 0:NB], [NB, NB, 512]), ALU.mult).then_inc(kmd, 1)
            ch.link(nc.vector.tensor_tensor(h3(nn[:]), h3(nn[:]), bc(e3[:, 0, :], [NB, H, DH]), ALU.mult))
            nc.vector.tensor_tensor(nn[:], nn[:], kw[:], ALU.add).then_inc(nd, 1)
            dve.wait_ge(cbp, 1)
            ch.link(nc.vector.tensor_copy(cb[:].rearrange("p b x h -> p (b x h)"), ps[:, 2, 0:NB * 3 * H]))
            ch.mark(nc.vector.tensor_copy(d2[halves[0]], cb[halves[0], :, 0, 0::2]))
            ch.mark(nc.vector.tensor_copy(d2[halves[1]], cb[halves[1], :, 0, 1::2]))
            dve.wait_ge(hq, 1)
            ch.mark(nc.vector.tensor_tensor(ht[:], cb[:, :, 1, :].rearrange("p b h -> p h b"),
                                            ps[:, 1, 0:NB * H].rearrange("p (b h) -> p h b", b=NB), ALU.mult))
            ch.link(nc.vector.tensor_tensor(vt[:], vt[:], cb[:, :, 2, :].rearrange("p b h -> p h b"), ALU.mult))
            nc.vector.tensor_tensor(ht[:], ht[:], vt[:], ALU.add).then_inc(hd, 1)
            for b in range(NB):
                dve.wait_ge(up, b + 1)
                for j in range(4):
                    nc.vector.scalar_tensor_tensor(st[:, b, j, :], st[:, b, j, :], d2[:, b, j:j + 1],
                                                   ps[:, 4 + b % 2, j * DV:(j + 1) * DV], ALU.mult,
                                                   ALU.add).then_inc(std, 1)


def seg3(ap):
    return ap.rearrange("p (s c) -> p s c", s=3)


def project_across(core, nk, p0, cols, rhs, bank, release):
    nc, ps = core.nc, core.ps
    hi, lo = rhs
    m = cols.stop - cols.start
    for k in range(nk):
        w_hi, w_lo = core.weight(p0 + k, cols)
        for i, (w, x) in enumerate(((w_hi, hi), (w_hi, lo), (w_lo, hi))):
            for s in range(3):
                last = nc.tensor.matmul(ps[0:m, bank + s, 0:SEG], w, x[:, k, s * SEG:(s + 1) * SEG],
                                        start=(k == 0 and i == 0), stop=(k == nk - 1 and i == 2))
        if release:
            last.then_inc(core.w_used, 1)
    return last


class Groups:

    def __init__(self, core, name, groups, nk):
        self.core, self.nk, self.per, self.n = core, nk, CW // P, groups * (CW // P)
        self.p0 = core.taken
        core.taken += groups * nk
        self.mm = core.sem(name)

    def product(self, pe, u, rhs):
        g, m = divmod(u, self.per)
        if m == 0:
            pe.wait_ge(self.core.w_lo, self.p0 + (g + 1) * self.nk)
        end = m == self.per - 1
        last = project_across(self.core, self.nk, self.p0 + g * self.nk, slice(m * P, (m + 1) * P), rhs,
                              3 * (u % 2), end)
        if not end:
            last.then_inc(self.mm, 1)

    def wait(self, eng, u):
        if u % self.per == self.per - 1:
            eng.wait_ge(self.core.w_used, self.p0 + (u // self.per + 1) * self.nk)
        else:
            eng.wait_ge(self.mm, u + 1 - (u + 1) // self.per)


def banks(core, u):
    return core.ps[:, 3 * (u % 2):3 * (u % 2) + 3, 0:SEG]


def gate_projections(core):
    nc, sem, sb = core.nc, core.sem, core.sb
    with ExitStack() as c:
        sg = sb("e_sg", [P, 2, T], ctx=c)
        hm = sb("e_hm", [P, 2, T], ctx=c)
        units = Groups(core, "e_mm", 6, KD)
        ev, mul = sem("e_ev"), sem("e_mul")
        h_in = [sem(f"e_hin{i}") for i in range(2)]
        out = [sem(f"e_out{i}") for i in range(2)]
        block = c.enter_context(nc.Block())

        @block.sync
        def _(sp):
            for u in range(2):
                sp.dma_start(hm[:, u, :], core.h_mem[u]).then_inc(h_in[u], 16)
            core.load_weights(core.taken + 8)

        @block.gpsimd
        def _(pool):
            core.split_weights(core.taken + 8)

        @block.tensor
        def _(pe):
            for u in range(units.n):
                if u >= 2:
                    pe.wait_ge(ev, u - 1)
                units.product(pe, u, (core.hhi, core.hlo))

        @block.scalar
        def _(act):
            for u in range(units.n):
                units.wait(act, u)
                if u >= 2:
                    act.wait_ge(out[u % 2], 16 * (u // 2))
                nc.scalar.activation(seg3(sg[:, u % 2, :]), banks(core, u), ACT.Sigmoid).then_inc(ev, 1)
                if u < KD:
                    act.wait_ge(mul, u + 1)
                    act.dma_start(core.hm_t[u], hm[:, u % 2, :]).then_inc(out[u % 2], 16)
                    if u + 2 < KD:
                        act.wait_ge(out[u % 2], 16 * (u // 2 + 1))
                        act.dma_start(hm[:, u % 2, :], core.h_mem[u + 2]).then_inc(h_in[u % 2], 16)
                else:
                    act.wait_ge(ev, u + 1)
                    act.dma_start(core.gates[u - KD], sg[:, u % 2, :]).then_inc(out[u % 2], 16)
            for i in range(2):
                act.wait_ge(out[i], 16 * units.n // 2)

        @block.vector
        def _(dve):
            for u in range(KD):
                dve.wait_ge(ev, u + 1)
                dve.wait_ge(h_in[u % 2], 16 * (u // 2 + 1))
                nc.vector.tensor_tensor(hm[:, u % 2, :], hm[:, u % 2, :], sg[:, u % 2, :], ALU.mult).then_inc(mul, 1)


def merge_product(core, tag, src, nk, gate0):
    nc, sem, sb, acc = core.nc, core.sem, core.sb, core.acc
    with ExitStack() as c:
        hi = sb(f"{tag}_hi", [P, nk, T], F32R, c)
        lo = sb(f"{tag}_lo", [P, nk, T], F32R, c)
        rw = sb(f"{tag}_rw", [P, 2, T], ctx=c)
        units = Groups(core, f"{tag}_mm", 2, nk)
        his, los, ev, add = sem(f"{tag}_his"), sem(f"{tag}_los"), sem(f"{tag}_ev"), sem(f"{tag}_add")
        r_in = [sem(f"{tag}_in{i}") for i in range(2)]
        block = c.enter_context(nc.Block())

        @block.sync
        def _(sp):
            for k in range(nk):
                if k >= 2:
                    sp.wait_ge(los, k - 1)
                sp.dma_start(rw[:, k % 2, :], src[k]).then_inc(r_in[k % 2], 16)
            core.load_weights(core.taken + 8)

        @block.gpsimd
        def _(pool):
            core.split_weights(core.taken + 8)

        @block.scalar
        def _(act):
            for k in range(nk):
                act.wait_ge(r_in[k % 2], 16 * (k // 2 + 1))
                nc.scalar.activation(hi[:, k, :], rw[:, k % 2, :], ACT.Copy).then_inc(his, 1)
            for u in range(KD):
                if u < 2:
                    act.wait_ge(los, nk - 1 + u)
                else:
                    act.wait_ge(ev, u - 1)
                act.dma_start(rw[:, u % 2, :], core.gates[gate0 + u]).then_inc(r_in[u % 2], 16)

        @block.vector
        def _(dve):
            for k in range(nk):
                dve.wait_ge(his, k + 1)
                nc.vector.tensor_tensor(lo[:, k, :], rw[:, k % 2, :], hi[:, k, :].bitcast(F32),
                                        ALU.subtract).then_inc(los, 1)
            for u in range(KD):
                units.wait(dve, u)
                dve.wait_ge(r_in[u % 2], 16 * (nk // 2 + u // 2 + 1))
                if gate0 == 0:
                    nc.vector.tensor_tensor(seg3(acc[:, u, :]), banks(core, u), seg3(rw[:, u % 2, :]),
                                            ALU.mult).then_inc(ev, 1)
                else:
                    nc.vector.tensor_tensor(seg3(rw[:, u % 2, :]), banks(core, u), seg3(rw[:, u % 2, :]),
                                            ALU.mult).then_inc(add, 1)
                    dve.wait_ge(add, u + 1)
                    nc.vector.tensor_tensor(acc[:, u, :], acc[:, u, :], rw[:, u % 2, :], ALU.add).then_inc(ev, 1)

        @block.tensor
        def _(pe):
            pe.wait_ge(los, nk)
            for u in range(KD):
                if u >= 2:
                    pe.wait_ge(ev, u - 1)
                units.product(pe, u, (hi, lo))


def output_projection(core):
    nc, t, sem, sb, acc, ident, ps = core.nc, core.t, core.sem, core.sb, core.acc, core.ident, core.ps
    with ExitStack() as c:
        hi = sb("o_hi", [P, KD, T], F32R, c)
        lo = sb("o_lo", [P, KD, T], F32R, c)
        xr = sb("o_x", [P, 2, D], ctx=c)
        units = Groups(core, "o_mm", 2, KD)
        his, los, tr, xt, ev = (sem(f"o_{x}") for x in ("his", "los", "tr", "xt", "ev"))
        x_in = [sem(f"o_xin{i}") for i in range(2)]
        block = c.enter_context(nc.Block())

        @block.sync
        def _(sp):
            for n in range(NT + 1):
                if n >= 2:
                    sp.wait_ge(tr, 2 * n - 2)
                if n < NT:
                    sp.dma_start(xr[:, n % 2, :], t["x_prompt"][0, n * P:(n + 1) * P, :]).then_inc(x_in[n % 2], 16)
                else:
                    sp.dma_start(xr[0:NB, n % 2, :], t["x_sample"].rearrange("b s d -> (b s) d")).then_inc(x_in[n % 2], 16)
            core.load_weights(core.taken + 8)

        @block.gpsimd
        def _(pool):
            core.split_weights(core.taken + 8)

        @block.scalar
        def _(act):
            for k in range(KD):
                nc.scalar.activation(hi[:, k, :], acc[:, k, :], ACT.Copy).then_inc(his, 1)
            act.wait_ge(los, KD)
            for v in range(2 * (NT + 1)):
                n, kk = divmod(v, 2)
                cols = P if n < NT else NB
                act.wait_ge(tr, v + 1)
                nc.scalar.activation(acc[:, 4 * kk:4 * kk + 4, n * P:n * P + cols],
                                     ps[:, 6 + v % 2, :].rearrange("p (k c) -> p k c", k=4)[:, :, 0:cols],
                                     ACT.Copy).then_inc(xt, 1)

        @block.vector
        def _(dve):
            for k in range(KD):
                dve.wait_ge(his, k + 1)
                nc.vector.tensor_tensor(lo[:, k, :], acc[:, k, :], hi[:, k, :].bitcast(F32), ALU.subtract).then_inc(los, 1)
            dve.wait_ge(xt, 2 * (NT + 1))
            for u in range(KD):
                units.wait(dve, u)
                nc.vector.tensor_tensor(seg3(acc[:, u, :]), seg3(acc[:, u, :]), banks(core, u), ALU.add).then_inc(ev, 1)

        @block.tensor
        def _(pe):
            for v in range(2 * (NT + 1)):
                n, kk = divmod(v, 2)
                rows = P if n < NT else NB
                pe.wait_ge(x_in[n % 2], 16 * (n // 2 + 1))
                if v >= 2:
                    pe.wait_ge(xt, v - 1)
                for k in range(4):
                    last = nc.tensor.transpose(ps[:, 6 + v % 2, k * P:k * P + rows],
                                               xr[0:rows, n % 2, (4 * kk + k) * P:(4 * kk + k + 1) * P],
                                               ident[0:rows, 0:rows])
                last.then_inc(tr, 1)
            for u in range(KD):
                if u >= 2:
                    pe.wait_ge(ev, u - 1)
                units.product(pe, u, (hi, lo))


def norm_ffn_input(core):
    nc, t, sem, sb, acc, ps = core.nc, core.t, core.sem, core.sb, core.acc, core.ps
    hi, lo = core.h2hi, core.h2lo
    with ExitStack() as c:
        g2 = sb("n_g", [P, KD], ctx=c)
        sq = sb("n_sq", [P, 2, T], ctx=c)
        rs = sb("n_rs", [P, T], ctx=c)
        g_in, sqd, mm, var, std, scl, his, los = (sem(f"n_{x}") for x in
                                                  ("gin", "sq", "mm", "var", "std", "scl", "hi", "lo"))
        block = c.enter_context(nc.Block())

        @block.sync
        def _(sp):
            with nc.allow_non_contiguous_dma(reason="1024 gains"):
                sp.dma_start(g2[:], t["norm2_g"].rearrange("(k p) -> p k", p=P)).then_inc(g_in, 16)
            core.load_weights(core.taken + 8)
            sp.wait_ge(g_in, 16)

        @block.tensor
        def _(pe):
            for k in range(KD):
                pe.wait_ge(sqd, k + 1)
                for s in range(3):
                    last = nc.tensor.matmul(ps[:, s, 0:SEG], core.ones[:], sq[:, k % 2, s * SEG:(s + 1) * SEG],
                                            start=(k == 0), stop=(k == KD - 1))
                last.then_inc(mm, 1)

        @block.scalar
        def _(act):
            for k in range(KD):
                if k >= 2:
                    act.wait_ge(mm, k - 1)
                nc.scalar.activation(sq[:, k % 2, :], acc[:, k, :], ACT.Square).then_inc(sqd, 1)
            act.wait_ge(var, 1)
            nc.scalar.activation(rs[:], rs[:], ACT.Sqrt).then_inc(std, 1)
            for k in range(KD):
                act.wait_ge(scl, k + 1)
                nc.scalar.activation(hi[:, k, :], sq[:, k % 2, :], ACT.Copy).then_inc(his, 1)

        @block.vector
        def _(dve):
            ch = core.dve
            dve.wait_ge(mm, KD)
            nc.vector.tensor_scalar(seg3(rs[:]), ps[:, 0:3, 0:SEG], 1.0 / D, EPS, ALU.mult, ALU.add).then_inc(var, 1)
            dve.wait_ge(std, 1)
            ch.link(nc.vector.reciprocal(rs[:], rs[:]))
            dve.wait_ge(g_in, 16)
            for k in range(KD):
                if k >= 2:
                    dve.wait_ge(los, k - 1)
                nc.vector.scalar_tensor_tensor(sq[:, k % 2, :], acc[:, k, :], g2[:, k:k + 1], rs[:], ALU.mult,
                                               ALU.mult).then_inc(scl, 1)
                dve.wait_ge(his, k + 1)
                nc.vector.tensor_tensor(lo[:, k, :], sq[:, k % 2, :], hi[:, k, :].bitcast(F32),
                                        ALU.subtract).then_inc(los, 1)


def ffn(core):
    nc, sem, sb, acc = core.nc, core.sem, core.sb, core.acc
    J = DFF // 256
    p0 = core.taken
    core.taken += J * (KD + 4)
    with ExitStack() as c:
        sg = sb("ff_sg", [P, T], ctx=c)
        fh = sb("ff_hi", [P, 2, 2, T], F32R, c)
        fl = sb("ff_lo", [P, 2, 2, T], F32R, c)
        mm, sil, mul, his, los, add = (sem(f"ff_{x}") for x in ("mm", "sil", "mul", "hi", "lo", "add"))
        block = c.enter_context(nc.Block())

        def first(j):
            return p0 + j * (KD + 4) - (4 if j else 0)

        def first_down(j):
            return first(j + 1) + KD if j < J - 1 else p0 + J * (KD + 4) - 4

        order = []
        for j in range(J + 1):
            if j < J:
                order += [("gu", j, m) for m in range(4)]
            if j >= 1:
                order += [("dn", j - 1, m) for m in range(KD)]
        index = {x: i for i, x in enumerate(order)}
        ends = {}
        n = 0
        for i, (kind, j, m) in enumerate(order):
            frees = (kind == "gu" and m == 3) or (kind == "dn" and m in (3, 7))
            if not frees:
                n += 1
            ends[i] = (frees, n)

        def complete(eng, x):
            kind, j, m = x
            frees, count = ends[index[x]]
            if not frees:
                eng.wait_ge(mm, count)
            elif kind == "gu":
                eng.wait_ge(core.w_used, first(j) + KD)
            else:
                eng.wait_ge(core.w_used, first_down(j) + (2 if m == 3 else 4))

        def taken(eng, i):
            kind, j, m = order[i]
            if kind == "dn":
                eng.wait_ge(add, KD * j + m + 1)
            elif m % 2 == 0:
                eng.wait_ge(sil, 2 * j + m // 2 + 1)
            else:
                eng.wait_ge(mul, 2 * j + m // 2 + 1)

        def res(i):
            return core.ps[:, 3 * (i % 2):3 * (i % 2) + 3, 0:SEG]

        @block.sync
        def _(sp):
            core.load_weights(core.taken + 8)

        @block.gpsimd
        def _(pool):
            core.split_weights(core.taken + 8)

        @block.tensor
        def _(pe):
            for i, (kind, j, m) in enumerate(order):
                if i >= 2:
                    taken(pe, i - 2)
                frees = ends[i][0]
                if kind == "gu":
                    if m == 0:
                        pe.wait_ge(core.w_lo, first(j) + KD)
                    tile, up = divmod(m, 2)
                    at = 256 * up + P * tile
                    last = project_across(core, KD, first(j), slice(at, at + P), (core.h2hi, core.h2lo), 3 * (i % 2), frees)
                else:
                    p = first_down(j) + (0 if m < 4 else 2)
                    if m % 4 == 0:
                        pe.wait_ge(core.w_lo, p + 2)
                    if m == 0:
                        pe.wait_ge(los, 2 * j + 2)
                    last = project_across(core, 2, p, slice(P * (m % 4), P * (m % 4) + P),
                                          (fh[:, j % 2], fl[:, j % 2]), 3 * (i % 2), frees)
                if not frees:
                    last.then_inc(mm, 1)

        @block.scalar
        def _(act):
            for j in range(J):
                for tile in range(2):
                    v = 2 * j + tile
                    x = ("gu", j, 2 * tile)
                    complete(act, x)
                    if v >= 1:
                        act.wait_ge(los, v)
                    nc.scalar.activation(seg3(sg[:]), res(index[x]), ACT.Silu).then_inc(sil, 1)
                    act.wait_ge(mul, v + 1)
                    if j >= 2:
                        complete(act, ("dn", j - 2, 7))
                    nc.scalar.activation(fh[:, j % 2, tile, :], sg[:], ACT.Copy).then_inc(his, 1)

        @block.vector
        def _(dve):
            def split(v):
                j, tile = divmod(v, 2)
                x = ("gu", j, 2 * tile + 1)
                complete(dve, x)
                dve.wait_ge(sil, v + 1)
                nc.vector.tensor_tensor(seg3(sg[:]), seg3(sg[:]), res(index[x]), ALU.mult).then_inc(mul, 1)
                dve.wait_ge(his, v + 1)
                nc.vector.tensor_tensor(fl[:, j % 2, tile, :], sg[:], fh[:, j % 2, tile, :].bitcast(F32),
                                        ALU.subtract).then_inc(los, 1)

            for j in range(J + 1):
                if j < J:
                    split(2 * j)
                    split(2 * j + 1)
                if j >= 1:
                    for m in range(KD):
                        x = ("dn", j - 1, m)
                        complete(dve, x)
                        if j >= 2:
                            dve.wait_ge(add, KD * (j - 2) + m + 1)
                        nc.vector.tensor_tensor(seg3(acc[:, m, :]), seg3(acc[:, m, :]), res(index[x]),
                                                ALU.add).then_inc(add, 1)


def store_output(core):
    nc, o, sem, sb, acc, ps = core.nc, core.o, core.sem, core.sb, core.acc, core.ps
    with ExitStack() as c:
        yt = sb("y_t", [P, 2, D], ctx=c)
        tr, ea, ev = sem("y_tr"), sem("y_ea"), sem("y_ev")
        out = [core.store_sem(f"y_out{i}") for i in range(2)]
        block = c.enter_context(nc.Block())

        @block.tensor
        def _(pe):
            for n in range(NT + 1):
                cols = P if n < NT else NB
                if n >= 2:
                    pe.wait_ge(ea, n - 1)
                    pe.wait_ge(ev, n - 1)
                for k in range(KD):
                    last = nc.tensor.transpose(ps[0:cols, 2 * (n % 2) + k // 4, (k % 4) * P:(k % 4 + 1) * P],
                                               acc[:, k, n * P:n * P + cols], core.ident[:])
                last.then_inc(tr, 1)

        def half(n, k):
            rows = P if n < NT else NB
            return yt[0:rows, n % 2, k * 512:(k + 1) * 512], ps[0:rows, 2 * (n % 2) + k, :]

        @block.scalar
        def _(act):
            for n in range(NT + 1):
                act.wait_ge(tr, n + 1)
                if n >= 2:
                    act.wait_ge(out[n % 2], 16 * (n // 2))
                nc.scalar.activation(*half(n, 0), ACT.Copy).then_inc(ea, 1)

        @block.vector
        def _(dve):
            for n in range(NT + 1):
                dve.wait_ge(tr, n + 1)
                if n >= 2:
                    dve.wait_ge(out[n % 2], 16 * (n // 2))
                nc.vector.tensor_copy(*half(n, 1)).then_inc(ev, 1)

        @block.sync
        def _(sp):
            for n in range(NT + 1):
                sp.wait_ge(ea, n + 1)
                sp.wait_ge(ev, n + 1)
                dst = o[0][0, n * P:(n + 1) * P, :] if n < NT else o[1].rearrange("b s d -> (b s) d")
                rows = P if n < NT else NB
                sp.dma_start(dst, yt[0:rows, n % 2, :]).then_inc(out[n % 2], 16)
            for i in range(2):
                sp.wait_ge(out[i], 16 * (NT // 2 + (i == 0)))
            sp.wait_ge(core.cache_out, 16 * len(core.copies))


def program(nc, t, o, stop=99):
    with ExitStack() as top:
        core = Core(nc, t, o, top)
        core.pieces = core.pieces[:{1: 24, 2: 72, 3: 104}.get(stop, 9999)]
        with ExitStack() as ch:
            core.hhi = core.sb("hhi", [P, KD, T], F32R, ch)
            core.hlo = core.sb("hlo", [P, KD, T], F32R, ch)
            core.phase = []
            norm_input(core)
            for g in range(G):
                with ExitStack() as cg:
                    core.qT = core.sb(f"qT{g}", [P, 4, S], ctx=cg)
                    core.kT = core.sb(f"kT{g}", [P, 4, S], ctx=cg)
                    core.vv = core.sb(f"vv{g}", [P, NT, 512], ctx=cg)
                    project_attention(core, g)
                    attend(core, g)
                core.clear_phase()
                if stop == 1: return
            merge_groups(core)
            if stop == 2: return
            with ExitStack() as cm:
                core.igf = core.sb("igf", [8, T], ctx=cm)
                core.lfg = core.sb("lfg", [8, T], ctx=cm)
                project_mlstm(core)
                core.clear_phase()
                core.bands = core.sb("bands", [P, S], ctx=cm)
                core.neg_m = core.sb("neg_m", [8, S], ctx=cm)
                mlstm_gates(core)
                mlstm_chunks(core)
                core.clear_phase()
            if stop == 3: return
            sample_attention(core)
            core.clear_phase()
            sample_mlstm(core)
            core.clear_phase()
            gate_projections(core)
            core.clear_phase()
        with ExitStack() as ca:
            core.acc = core.sb("acc", [P, KD, T], ctx=ca)
            merge_product(core, "f", core.att_t, 4, 0)
            merge_product(core, "m", core.hm_t, KD, KD)
            core.clear_phase()
            output_projection(core)
            core.clear_phase()
            core.h2hi = core.sb("h2hi", [P, KD, T], F32R, ca)
            core.h2lo = core.sb("h2lo", [P, KD, T], F32R, ca)
            norm_ffn_input(core)
            ffn(core)
            core.clear_phase()
            store_output(core)


def rope_tables():
    import numpy as np
    half = DH // 8
    pos = np.concatenate([np.arange(S), [PAST]]).astype(np.float32)
    freq = np.exp(np.float32(-math.log(500000.0)) * np.arange(0, 2 * half, 2, dtype=np.float32) / np.float32(2 * half))
    ang = pos[:, None] * freq[None, :].astype(np.float32)
    c, s = np.cos(ang), np.sin(ang)
    return np.concatenate([c, c, -s, s], axis=1).astype(np.float32)


def alternate_mask():
    import numpy as np
    q, k = np.arange(P)[:, None], np.arange(P)[None, :]
    return np.where((q >= k) & ((q - k) % 2 == 0), 0.0, NEG).astype(np.float32)


_INS = ["x_prompt", "x_sample", "cache_kv_w128", "cache_kv_w512", "cache_kv_w2048", "state_mlstm_C", "state_mlstm_n",
        "state_mlstm_m", "norm1_g", "w_in", "b_if", "q_norm_g", "k_norm_g", "w_att_out", "w_m_out", "w_o", "norm2_g",
        "w_gate", "w_up", "w_down"]
_OUTS = [(1, S, D), (NB, 1, D)] + [(1, min(w, S), 2, H, DH) for w in WINDOWS] + \
    [(1, H, DH, DV), (1, H, DH), (1, H)] + [(NB, w, 2, H, DH) for w in WINDOWS] + \
    [(NB, H, DH, DV), (NB, H, DH), (NB, H)]


def kernel(**inputs):
    import numpy as _np
    import concourse.bacc as _bacc
    from concourse.bass_utils import run_bass_kernel_spmd as _run

    nc = _bacc.Bacc("TRN2", target_bir_lowering=False, num_devices=1)
    arrays = {f"in_{n}": _np.ascontiguousarray(inputs[n]) for n in _INS}
    arrays["in_rope_table"], arrays["in_mask_halves"] = rope_tables(), alternate_mask()
    t = {n[3:]: nc.dram_tensor(n, a.shape, mybir.dt.from_np(a.dtype), kind="ExternalInput").ap()
         for n, a in arrays.items()}
    o = [nc.dram_tensor(f"out_{i}", s, F32, kind="ExternalOutput").ap() for i, s in enumerate(_OUTS)]
    program(nc, t, o)
    r = _run(nc, [arrays], core_ids=[0])
    return tuple(r.results[0][f"out_{i}"] for i in range(len(_OUTS)))
```

```python
import math
from contextlib import ExitStack

import concourse.bass as bass
from concourse import mybir

F32 = mybir.dt.float32
F32R = mybir.dt.float32r
ALU = mybir.AluOpType
ACT = mybir.ActivationFunctionType
AX = mybir.AxisListType

P = 128
D = 1024
S = 1024
NB = 8
T = S + NB
SEG = T // 3
KD = D // P
NT = S // P
H = 8
DH = 64
DV = 128
G = 3
WINDOWS = (128, 512, 2048)
DILS = (1, 4, 16)
AW = G * H * DH
DFF = 2816
EPS = 1e-6
NEG = -1e30
SCALE = DH ** -0.5
CQM, CKM, CVM, COM = 3 * AW, 3 * AW + 512, 3 * AW + 1024, 3 * AW + 2048
CIF = COM + 1024
CGA, CGB = CIF + 16, CIF + 16 + 1024
CW = 512
RAW = 3
RING = 15
PAST = 2048


def bc(ap, shape):
    return ap.unsqueeze(len(shape) - 1).to_broadcast(shape)


STEPS = tuple(min(d, S // P) for d in DILS)


def residues(ap, g, n):
    length = S // STEPS[g]
    r, i = n * P // length, n * P % length
    if len(ap.shape) == 2:
        return ap.rearrange("p (i d) -> p d i", d=STEPS[g])[:, r, i:i + P]
    return ap.rearrange("p k (i d) -> p k d i", d=STEPS[g])[:, :, r, i:i + P]


def token_rows(ap, g, n):
    length = S // STEPS[g]
    return ap.rearrange("(i d) c -> d i c", d=STEPS[g])[n * P // length, n * P % length:n * P % length + P, :]


def has_prev(g, n):
    return n * P % (S // STEPS[g]) != 0


class Chain:

    def __init__(self, eng, sem):
        self.eng, self.sem, self.n = eng, sem, 0

    def mark(self, ins):
        self.n += 1
        ins.then_inc(self.sem, 1)
        return self.n

    def wait(self, n=None):
        self.eng.wait_ge(self.sem, self.n if n is None else n)

    def link(self, ins):
        self.mark(ins)
        self.wait()


def weight_pieces(t):
    w_in = t["w_in"]
    cols = [x * AW + g * 512 for g in range(G) for x in range(3)] + [CQM, CKM, CVM, CVM + 512]
    cols += [CGA, CGA + 512, CGB, CGB + 512, COM, COM + 512]
    out = [[(w_in[k * P:(k + 1) * P, c:c + CW], 0)] for c in cols for k in range(KD)]
    for name, nk in (("w_att_out", 4), ("w_m_out", KD), ("w_o", KD)):
        out += [[(t[name][k * P:(k + 1) * P, c:c + CW], 0)] for c in (0, CW) for k in range(nk)]
    down = []
    for j in range(DFF // 256):
        out += [[(t["w_gate"][k * P:(k + 1) * P, j * 256:(j + 1) * 256], 0),
                 (t["w_up"][k * P:(k + 1) * P, j * 256:(j + 1) * 256], 256)] for k in range(KD)]
        out += down
        down = [[(t["w_down"][(2 * j + k) * P:(2 * j + k + 1) * P, c:c + CW], 0)] for c in (0, CW) for k in range(2)]
    out += down
    return out


def cache_copies(t, o):
    out = []
    for g, w in enumerate(WINDOWS):
        cache = t[f"cache_kv_w{w}"].rearrange("b w a h c -> b (w a h c)")
        new = o[8 + g].rearrange("b w a h c -> b (w a h c)")
        row = 2 * H * DH
        for b in range(NB):
            for r in range(0, w - 1, P):
                n = min(P, w - 1 - r) * row
                src = cache[b, (r + 1) * row:(r + 1) * row + n].rearrange("(a c) -> a c", a=16)
                out.append((new[b, r * row:r * row + n].rearrange("(a c) -> a c", a=16), src))
    return out


class Core:

    def __init__(self, nc, t, o, top):
        self.nc, self.t, self.o, self.top = nc, t, o, top
        self.phase = None
        sb, sem, dram = self.sb, self.sem, self.dram
        self.ps = top.enter_context(nc.psum_tensor("ps", [P, 8, 512], F32))

        self.pieces = weight_pieces(t)
        self.raw = sb("raw", [P, RAW, CW])
        self.whi = sb("whi", [P, RING, CW], F32R)
        self.wlo = sb("wlo", [P, RING, CW], F32R)
        self.raw_in = [sem(f"raw_in{i}") for i in range(RAW)]
        self.w_hi, self.w_lo, self.w_used = sem("w_hi"), sem("w_lo"), sem("w_used")
        self.landed, at = [], [0] * RAW
        for p, parts in enumerate(self.pieces):
            at[p % RAW] += 16 * len(parts)
            self.landed.append(at[p % RAW])
        self.loaded = self.split = self.taken = 0
        self.copies = cache_copies(t, o)
        self.copied = 0
        self.cache_out = sem("cache_out")

        names = [f"b_zout{g}_{i}" for g in (*range(G), "m") for i in range(4)]
        names += ["g_mout", "c_out", "s_rows", "r_out", "y_out0", "y_out1"]
        self.stores = {name: sem(name) for name in names}

        self.ident = sb("ident", [P, P])
        self.mask_pair = sb("mask_pair", [P, 2 * P])
        self.mask_halves = sb("mask_halves", [P, P])
        self.mask_later = sb("mask_later", [P, P])
        self.ones = sb("ones", [P, P])
        self.gq = sb("gq", [P, DH])
        self.gk = sb("gk", [P, DH])
        self.rope = sb("rope", [P, G, NT + 1, 32])
        self.mstat = sb("mstat", [P, G, NT, 2, H])

        self.z_s = dram("z_s", (G, 3, NB, 512))
        self.m_tok = dram("m_tok", (NT, P, 3, 512))
        self.m_tr = dram("m_tr", (2, NT, P, 512))
        self.zm_s = dram("zm_s", (NB, 2048))
        self.if_s = dram("if_s", (2, H, NB))
        self.om_s = dram("om_s", (KD, P, NB))
        self.a_tr = dram("a_tr", (G, 2, NT, P, 512))
        self.a_v = dram("a_v", (G, NT, P, 512))
        self.o_grp = dram("o_grp", (G, NT, P, 512))
        self.ml_nat = dram("ml_nat", (G, S, 16))
        self.cf_nat = dram("cf_nat", (G, S, 8))
        self.h_mem = dram("h_mem", (KD, P, T))
        self.gates = dram("gates", (2 * KD, P, T))
        self.att_t = dram("att_t", (4, P, T))
        self.hm_t = dram("hm_t", (KD, P, T))

        self.dve = Chain(nc.vector, sem("dve_c"))
        self.act = Chain(nc.scalar, sem("act_c"))
        self.pool = Chain(nc.gpsimd, sem("pool_c"))

    def sem(self, name):
        handle = self.nc.alloc_semaphore(name=name)
        if self.phase is not None:
            self.phase.append(handle)
        return handle

    def store_sem(self, name):
        return self.stores[name]

    def clear_phase(self):
        nc, handles = self.nc, self.phase or []
        if handles:
            with nc.Block() as block:
                @block.gpsimd
                def _(pool):
                    for h in handles:
                        pool.sem_clear(h)
        for h in handles:
            nc.release_semaphore(h)
        self.phase = []

    def sb(self, name, shape, dt=F32, ctx=None):
        return (ctx or self.top).enter_context(self.nc.sbuf_tensor(name, shape, dt))

    def dram(self, name, shape):
        return self.nc.dram_tensor(name, shape, F32, kind="Internal").ap()

    def load_weights(self, until):
        sp = self.nc.sync
        for p in range(self.loaded, min(until + RAW, len(self.pieces))):
            if p >= RAW:
                sp.wait_ge(self.w_lo, p - RAW + 1)
            for src, c in self.pieces[p]:
                sp.dma_start(self.raw[:, p % RAW, c:c + src.shape[1]], src).then_inc(self.raw_in[p % RAW], 16)
            self.loaded = p + 1
            while self.copied < len(self.copies) * (p + 1) // len(self.pieces):
                dst, src = self.copies[self.copied]
                sp.dma_start(dst, src).then_inc(self.cache_out, 16)
                self.copied += 1

    def split_weights(self, until):
        pool = self.nc.gpsimd
        for p in range(self.split, min(until, len(self.pieces))):
            pool.wait_ge(self.raw_in[p % RAW], self.landed[p])
            if p >= RING:
                pool.wait_ge(self.w_used, p - RING + 1)
            pool.tensor_copy(self.whi[:, p % RING, :], self.raw[:, p % RAW, :]).then_inc(self.w_hi, 1)
            pool.wait_ge(self.w_hi, p + 1)
            pool.tensor_tensor(self.wlo[:, p % RING, :], self.raw[:, p % RAW, :],
                               self.whi[:, p % RING, :].bitcast(F32), ALU.subtract).then_inc(self.w_lo, 1)
            self.split = p + 1

    def weight(self, p, cols):
        return self.whi[:, p % RING, cols], self.wlo[:, p % RING, cols]


def products(nc, out, lhs, rhs, start, stop):
    nc.tensor.matmul(out, lhs[0], rhs[0], start=start, stop=False)
    nc.tensor.matmul(out, lhs[0], rhs[1], start=False, stop=False)
    return nc.tensor.matmul(out, lhs[1], rhs[0], start=False, stop=stop)


def norm_input(core):
    nc, t, ps, sem, sb = core.nc, core.t, core.ps, core.sem, core.sb
    ident, hhi, hlo = core.ident, core.hhi, core.hlo
    with ExitStack() as c:
        x_sb = sb("x_sb", [P, NT + 1, D], ctx=c)
        g1 = sb("g1", [P, D], ctx=c)
        sq_a = sb("sq_a", [P, 2, D], ctx=c)
        ssq = sb("ssq", [P, NT + 1], ctx=c)
        a_in = [sem(f"a_in{n}") for n in range(NT + 1)]
        a_g, a_const, a_ssq, a_var, a_std, a_xn = (sem(x) for x in ("a_g", "a_const", "a_ssq", "a_var", "a_std", "a_xn"))
        a_tr, a_hi, a_lo = sem("a_tr"), sem("a_hi"), sem("a_lo")
        c_in = sem("c_in")
        block = c.enter_context(nc.Block())

        @block.sync
        def _(sp):
            for n in range(NT):
                sp.dma_start(x_sb[:, n, :], t["x_prompt"][0, n * P:(n + 1) * P, :]).then_inc(a_in[n], 16)
            sp.dma_start(x_sb[0:NB, NT, :], t["x_sample"].rearrange("b s d -> (b s) d")).then_inc(a_in[NT], 16)
            sp.dma_start(g1[:], t["norm1_g"].rearrange("(a d) -> a d", a=1).to_broadcast([P, D])).then_inc(a_g, 16)
            sp.dma_start(core.gq[:], t["q_norm_g"].rearrange("(a d) -> a d", a=1).to_broadcast([P, DH])).then_inc(c_in, 16)
            sp.dma_start(core.mask_halves[:], t["mask_halves"]).then_inc(c_in, 16)
            sp.dma_start(core.gk[:], t["k_norm_g"].rearrange("(a d) -> a d", a=1).to_broadcast([P, DH])).then_inc(c_in, 16)
            for g in range(G):
                for n in range(NT):
                    sp.dma_start(core.rope[:, g, n, :], token_rows(t["rope_table"][0:S, :], g, n)).then_inc(c_in, 16)
                sp.dma_start(core.rope[0:NB, g, NT, :], t["rope_table"][S:S + 1, :].to_broadcast([NB, 32])).then_inc(c_in, 16)
            core.load_weights(8)
            sp.wait_ge(c_in, 16 * (3 + G * NT + G))

        @block.gpsimd
        def _(pool):
            ch = core.pool
            ch.link(pool.memset(ident[:], 0.0))
            ch.link(pool.affine_select(out=ident[:], in_=ident[:], compare_op=ALU.not_equal, fill=1.0, base=0,
                                       pattern=[[-1, P]], channel_multiplier=1))
            pool.memset(core.ones[:], 1.0).then_inc(a_const, 1)
            for m in (core.mask_pair, core.mask_later):
                ch.mark(pool.memset(m[:], 0.0))
            ch.wait()
            ch.mark(pool.affine_select(out=core.mask_pair[:, 0:P], in_=core.mask_pair[:, 0:P], compare_op=ALU.is_ge, fill=NEG,
                                       base=0, pattern=[[1, P]], channel_multiplier=-1))
            ch.mark(pool.affine_select(out=core.mask_pair[:, P:2 * P], in_=core.mask_pair[:, P:2 * P], compare_op=ALU.is_ge,
                                       fill=NEG, base=0, pattern=[[-1, P]], channel_multiplier=1))
            ch.mark(pool.affine_select(out=core.mask_later[:], in_=core.mask_later[:], compare_op=ALU.is_ge, fill=NEG,
                                       base=0, pattern=[[1, P]], channel_multiplier=-1))
            ch.wait()
            pool.memset(core.mstat[:], 0.0).then_inc(a_const, 1)
            core.split_weights(8)

        @block.scalar
        def _(act):
            ch = core.act
            for n in range(NT + 1):
                rows = P if n < NT else NB
                act.wait_ge(a_in[n], 16)
                if n == 0:
                    act.wait_ge(a_var, 1)
                if n >= 2:
                    ch.wait(ch.n - 1)
                ch.mark(nc.scalar.activation(sq_a[0:rows, n % 2, :], x_sb[0:rows, n, :], ACT.Square,
                                             accum_out=ssq[0:rows, n:n + 1]))
            ch.wait()
            nc.scalar.activation(ssq[0:1, 0:1], ssq[0:1, 0:1], ACT.Copy).then_inc(a_ssq, 1)
            act.wait_ge(a_var, 2)
            nc.scalar.activation(ssq[:], ssq[:], ACT.Sqrt).then_inc(a_std, 1)
            for u in range(2 * (NT + 1)):
                n, kk = divmod(u, 2)
                cols = P if n < NT else NB
                act.wait_ge(a_tr, u + 1)
                nc.scalar.activation(hhi[:, 4 * kk:4 * kk + 4, n * P:n * P + cols],
                                     ps[:, u % 4, :].rearrange("p (k c) -> p k c", k=4)[:, :, 0:cols],
                                     ACT.Copy).then_inc(a_hi, 1)

        @block.vector
        def _(dve):
            ch = core.dve
            nc.vector.memset(ssq[:], 1.0).then_inc(a_var, 1)
            dve.wait_ge(a_ssq, 1)
            nc.vector.tensor_scalar(ssq[:], ssq[:], 1.0 / D, EPS, ALU.mult, ALU.add).then_inc(a_var, 1)
            dve.wait_ge(a_std, 1)
            ch.link(nc.vector.reciprocal(ssq[:], ssq[:]))
            dve.wait_ge(a_g, 16)
            for n in range(NT + 1):
                rows = P if n < NT else NB
                nc.vector.scalar_tensor_tensor(x_sb[0:rows, n, :], x_sb[0:rows, n, :], ssq[0:rows, n:n + 1],
                                               g1[0:rows, :], ALU.mult, ALU.mult).then_inc(a_xn, 1)
            for u in range(2 * (NT + 1)):
                n, kk = divmod(u, 2)
                cols = P if n < NT else NB
                dve.wait_ge(a_hi, u + 1)
                part = slice(4 * kk, 4 * kk + 4), slice(n * P, n * P + cols)
                nc.vector.tensor_tensor(hlo[:, part[0], part[1]],
                                        ps[:, u % 4, :].rearrange("p (k c) -> p k c", k=4)[:, :, 0:cols],
                                        hhi[:, part[0], part[1]].bitcast(F32), ALU.subtract).then_inc(a_lo, 1)

        @block.tensor
        def _(pe):
            pe.wait_ge(a_const, 1)
            for u in range(2 * (NT + 1)):
                n, kk = divmod(u, 2)
                rows = P if n < NT else NB
                pe.wait_ge(a_xn, n + 1)
                if u >= 4:
                    pe.wait_ge(a_lo, u - 3)
                for k in range(4):
                    last = nc.tensor.transpose(ps[:, u % 4, k * P:k * P + rows],
                                               x_sb[0:rows, n, (4 * kk + k) * P:(4 * kk + k + 1) * P],
                                               ident[0:rows, 0:rows])
                last.then_inc(a_tr, 1)



class Projection:

    Z = 4

    def __init__(self, core, c, g):
        self.core, self.g = core, g
        sb, sem, Z = core.sb, core.sem, self.Z
        self.groups = 3 if g is not None else 4
        self.units = self.groups * (NT + 1)
        self.nq = 2 * (NT + 1)
        self.steps = self.units + 2
        self.p0 = core.taken
        core.taken += self.groups * KD
        tag = "m" if g is None else g
        self.zt = sb(f"zt{tag}", [P, Z, 512], ctx=c)
        self.tt = sb(f"tt{tag}", [P, 2, 512], ctx=c)
        if g is not None:
            self.sq = sb(f"sq{g}", [P, 512], ctx=c)
            self.st = sb(f"st{g}", [P, Z, H], ctx=c)
            self.rt = sb(f"rt{g}", [P, 2, H, 16], ctx=c)
        (self.mm, self.ev, self.var, self.std, self.nrm, self.tr, self.tre) = (
            sem(f"b_{x}{tag}") for x in ("mm", "ev", "var", "std", "nrm", "tr", "tre"))
        self.zout = [core.store_sem(f"b_zout{tag}_{i}") for i in range(Z)]
        self.tout = [sem(f"b_tout{tag}_{i}") for i in range(2)]
        self.n_out, self.done_at = [0] * Z, {}
        for u in range(self.units):
            self.n_out[u % Z] += 16 * len(self.stores(u))
            self.done_at[u] = self.n_out[u % Z]

    def stores(self, u):
        core, g = self.core, self.g
        x, n = divmod(u, NT + 1)
        if g is None:
            if n == NT:
                return [core.zm_s[:, x * 512:(x + 1) * 512]]
            return [core.m_tok[n, :, x - 1, :]] if x else []
        if n == NT:
            return [core.z_s[g, x]]
        out = [core.a_v[g, n]] if x == 2 else []
        keep, length = min(WINDOWS[g], S), S // STEPS[g]
        if x and (keep == S or (n + 1) * P % length == 0):
            rows = core.o[2 + g][0][:, x - 1].rearrange("(i d) h c -> d i (h c)", d=STEPS[g])
            out.append(rows[n * P // length])
        return out

    def wait_turned(self, eng, u):
        m = min(u + 1, self.nq)
        eng.wait_ge(self.tr, m - m // (NT + 1))

    def wait_whole(self, eng, u):
        if self.g is not None and u < self.nq:
            eng.wait_ge(self.nrm, u + 1)
        else:
            eng.wait_ge(self.ev, u + 1)

    def pe(self, u):
        core, nc, ps, g = self.core, self.core.nc, self.core.ps, self.g
        pe = nc.tensor
        if u < self.units:
            x, n = divmod(u, NT + 1)
            rows = P if n < NT else NB
            if n == 0:
                pe.wait_ge(core.w_lo, self.p0 + (x + 1) * KD)
            if u >= 2:
                pe.wait_ge(self.ev, u - 1)
            for k in range(KD):
                if n == NT:
                    lhs = [a[:, k, S:T] for a in (core.hhi, core.hlo)]
                else:
                    lhs = [residues(a[:, k, 0:S], g or 0, n) for a in (core.hhi, core.hlo)]
                last = products(nc, ps[0:rows, u % 2, :], lhs, core.weight(self.p0 + x * KD + k, slice(0, CW)),
                                k == 0, k == KD - 1)
                if n == NT:
                    last.then_inc(core.w_used, 1)
            if n < NT:
                last.then_inc(self.mm, 1)
        v = u - 2
        if 0 <= v < self.nq and v % (NT + 1) < NT:
            self.wait_whole(pe, v)
            t = v - v // (NT + 1)
            if t >= 1:
                pe.wait_ge(self.tre, t)
            for j in range(4):
                last = pe.transpose(ps[:, 2, j * P:(j + 1) * P], self.zt[:, v % self.Z, j * P:(j + 1) * P],
                                    core.ident[:])
            last.then_inc(self.tr, 1)

    def act(self, u):
        core, nc, ps, g, Z = self.core, self.core.nc, self.core.ps, self.g, self.Z
        act = nc.scalar
        if u < self.units:
            x, n = divmod(u, NT + 1)
            rows = P if n < NT else NB
            if n < NT:
                act.wait_ge(self.mm, u + 1 - (u + 1) // (NT + 1))
            else:
                act.wait_ge(core.w_used, self.p0 + (x + 1) * KD)
            if u >= Z:
                self.wait_turned(act, u - Z)
                if self.done_at[u - Z]:
                    act.wait_ge(self.zout[u % Z], self.done_at[u - Z])
            act.activation(self.zt[0:rows, u % Z, :], ps[0:rows, u % 2, :], ACT.Copy,
                           scale=SCALE if g is None and x == 0 else 1.0).then_inc(self.ev, 1)
        v = u - 1
        if g is not None and 0 <= v < self.nq:
            rows = P if v % (NT + 1) < NT else NB
            act.wait_ge(self.var, v + 1)
            act.activation(self.st[0:rows, v % Z, :], self.st[0:rows, v % Z, :], ACT.Sqrt).then_inc(self.std, 1)
        v = u - 2
        if v < 0:
            return
        x, n = divmod(v, NT + 1)
        if v < self.nq and n < NT:
            t = v - v // (NT + 1)
            act.wait_ge(self.tr, t + 1)
            if t >= 2:
                act.wait_ge(self.tout[t % 2], 16 * (t // 2))
            act.activation(self.tt[:, t % 2, :], ps[:, 2, :], ACT.Copy).then_inc(self.tre, 1)
            act.wait_ge(self.tre, t + 1)
            dst = core.m_tr[x, n] if g is None else core.a_tr[g, x, n]
            act.dma_start(dst, self.tt[:, t % 2, :]).then_inc(self.tout[t % 2], 16)
        for dst in self.stores(v):
            self.wait_whole(act, v)
            act.dma_start(dst, self.zt[0:NB if n == NT else P, v % Z, :]).then_inc(self.zout[v % Z], 16)

    def act_end(self):
        for i in range(self.Z):
            self.core.nc.scalar.wait_ge(self.zout[i], self.n_out[i])
        for i in range(2):
            self.core.nc.scalar.wait_ge(self.tout[i], 16 * NT)

    def dve(self, u):
        core, nc, Z, ch, g = self.core, self.core.nc, self.Z, self.core.dve, self.g
        dve = nc.vector
        if g is None:
            return
        if u < self.nq:
            rows = P if u % (NT + 1) < NT else NB
            z, st = self.zt[0:rows, u % Z, :], self.st[0:rows, u % Z, :]
            dve.wait_ge(self.ev, u + 1)
            ch.link(dve.tensor_tensor(self.sq[0:rows, :], z, z, ALU.mult))
            ch.link(dve.tensor_reduce(st, self.sq[0:rows, :].rearrange("p (h c) -> p h c", h=H), AX.X, ALU.add))
            dve.tensor_scalar(st, st, 1.0 / DH, EPS, ALU.mult, ALU.add).then_inc(self.var, 1)
        v = u - 1
        if 0 <= v < self.nq:
            x, n = divmod(v, NT + 1)
            rows = P if n < NT else NB
            z = self.zt[0:rows, v % Z, :].rearrange("p (h c) -> p h c", h=H)
            st, r = self.st[0:rows, v % Z, :], self.rt[0:rows]
            gain = (core.gq, core.gk)[x][0:rows, :].unsqueeze(1).to_broadcast([rows, H, DH])
            tab = core.rope[0:rows, g, n, :].unsqueeze(1).to_broadcast([rows, H, 32])
            dve.wait_ge(self.std, v + 1)
            ch.link(dve.reciprocal(st, st))
            ch.link(dve.tensor_tensor(z, z, bc(st, [rows, H, DH]), ALU.mult))
            ch.link(dve.tensor_tensor(z, z, gain, ALU.mult))
            ch.mark(dve.tensor_tensor(r[:, 0], z[:, :, 0:16], tab[:, :, 0:16], ALU.mult))
            ch.mark(dve.tensor_tensor(r[:, 1, :, 0:8], z[:, :, 8:16], tab[:, :, 16:24], ALU.mult))
            ch.link(dve.tensor_tensor(r[:, 1, :, 8:16], z[:, :, 0:8], tab[:, :, 24:32], ALU.mult))
            dve.tensor_tensor(z[:, :, 0:16], r[:, 0], r[:, 1], ALU.add).then_inc(self.nrm, 1)


class Attention:

    def __init__(self, core, c, g):
        self.core, self.g = core, g
        sb, sem = core.sb, core.sem
        self.items = [(n, hh) for n in range(NT) for hh in range(2)]
        self.steps = len(self.items) + 2
        self.q = sb(f"aq{g}", [P, 2, 4, P], ctx=c)
        self.k = sb(f"ak{g}", [P, 3, 4, P], ctx=c)
        self.v = sb(f"av{g}", [P, 4, 512], ctx=c)
        self.sc = sb(f"sc{g}", [P, 2, 4, 2 * P], ctx=c)
        self.pt = sb(f"pt{g}", [P, 4, 2 * P], ctx=c)
        self.nm = sb(f"nm{g}", [P, 2, 4], ctx=c)
        self.ot = sb(f"ot{g}", [P, 2, 512], ctx=c)
        (self.qk, self.msk, self.neg, self.prb, self.ptr, self.pte_a, self.pte_v, self.pv, self.oev) = (
            sem(f"t_{x}{g}") for x in ("qk", "msk", "neg", "prb", "ptr", "pte_a", "pte_v", "pv", "oev"))
        self.o_out = [sem(f"t_out{g}_{i}") for i in range(2)]
        self.t_in = [sem(f"t_in{g}_{i}") for i in range(2)]

    def blocks(self, n):
        return [n - 1, n] if has_prev(self.g, n) else [n]

    def heads(self, hh):
        return [(4 * hh + 2 * i + par, par, i) for i in range(2) for par in range(2)]

    def load(self, n):
        act, core, g = self.core.nc.scalar, self.core, self.g
        for dst, src in ((self.q[:, n % 2], core.a_tr[g, 0, n].rearrange("p (j c) -> p j c", j=4)),
                         (self.k[:, n % 3], core.a_tr[g, 1, n].rearrange("p (j c) -> p j c", j=4)),
                         (self.v[:, n % 4, :], core.a_v[g, n])):
            act.dma_start(dst, src).then_inc(self.t_in[n % 2], 16)

    def pe(self, i):
        core, ps = self.core, self.core.ps
        pe = core.nc.tensor
        if i < len(self.items):
            n, hh = self.items[i]
            tiles = self.blocks(n)
            if hh == 0:
                pe.wait_ge(self.t_in[n % 2], 48 * (n // 2 + 1))
            if i >= 1:
                pe.wait_ge(self.msk, i)
            for h, par, j in self.heads(hh):
                rows = slice(DH * par, DH * par + DH)
                for b, m in enumerate(tiles):
                    at = (2 * j + b) * P
                    last = pe.matmul(ps[:, 3 + par, at:at + P], self.q[rows, n % 2, h // 2, :],
                                     self.k[rows, m % 3, h // 2, :], start=True, stop=True)
            last.then_inc(self.qk, 1)
        w = i - 2
        if w >= 0:
            n, hh = self.items[w]
            tiles = self.blocks(n)
            pe.wait_ge(self.pte_a, w + 1)
            pe.wait_ge(self.pte_v, w + 1)
            if hh == 0 and n >= 1:
                pe.wait_ge(self.oev, n)
            for h, par, j in self.heads(hh):
                for b, m in enumerate(tiles):
                    last = pe.matmul(ps[:, 7, h * DH:(h + 1) * DH], self.pt[:, 2 * par + j, b * P:(b + 1) * P],
                                     self.v[:, m % 4, h * DH:(h + 1) * DH], start=(b == 0),
                                     stop=(b == len(tiles) - 1))
            last.then_inc(self.pv, 1)
        w = i - 1
        if 0 <= w < len(self.items):
            n, hh = self.items[w]
            pe.wait_ge(self.prb, w + 1)
            if w >= 1:
                pe.wait_ge(self.pte_a, w)
                pe.wait_ge(self.pte_v, w)
            for h, par, j in self.heads(hh):
                for b in range(len(self.blocks(n))):
                    at = (2 * j + b) * P
                    last = pe.transpose(ps[:, 5 + par, at:at + P], self.sc[:, w % 2, 2 * par + j, b * P:(b + 1) * P],
                                        core.ident[:])
            last.then_inc(self.ptr, 1)

    def dve_first(self, i):
        core, ps, g, ch = self.core, self.core.ps, self.g, self.core.dve
        dve = core.nc.vector
        w = i - 1
        if not 0 <= w < len(self.items):
            return
        n, hh = self.items[w]
        span = P * len(self.blocks(n))
        mask = core.mask_halves[:] if g == 2 else core.mask_pair[:, 2 * P - span:]
        dve.wait_ge(self.qk, w + 1)
        if w >= 2:
            dve.wait_ge(self.ptr, w - 1)
            dve.wait_ge(self.prb, w - 1)
        for h, par, j in self.heads(hh):
            ins = dve.tensor_tensor_reduce(self.sc[:, w % 2, 2 * par + j, 0:span],
                                           ps[:, 3 + par, 2 * j * P:2 * j * P + span], mask, SCALE, 3 * NEG,
                                           ALU.add, ALU.max, core.mstat[:, g, n, 0, h:h + 1])
            if (par, j) == (1, 1):
                ins.then_inc(self.msk, 1)
            else:
                ch.mark(ins)
        ch.wait()
        dve.wait_ge(self.msk, w + 1)
        dve.tensor_scalar(self.nm[:, w % 2, :], core.mstat[:, g, n, 0, 4 * hh:4 * hh + 4], -1.0, None,
                          ALU.mult).then_inc(self.neg, 1)

    def act_first(self, i):
        core, g, ch = self.core, self.g, self.core.act
        act = core.nc.scalar
        if i == 0:
            self.load(0)
            self.load(1)
        elif i % 2 == 0 and 2 <= i // 2 + 1 < NT:
            act.wait_ge(self.qk, i)
            if i >= 4:
                act.wait_ge(self.pv, i - 3)
            self.load(i // 2 + 1)
        w = i - 1
        if not 0 <= w < len(self.items):
            return
        n, hh = self.items[w]
        span = P * len(self.blocks(n))
        act.wait_ge(self.neg, w + 1)
        for h, par, j in self.heads(hh):
            row = self.sc[:, w % 2, 2 * par + j, 0:span]
            ins = act.activation(row, row, ACT.Exp, bias=self.nm[:, w % 2, h - 4 * hh:h - 4 * hh + 1],
                                 accum_out=core.mstat[:, g, n, 1, h:h + 1])
            if (par, j) == (1, 1):
                ins.then_inc(self.prb, 1)
            else:
                ch.mark(ins)

    def take(self, eng, copy, par, w, sem):
        eng.wait_ge(self.ptr, w + 1)
        if w >= 1:
            eng.wait_ge(self.pv, w)
        span = P * len(self.blocks(self.items[w][0]))
        copy(self.pt[:, 2 * par:2 * par + 2, 0:span],
             self.core.ps[:, 5 + par, :].rearrange("p (i c) -> p i c", i=2)[:, :, 0:span]).then_inc(sem, 1)

    def dve_last(self, i):
        dve, ps = self.core.nc.vector, self.core.ps
        if 1 <= i <= len(self.items):
            self.take(dve, dve.tensor_copy, 1, i - 1, self.pte_v)
        if i >= 3 and i % 2 == 1:
            n = (i - 3) // 2
            dve.wait_ge(self.pv, 2 * n + 2)
            if n >= 2:
                dve.wait_ge(self.o_out[n % 2], 16 * (n // 2))
            dve.tensor_copy(self.ot[:, n % 2, :], ps[:, 7, :]).then_inc(self.oev, 1)

    def act_last(self, i):
        act = self.core.nc.scalar
        if 1 <= i <= len(self.items):
            self.take(act, act.copy, 0, i - 1, self.pte_a)
        if i >= 3 and i % 2 == 1:
            n = (i - 3) // 2
            act.wait_ge(self.oev, n + 1)
            act.dma_start(self.core.o_grp[self.g, n], self.ot[:, n % 2, :]).then_inc(self.o_out[n % 2], 16)

    def act_end(self):
        for i in range(2):
            self.core.nc.scalar.wait_ge(self.o_out[i], 16 * NT // 2)


def project(core, g, att_g, with_gates):
    nc = core.nc
    with ExitStack() as c:
        proj = Projection(core, c, g)
        att = Attention(core, c, att_g) if att_g is not None else None
        gates = Gates(core, c) if with_gates else None
        steps = range(max(proj.steps, att.steps if att else 0))
        block = c.enter_context(nc.Block())

        @block.sync
        def _(sp):
            if gates:
                gates.load()
            core.load_weights(core.taken + 8)
            if gates:
                gates.store_m()

        @block.gpsimd
        def _(pool):
            core.split_weights(core.taken + 8)

        @block.tensor
        def _(pe):
            if gates:
                gates.pe()
            for i in steps:
                if i < proj.steps:
                    proj.pe(i)
                if att and i < att.steps:
                    att.pe(i)

        @block.scalar
        def _(act):
            if gates:
                gates.act()
            for i in steps:
                if att and i < att.steps:
                    att.act_first(i)
                if i < proj.steps:
                    proj.act(i)
                if att and i < att.steps:
                    att.act_last(i)
            proj.act_end()
            if att:
                att.act_end()

        @block.vector
        def _(dve):
            if gates:
                gates.dve()
            for i in steps:
                if att and i < att.steps:
                    att.dve_first(i)
                if i < proj.steps:
                    proj.dve(i)
                if att and i < att.steps:
                    att.dve_last(i)


def merge_groups(core):
    nc, ps, sem, sb = core.nc, core.ps, core.sem, core.sb
    with ExitStack() as c:
        ml = sb("ml", [P, NT, G, 2, H], ctx=c)
        mx = sb("mx", [P, NT, H], ctx=c)
        cf = sb("cf", [P, NT, G, H], ctx=c)
        cr = sb("cr", [P, G, NT, H], ctx=c)
        og = sb("og", [P, 3, 512], ctx=c)
        at = sb("at", [P, 4, S], ctx=c)
        m_out, m_in, e_sub, e_exp, c_done, c_out, c_in, scaled, tr, added, a_out = (sem(f"m_{x}") for x in
            ("out", "in", "sub", "exp", "done", "cout", "cin", "scaled", "tr", "added", "aout"))
        o_in = [sem(f"m_oin{i}") for i in range(3)]
        units = [(g, n) for g in range(G) for n in range(NT)]
        block = c.enter_context(nc.Block())

        @block.scalar
        def _(act):
            for g, n in units:
                act.dma_start(token_rows(core.ml_nat[g], g, n),
                              core.mstat[:, g, n].rearrange("p a h -> p (a h)")).then_inc(m_out, 16)
            act.wait_ge(m_out, 16 * len(units))
            for g in range(G):
                act.dma_start(ml[:, :, g].rearrange("p n a h -> p n (a h)"),
                              core.ml_nat[g].rearrange("(n p) c -> p n c", p=P)).then_inc(m_in, 16)
            act.wait_ge(e_sub, 1)
            nc.scalar.activation(cf[:], cf[:], ACT.Exp).then_inc(e_exp, 1)
            act.wait_ge(c_done, 1)
            for g in range(G):
                act.dma_start(core.cf_nat[g].rearrange("(n p) c -> p n c", p=P), cf[:, :, g, :]).then_inc(c_out, 16)
            act.wait_ge(c_out, 16 * G)
            for g, n in units:
                act.dma_start(cr[:, g, n], token_rows(core.cf_nat[g], g, n)).then_inc(c_in, 16)
            act.wait_ge(added, len(units))
            act.dma_start(core.att_t[:, :, 0:S].rearrange("k p t -> p k t"), at[:]).then_inc(a_out, 16)
            act.wait_ge(a_out, 16)

        @block.sync
        def _(sp):
            for u, (g, n) in enumerate(units):
                if u >= 3:
                    sp.wait_ge(tr, u - 2)
                sp.dma_start(og[:, u % 3, :], core.o_grp[g, n]).then_inc(o_in[u % 3], 16)
            core.load_weights(core.taken + 8)

        @block.vector
        def _(dve):
            ch = core.dve
            dve.wait_ge(m_in, 16 * G)
            m = [ml[:, :, g, 0, :] for g in range(G)]
            ch.link(nc.vector.tensor_tensor(mx[:], m[0], m[1], ALU.max))
            ch.link(nc.vector.tensor_tensor(mx[:], mx[:], m[2], ALU.max))
            for g in range(G - 1):
                ch.mark(nc.vector.tensor_tensor(cf[:, :, g, :], m[g], mx[:], ALU.subtract))
            ch.wait()
            nc.vector.tensor_tensor(cf[:, :, G - 1, :], m[G - 1], mx[:], ALU.subtract).then_inc(e_sub, 1)
            dve.wait_ge(e_exp, 1)
            for g in range(G):
                ch.link(nc.vector.tensor_tensor(ml[:, :, g, 1, :], ml[:, :, g, 1, :], cf[:, :, g, :], ALU.mult))
            ch.link(nc.vector.tensor_tensor(mx[:], ml[:, :, 0, 1, :], ml[:, :, 1, 1, :], ALU.add))
            ch.link(nc.vector.tensor_tensor(mx[:], mx[:], ml[:, :, 2, 1, :], ALU.add))
            ch.link(nc.vector.reciprocal(mx[:], mx[:]))
            for g in range(G - 1):
                ch.mark(nc.vector.tensor_tensor(cf[:, :, g, :], cf[:, :, g, :], mx[:], ALU.mult))
            ch.wait()
            nc.vector.tensor_tensor(cf[:, :, G - 1, :], cf[:, :, G - 1, :], mx[:], ALU.mult).then_inc(c_done, 1)
            dve.wait_ge(c_in, 16 * len(units))

            def scale(u):
                g, n = units[u]
                dve.wait_ge(o_in[u % 3], 16 * (u // 3 + 1))
                v = og[:, u % 3, :].rearrange("p (h c) -> p h c", h=H)
                nc.vector.tensor_tensor(v, v, bc(cr[:, g, n, :], [P, H, DH]), ALU.mult).then_inc(scaled, 1)

            scale(0)
            for u, (g, n) in enumerate(units):
                if u + 1 < len(units):
                    scale(u + 1)
                dve.wait_ge(tr, u + 1)
                dst = residues(at[:], g, n)
                src = ps[:, u % 2, :].rearrange("p (k c) -> p k c", k=4)
                if g == 0:
                    nc.vector.tensor_copy(dst, src).then_inc(added, 1)
                else:
                    if n == 0:
                        dve.wait_ge(added, u)
                    nc.vector.tensor_tensor(dst, dst, src, ALU.add).then_inc(added, 1)

        @block.tensor
        def _(pe):
            for u in range(len(units)):
                pe.wait_ge(scaled, u + 1)
                if u >= 2:
                    pe.wait_ge(added, u - 1)
                for j in range(4):
                    last = nc.tensor.transpose(ps[:, u % 2, j * P:(j + 1) * P], og[:, u % 3, j * P:(j + 1) * P],
                                               core.ident[:])
                last.then_inc(tr, 1)


class Gates:

    def __init__(self, core, c):
        self.core = core
        sb, sem = core.sb, core.sem
        self.w = sb("wif", [P, KD, 16], ctx=c)
        self.hi = sb("wif_hi", [P, KD, 40], F32R, c)
        self.lo = sb("wif_lo", [P, KD, 40], F32R, c)
        self.bias = sb("bif", [40, 1], ctx=c)
        self.yy = sb("yif", [40, T], ctx=c)
        self.ab = sb("aif", [40, T], ctx=c)
        self.ig = sb("igf", [8, T], ctx=c)
        self.lf = sb("lfg", [8, T], ctx=c)
        self.bb = sb("g_b", [8, S], ctx=c)
        self.mx = sb("g_m", [8, S], ctx=c)
        self.zero = sb("g_zero", [8, P], ctx=c)
        self.m_run = sb("g_run", [8, NT + 1], ctx=c)
        (self.w_in, self.w_hi, self.w_lo, self.mm, self.ab_set, self.ln, self.done, self.out, self.end) = (
            sem(f"g_{x}") for x in ("w_in", "w_hi", "w_lo", "mm", "ab_set", "ln", "done", "out", "end"))
        self.m_out = core.store_sem("g_mout")

    def load(self):
        t, sp = self.core.t, self.core.nc.sync
        sp.dma_start(self.w[:], t["w_in"].rearrange("(k p) c -> p k c", p=P)[:, :, CIF:CIF + 16]).then_inc(self.w_in, 16)
        for rows, at in ((slice(0, 8), 0), (slice(32, 40), 8)):
            sp.dma_start(self.bias[rows, :], t["b_if"].rearrange("(h a) -> h a", a=1)[at:at + 8, :]).then_inc(self.w_in, 16)

    def store_m(self):
        sp = self.core.nc.sync
        sp.wait_ge(self.end, 1)
        sp.dma_start(self.core.o[7].rearrange("a h -> h a"), self.m_run[:, NT:NT + 1]).then_inc(self.m_out, 16)
        sp.wait_ge(self.m_out, 16)

    def pe(self):
        core, nc = self.core, self.core.nc
        nc.tensor.wait_ge(self.w_lo, 2)
        for s in range(3):
            seg = slice(s * SEG, (s + 1) * SEG)
            for k in range(KD):
                last = products(nc, core.ps[0:40, 5 + s, 0:SEG], (self.hi[:, k, :], self.lo[:, k, :]),
                                (core.hhi[:, k, seg], core.hlo[:, k, seg]), k == 0, k == KD - 1)
        last.then_inc(self.mm, 1)

    def act(self):
        act, core = self.core.nc.scalar, self.core
        ab = self.ab[32:40, :]
        act.wait_ge(self.ab_set, 1)
        act.activation(ab, ab, ACT.Exp, scale=-1.0).then_inc(self.ln, 1)
        act.wait_ge(self.ln, 1)
        act.activation(ab, ab, ACT.Ln, bias=1.0).then_inc(self.ln, 1)
        act.wait_ge(self.done, 1)
        act.dma_start(core.if_s[0], self.ig[0:8, S:T]).then_inc(self.out, 16)
        act.dma_start(core.if_s[1], self.lf[0:8, S:T]).then_inc(self.out, 16)
        act.wait_ge(self.out, 32)

    def dve(self):
        core, ch = self.core, self.core.dve
        dve, bands, neg_m = core.nc.vector, core.bands, core.neg_m
        ig, lf, bb, mx, zero, m_run = self.ig, self.lf, self.bb, self.mx, self.zero, self.m_run
        yy, ab = self.yy[32:40, :], self.ab[32:40, :]
        for w in (self.hi, self.lo):
            ch.mark(dve.memset(w[:].bitcast(F32), 0.0))
        ch.mark(dve.memset(zero[:], 0.0))
        ch.mark(dve.memset(m_run[:], 0.0))
        ch.mark(dve.memset(bands[:], 0.0))
        dve.wait_ge(self.w_in, 48)
        ch.wait()
        for at, frm in ((0, 0), (32, 8)):
            dve.tensor_copy(self.hi[:, :, at:at + 8], self.w[:, :, frm:frm + 8]).then_inc(self.w_hi, 1)
        dve.wait_ge(self.w_hi, 2)
        for at, frm in ((0, 0), (32, 8)):
            dve.tensor_tensor(self.lo[:, :, at:at + 8], self.w[:, :, frm:frm + 8],
                              self.hi[:, :, at:at + 8].bitcast(F32), ALU.subtract).then_inc(self.w_lo, 1)
        dve.wait_ge(self.mm, 1)
        src = core.ps[:, 5:8, 0:SEG]
        ch.mark(dve.tensor_scalar(seg3(ig[0:8, :]), src[0:8], self.bias[0:8, :], None, ALU.add))
        ch.link(dve.tensor_scalar(seg3(yy), src[32:40], self.bias[32:40, :], None, ALU.add))
        dve.scalar_tensor_tensor(ab, yy, -1.0, yy, ALU.mult, ALU.max).then_inc(self.ab_set, 1)
        dve.wait_ge(self.ab_set, 1)
        ch.link(dve.tensor_scalar(yy, yy, 0.0, None, ALU.min))
        dve.wait_ge(self.ln, 2)
        dve.tensor_tensor(lf[0:8, :], yy, ab, ALU.subtract).then_inc(self.done, 1)
        dve.wait_ge(self.done, 1)
        for n in range(NT):
            cols = slice(n * P, (n + 1) * P)
            ch.mark(dve.tensor_tensor_scan(bb[:, cols], lf[0:8, cols], zero[:], 0.0, ALU.add, ALU.add))
        ch.wait()
        ch.link(dve.tensor_tensor(bands[0:8, :], ig[0:8, 0:S], bb[:], ALU.subtract))
        for n in range(NT):
            cols = slice(n * P, (n + 1) * P)
            end = slice(n * P + P - 1, n * P + P)
            ch.link(dve.tensor_tensor_scan(mx[:, cols], zero[:], bands[0:8, cols], m_run[:, n:n + 1], ALU.add, ALU.max))
            ch.mark(dve.tensor_tensor(m_run[:, n + 1:n + 2], bb[:, end], mx[:, end], ALU.add))
            ch.mark(dve.tensor_scalar(bands[32:40, cols], mx[:, cols], -1.0, m_run[:, n:n + 1], ALU.mult, ALU.add))
            ch.link(dve.tensor_scalar(bands[96:104, cols], bands[0:8, cols], mx[:, end], None, ALU.subtract))
        ch.mark(dve.scalar_tensor_tensor(bands[64:72, :], mx[:], -1.0, bb[:], ALU.mult, ALU.subtract))
        ch.link(dve.tensor_scalar(neg_m[:], mx[:], -1.0, None, ALU.mult))
        dve.tensor_copy(m_run[:, 0:1], zero[:, 0:1]).then_inc(self.end, 1)


class Chunks:

    STEPS = 5

    def __init__(self, core, c):
        self.core = core
        sb, sem = core.sb, core.sem
        self.E = E = DV + 1
        self.q = sb("c_q", [P, 2, 4, P], ctx=c)
        self.k = sb("c_k", [P, 2, 4, P], ctx=c)
        self.kk = sb("c_kk", [P, 2, H, DH], ctx=c)
        self.v = sb("c_v", [P, 2, H, E], ctx=c)
        self.st = sb("c_state", [P, 4, E], ctx=c)
        self.xt = sb("c_xt", [P, P], ctx=c)
        self.xe = sb("c_xe", [P, 3, H], ctx=c)
        self.ww = sb("c_w", [P, H, P], ctx=c)
        self.num = sb("c_num", [P, H, E], ctx=c)
        self.den = sb("c_den", [P, H], ctx=c)
        self.ht = sb("c_ht", [P, H, P], ctx=c)
        self.kw = sb("c_kw", [P, H, DH], ctx=c)
        self.dec = sb("c_dec", [P, 4], ctx=c)
        (self.one, self.st0, self.xtp, self.xts, self.xex, self.mb, self.kq, self.wm, self.wex, self.wqk,
         self.inter, self.nsc, self.intra, self.num_set, self.dstp, self.kwd, self.up, self.std, self.hbd,
         self.htp, self.hts, self.hts2, self.h_out) = (
            sem(f"c_{x}") for x in ("one", "st0", "xtp", "xts", "xex", "mb", "kq", "wm", "wex", "wqk", "inter",
                "nsc", "intra", "num_set", "dstp", "kwd", "up", "std", "hbd", "htp", "hts", "hts2", "h_out"))
        self.c_in = [sem(f"c_in{i}") for i in range(2)]
        self.c_out = core.store_sem("c_out")

    def at(self, h):
        return 4 * (h % 2) + h // 2

    def rows(self, h):
        return slice(DH * (h % 2), DH * (h % 2) + DH)

    def inter_at(self, h):
        i, E = h // 2, self.E
        return (2 if i < 3 else 6) + h % 2, slice((i % 3) * E, (i % 3 + 1) * E)

    def intra_at(self, h):
        E = self.E
        return 4 + h // 3, slice((h % 3) * E, (h % 3 + 1) * E)

    def update_at(self, h):
        i, E = h // 2, self.E
        return (2, slice(i * E, (i + 1) * E)) if i < 3 else (3, slice(P, P + E))

    def load(self, n):
        act, core, b = self.core.nc.scalar, self.core, n % 2
        for dst, src in ((self.q[:, b], core.m_tr[0, n].rearrange("p (j c) -> p j c", j=4)),
                         (self.k[:, b], core.m_tr[1, n].rearrange("p (j c) -> p j c", j=4)),
                         (self.kk[:, b], core.m_tok[n, :, 0, :].rearrange("p (h c) -> p h c", h=H)),
                         (self.v[:, b, :, 0:DV], core.m_tok[n, :, 1:3, :].rearrange("p x (h c) -> p (x h) c", c=DV))):
            act.dma_start(dst, src).then_inc(self.c_in[b], 16)

    def pe(self, i):
        core, ps = self.core, self.core.ps
        pe = core.nc.tensor
        n, step = divmod(i, self.STEPS)
        b, cols = n % 2, slice(n * P, (n + 1) * P)
        if step == 0:
            if n >= 1:
                pe.wait_ge(self.std, n + 1)
                pe.wait_ge(self.hts, n)
                pe.wait_ge(self.hts2, n)
            pe.transpose(ps[:, 7, 0:P], core.bands[:, cols], core.ident[:]).then_inc(self.xtp, 1)
            for h in range(H):
                last = pe.matmul(ps[:, 2 + h % 2, (h // 2) * P:(h // 2 + 1) * P],
                                 core.ident[0:H, h:h + 1].to_broadcast([H, P]), core.neg_m[:, cols],
                                 start=True, stop=True)
            last.then_inc(self.mb, 1)
            pe.wait_ge(self.c_in[b], 64 * (n // 2 + 1))
            for h in range(H):
                last = pe.matmul(ps[:, 4 + h % 2, (h // 2) * P:(h // 2 + 1) * P], self.k[self.rows(h), b, h // 2, :],
                                 self.q[self.rows(h), b, h // 2, :], start=True, stop=True)
            last.then_inc(self.kq, 1)
        elif step == 1:
            if n == 0:
                pe.wait_ge(self.st0, 1)
            pe.wait_ge(self.wm, 2 * n + 2)
            pe.wait_ge(self.xts, n + 1)
            for h in range(H):
                bank, at = self.inter_at(h)
                last = pe.matmul(ps[:, bank, at], self.q[self.rows(h), b, h // 2, :], self.st[self.rows(h), h // 2, :],
                                 start=True, stop=True)
            last.then_inc(self.inter, 1)
        elif step == 2:
            pe.wait_ge(self.wqk, 2 * n + 2)
            pe.wait_ge(self.nsc, n + 1)
            for h in range(H):
                bank, at = self.intra_at(h)
                last = pe.matmul(ps[:, bank, at], self.ww[:, self.at(h), :], self.v[:, b, h, :], start=True, stop=True)
            last.then_inc(self.intra, 1)
        elif step == 3:
            pe.wait_ge(self.nsc, n + 1)
            pe.matmul(ps[:, 3, 0:H], core.ident[:, P - 1:P].to_broadcast([P, P]), self.xe[:, 0, :],
                      start=True, stop=True).then_inc(self.dstp, 1)
            pe.wait_ge(self.kwd, n + 1)
            for h in range(H):
                bank, at = self.update_at(h)
                last = pe.matmul(ps[self.rows(h), bank, at], self.kw[:, h, :], self.v[:, b, h, :], start=True, stop=True)
            last.then_inc(self.up, 1)
        else:
            pe.wait_ge(self.hbd, n + 1)
            for h in range(H):
                last = pe.transpose(ps[:, 4 + h // 4, (h % 4) * P:(h % 4 + 1) * P], self.num[:, h, 0:DV], core.ident[:])
            last.then_inc(self.htp, 1)

    def dve_init(self):
        dve = self.core.nc.vector
        dve.memset(self.v[:], 1.0).then_inc(self.one, 1)
        dve.memset(self.st[:], 0.0).then_inc(self.st0, 1)
        dve.memset(self.dec[:], 0.0).then_inc(self.std, 1)

    def dve(self, i):
        core, ps, ch, E = self.core, self.core.ps, self.core.dve, self.E
        dve = core.nc.vector
        n, step = divmod(i, self.STEPS)
        b = n % 2
        quad = lambda a: a.rearrange("p (i c) -> p i c", i=4)
        if step == 0:
            dve.wait_ge(self.xtp, n + 1)
            if n >= 1:
                dve.wait_ge(self.wex, n)
            dve.tensor_copy(self.xt[:], ps[:, 7, 0:P]).then_inc(self.xts, 1)
            dve.wait_ge(self.mb, n + 1)
            if n >= 1:
                dve.wait_ge(self.intra, n)
            mask = core.mask_later[:].unsqueeze(1).to_broadcast([P, 4, P])
            for q in range(2):
                dve.tensor_tensor(self.ww[:, 4 * q:4 * q + 4, :], quad(ps[:, 2 + q, :]), mask, ALU.add).then_inc(self.wm, 1)
            dve.wait_ge(self.xex, n + 1)
            dve.wait_ge(self.c_in[b], 64 * (n // 2 + 1))
            if n >= 1:
                dve.wait_ge(self.up, n)
            dve.tensor_tensor(self.kw[:], self.kk[:, b], bc(self.xe[:, 2, :], [P, H, DH]), ALU.mult).then_inc(self.kwd, 1)
            dve.wait_ge(self.kq, n + 1)
            for q in range(2):
                dve.wait_ge(self.wex, 2 * n + q + 1)
                part = self.ww[:, 4 * q:4 * q + 4, :]
                dve.tensor_tensor(part, part, quad(ps[:, 4 + q, :]), ALU.mult).then_inc(self.wqk, 1)
        elif step == 2:
            dve.wait_ge(self.intra, n + 1)
            dve.wait_ge(self.nsc, n + 1)
            for q, k in ((0, 3), (1, 3), (2, 2)):
                part = self.num[:, 3 * q:3 * q + k, :]
                ins = dve.tensor_tensor(part, part, ps[:, 4 + q, 0:k * E].rearrange("p (i c) -> p i c", i=k), ALU.add)
                if q == 2:
                    ins.then_inc(self.num_set, 1)
                else:
                    ch.mark(ins)
            ch.wait()
            dve.wait_ge(self.num_set, n + 1)
            den, col = self.den[:], self.num[:, :, DV]
            ch.link(dve.scalar_tensor_tensor(den, col, -1.0, col, ALU.mult, ALU.max))
            ch.link(dve.tensor_tensor(den, den, self.xe[:, 1, :], ALU.max))
            ch.link(dve.reciprocal(den, den))
            part = self.num[:, :, 0:DV]
            dve.tensor_tensor(part, part, bc(den, [P, H, DV]), ALU.mult).then_inc(self.hbd, 1)
        elif step == 3:
            dve.wait_ge(self.dstp, n + 1)
            dve.wait_ge(self.up, n + 1)
            dve.wait_ge(self.std, n + 1)
            ch.mark(dve.tensor_copy(self.dec[0:DH, :], ps[0:DH, 3, 0:H:2]))
            ch.link(dve.tensor_copy(self.dec[DH:P, :], ps[DH:P, 3, 1:H:2]))
            for j in range(4):
                bank, at = self.update_at(2 * j)
                ins = dve.scalar_tensor_tensor(self.st[:, j, :], self.st[:, j, :], self.dec[:, j:j + 1],
                                               ps[:, bank, at], ALU.mult, ALU.add)
                if j == 3:
                    ch.wait()
                    ins.then_inc(self.std, 1)
                else:
                    ch.mark(ins)
        elif step == 4:
            dve.wait_ge(self.htp, n + 1)
            if n >= 1:
                dve.wait_ge(self.h_out, 16 * n)
            dve.tensor_copy(self.ht[:, 0:4, :], quad(ps[:, 4, :])).then_inc(self.hts, 1)

    def act(self, i):
        core, ps, ch = self.core, self.core.ps, self.core.act
        act = core.nc.scalar
        n, step = divmod(i, self.STEPS)
        if step == 0:
            act.wait_ge(self.xts, n + 1)
            if n >= 1:
                act.wait_ge(self.dstp, n)
                act.wait_ge(self.hbd, n)
                act.wait_ge(self.kwd, n)
            act.activation(self.xe[:], self.xt[:].rearrange("p (b c) -> p b c", b=4)[:, 1:4, 0:H],
                           ACT.Exp).then_inc(self.xex, 1)
            for h in [0, 2, 4, 6, 1, 3, 5, 7]:
                if h < 2:
                    act.wait_ge(self.wm, 2 * n + h + 1)
                row = self.ww[:, self.at(h), :]
                ins = act.activation(row, row, ACT.Exp, bias=self.xt[:, h:h + 1])
                if h >= 6:
                    ch.wait()
                    ins.then_inc(self.wex, 1)
                else:
                    ch.mark(ins)
        elif step == 1:
            act.wait_ge(self.inter, n + 1)
            act.wait_ge(self.xex, n + 1)
            if n >= 1:
                act.wait_ge(self.htp, n)
            for h in range(H):
                bank, at = self.inter_at(h)
                ins = act.activation(self.num[:, h, :], ps[:, bank, at], ACT.Copy, scale=self.xe[:, 0, h:h + 1])
                if h == H - 1:
                    ch.wait()
                    ins.then_inc(self.nsc, 1)
                else:
                    ch.mark(ins)
        elif step == 3:
            if n + 2 < NT:
                act.wait_ge(self.up, n + 1)
                self.load(n + 2)
        elif step == 4:
            act.wait_ge(self.htp, n + 1)
            if n >= 1:
                act.wait_ge(self.h_out, 16 * n)
            act.activation(self.ht[:, 4:8, :], ps[:, 5, :].rearrange("p (i c) -> p i c", i=4),
                           ACT.Copy).then_inc(self.hts2, 1)
            act.wait_ge(self.hts, n + 1)
            act.wait_ge(self.hts2, n + 1)
            act.dma_start(core.h_mem[:, :, n * P:(n + 1) * P].rearrange("k p t -> p k t"), self.ht[:]).then_inc(self.h_out, 16)

    def act_init(self):
        self.core.nc.scalar.wait_ge(self.one, 1)
        self.load(0)
        self.load(1)

    def store_state(self):
        nc, o, st = self.core.nc, self.core.o, self.st
        act = nc.scalar
        act.wait_ge(self.std, NT + 1)
        dst = o[5][0].rearrange("(j two) d e -> two d j e", two=2)
        dstn = o[6][0].rearrange("(j two) d -> two d j", two=2)
        with nc.allow_non_contiguous_dma(reason="the normaliser's column"):
            for two in range(2):
                rows = slice(DH * two, DH * two + DH)
                act.dma_start(dst[two], st[rows, :, 0:DV]).then_inc(self.c_out, 16)
                act.dma_start(dstn[two], st[rows, :, DV]).then_inc(self.c_out, 16)
        act.wait_ge(self.c_out, 64)
        act.wait_ge(self.h_out, 16 * NT)


def seg3(ap):
    return ap.rearrange("p (s c) -> p s c", s=3)


def sample_attention(core):
    nc, t, o, ps, sem, sb, ident = core.nc, core.t, core.o, core.ps, core.sem, core.sb, core.ident
    caches = [t["cache_kv_w128"], t["cache_kv_w512"], t["cache_kv_w2048"]]
    C = NB * G * H
    with ExitStack() as c:
        zs = sb("s_z", [NB, G, 3, 512], ctx=c)
        pr = sb("s_pr", [NB, G, 512], ctx=c)
        sn = sb("s_sn", [NB, G * H], ctx=c)
        dg = sb("s_dg", [NB, NB, G * H], ctx=c)
        kc = sb("s_kc", [P, 3, 512], ctx=c)
        qb = sb("s_qb", [P, 3, 512], ctx=c)
        vc = sb("s_vc", [P, 2, G, 512], ctx=c)
        ss = sb("s_ss", [P, NB, G, H], ctx=c)
        sa = sb("s_sa", [P, NB, G, H], ctx=c)
        nw = sb("s_nw", [P, NB, G, H], ctx=c)
        mx = sb("s_mx", [P, NB, H], ctx=c)
        ll = sb("s_ll", [P, NB, H], ctx=c)
        l3 = sb("s_l3", [P, NB, G, H], ctx=c)
        vt = sb("s_vt", [P, G, 4, NB], ctx=c)
        pn = sb("s_pn", [P, G, 4, NB], ctx=c)
        rl = sb("s_rl", [P, 4, NB], ctx=c)
        ot = sb("s_ot", [P, 4, NB], ctx=c)
        z_in, snd, dgd, bcp, nwd, prd, sc, amx, sub, ex, vtp, lp, pv, done, out = (sem(f"s_{x}") for x in
            ("zin", "sn", "dg", "bcp", "nw", "pr", "sc", "amx", "sub", "ex", "vtp", "lp", "pv", "done", "out"))
        rows_out = core.store_sem("s_rows")
        k_in = [sem(f"s_kin{i}") for i in range(3)]
        v_in = [sem(f"s_vin{i}") for i in range(2)]
        units = [(b, g) for b in range(NB) for g in range(G)]
        block = c.enter_context(nc.Block())

        def cached(g, b, which):
            return caches[g][b].rearrange("(j d) a h c -> d j a (h c)", d=DILS[g])[0, :, which]

        @block.sync
        def _(sp):
            sp.dma_start(zs[:], core.z_s.rearrange("g x b c -> b g x c")).then_inc(z_in, 16)
            for u, (b, g) in enumerate(units):
                if u >= 3:
                    sp.wait_ge(sc, u - 2)
                sp.dma_start(kc[:, u % 3, :], cached(g, b, 0)).then_inc(k_in[u % 3], 16)
                sp.dma_start(qb[:, u % 3, :], core.z_s[g, 0, b:b + 1, :].to_broadcast([P, 512])).then_inc(k_in[u % 3], 16)
            for g in range(G):
                sp.dma_start(o[8 + g][:, -1 + WINDOWS[g]].rearrange("b a h c -> b a (h c)"),
                             zs[:, g, 1:3, :]).then_inc(rows_out, 16)
            core.load_weights(core.taken + 8)
            sp.wait_ge(rows_out, 16 * G)

        @block.scalar
        def _(act):
            for b in range(NB):
                if b >= 2:
                    act.wait_ge(pv, b - 1)
                for g in range(G):
                    act.dma_start(vc[:, b % 2, g, :], cached(g, b, 1)).then_inc(v_in[b % 2], 16)
                if b == 1:
                    act.wait_ge(sub, 2)
                    nc.scalar.activation(ss[:], ss[:], ACT.Exp, scale=SCALE).then_inc(ex, 1)
                    nc.scalar.activation(nw[:], nw[:], ACT.Exp, scale=SCALE).then_inc(ex, 1)
            act.wait_ge(done, 1)
            act.dma_start(core.att_t[:, :, S:T].rearrange("k p b -> p k b"), ot[:]).then_inc(out, 16)
            act.wait_ge(out, 16)

        @block.gpsimd
        def _(pool):
            pool.wait_ge(sc, len(units))
            pool.partition_all_reduce(sa[:].rearrange("p b g h -> p (b g h)"), ss[:].rearrange("p b g h -> p (b g h)"),
                                      P, bass.bass_isa.ReduceOp.max).then_inc(amx, 1)

        @block.vector
        def _(dve):
            ch = core.dve
            dve.wait_ge(z_in, 16)
            ch.link(nc.vector.tensor_tensor(pr[:], zs[:, :, 0, :], zs[:, :, 1, :], ALU.mult))
            nc.vector.tensor_reduce(sn[:], pr[:].rearrange("b g (h c) -> b (g h) c", h=H), AX.X, ALU.add).then_inc(snd, 1)
            dve.wait_ge(snd, 1)
            nc.vector.tensor_tensor(dg[:], sn[:].unsqueeze(1).to_broadcast([NB, NB, G * H]),
                                    bc(ident[0:NB, 0:NB], [NB, NB, G * H]), ALU.mult).then_inc(dgd, 1)
            for u, (b, g) in enumerate(units):
                dve.wait_ge(k_in[u % 3], 32 * (u // 3 + 1))
                ch.link(nc.vector.tensor_tensor(kc[:, u % 3, :], kc[:, u % 3, :], qb[:, u % 3, :], ALU.mult))
                nc.vector.tensor_reduce(ss[:, b, g, :], kc[:, u % 3, :].rearrange("p (h c) -> p h c", h=H),
                                        AX.X, ALU.add).then_inc(sc, 1)
            dve.wait_ge(bcp, 1)
            ch.link(nc.vector.tensor_copy(nw[:].rearrange("p b g h -> p (b g h)"), ps[:, 0, 0:C]))
            dve.wait_ge(amx, 1)
            ch.link(nc.vector.tensor_tensor(sa[:], sa[:], nw[:], ALU.max))
            ch.link(nc.vector.tensor_reduce(mx[:], sa[:].rearrange("p b g h -> p b h g"), AX.X, ALU.max))
            m4 = mx[:].unsqueeze(2).to_broadcast([P, NB, G, H])
            nc.vector.tensor_tensor(ss[:], ss[:], m4, ALU.subtract).then_inc(sub, 1)
            nc.vector.tensor_tensor(nw[:], nw[:], m4, ALU.subtract).then_inc(sub, 1)
            dve.wait_ge(vtp, 1)
            ch.mark(nc.vector.tensor_copy(vt[:].rearrange("p g j b -> p (g j b)"), ps[:, 1, 0:G * 4 * NB]))
            dve.wait_ge(ex, 2)
            dve.wait_ge(lp, 1)
            ch.link(nc.vector.tensor_tensor(l3[:].rearrange("p b g h -> p (b g h)"), ps[:, 2, 0:C],
                                            nw[:].rearrange("p b g h -> p (b g h)"), ALU.add))
            ch.link(nc.vector.tensor_reduce(ll[:], l3[:].rearrange("p b g h -> p b h g"), AX.X, ALU.add))
            ch.link(nc.vector.reciprocal(ll[:], ll[:]))
            for two in range(2):
                rows = slice(DH * two, DH * two + DH)
                for g in range(G):
                    ch.mark(nc.vector.tensor_copy(pn[rows, g], nw[rows, :, g, two::2].rearrange("p b j -> p j b")))
                ch.mark(nc.vector.tensor_copy(rl[rows], ll[rows, :, two::2].rearrange("p b j -> p j b")))
            ch.wait()
            ch.link(nc.vector.tensor_tensor(vt[:], vt[:], pn[:], ALU.mult))
            ch.link(nc.vector.tensor_tensor(vt[:, 0], vt[:, 0], vt[:, 1], ALU.add))
            ch.link(nc.vector.tensor_tensor(vt[:, 0], vt[:, 0], vt[:, 2], ALU.add))
            dve.wait_ge(pv, NB)
            for two in range(2):
                rows = slice(DH * two, DH * two + DH)
                src = ps[rows, 3, 0:NB * H].rearrange("p (b j two) -> p two j b", two=2, j=4)[:, two]
                ch.mark(nc.vector.tensor_tensor(ot[rows], vt[rows, 0], src, ALU.add))
            ch.wait()
            nc.vector.tensor_tensor(ot[:], ot[:], rl[:], ALU.mult).then_inc(done, 1)

        @block.tensor
        def _(pe):
            pe.wait_ge(dgd, 1)
            nc.tensor.matmul(ps[:, 0, 0:C], core.ones[0:NB, :], dg[:].rearrange("a b c -> a (b c)"),
                             start=True, stop=True).then_inc(bcp, 1)
            for g in range(G):
                for j in range(4):
                    at = (4 * g + j) * NB
                    last = nc.tensor.transpose(ps[:, 1, at:at + NB], zs[:, g, 2, j * P:(j + 1) * P], ident[0:NB, 0:NB])
            last.then_inc(vtp, 1)
            pe.wait_ge(ex, 2)
            nc.tensor.matmul(ps[:, 2, 0:C], core.ones[:], ss[:].rearrange("p b g h -> p (b g h)"),
                             start=True, stop=True).then_inc(lp, 1)
            for b in range(NB):
                pe.wait_ge(v_in[b % 2], 48 * (b // 2 + 1))
                for j in range(4):
                    for g in range(G):
                        at = (b * 4 + j) * 2
                        last = nc.tensor.matmul(ps[:, 3, at:at + 2], vc[:, b % 2, g, j * P:(j + 1) * P],
                                                ss[:, b, g, 2 * j:2 * j + 2], start=(g == 0), stop=(g == G - 1))
                last.then_inc(pv, 1)


def sample_mlstm(core):
    nc, t, o, ps, sem, sb, ident = core.nc, core.t, core.o, core.ps, core.sem, core.sb, core.ident
    with ExitStack() as c:
        z = sb("r_z", [NB, 2048], ctx=c)
        st = sb("r_c", [P, NB, 4, DV], ctx=c)
        nn = sb("r_n", [NB, 512], ctx=c)
        gt = sb("r_g", [NB, 3, H], ctx=c)
        tmp = sb("r_t", [NB, 512], ctx=c)
        kw = sb("r_kw", [NB, 512], ctx=c)
        km = sb("r_km", [NB, NB, 512], ctx=c)
        mt = sb("r_m", [NB, H], ctx=c)
        e3 = sb("r_e", [NB, 3, H], ctx=c)
        qk = sb("r_qk", [NB, H], ctx=c)
        qn = sb("r_qn", [NB, H], ctx=c)
        co = sb("r_co", [NB, 3, H], ctx=c)
        dg = sb("r_dg", [NB, NB, 3, H], ctx=c)
        cb = sb("r_cb", [P, NB, 3, H], ctx=c)
        d2 = sb("r_d2", [P, NB, 4], ctx=c)
        qd = sb("r_qd", [P, NB, 4, 2], ctx=c)
        vt = sb("r_vt", [P, H, NB], ctx=c)
        ht = sb("r_ht", [P, H, NB], ctx=c)
        om = sb("r_om", [P, H, NB], ctx=c)
        z_in, g_in, s_in, tr, qdd, gsub, gexp, dgd, cbp, cbd, kmd, up, std, hq, hd = (sem(f"r_{x}") for x in
            ("zin", "gin", "sin", "tr", "qd", "gsub", "gexp", "dg", "cbp", "cb", "km", "up", "st", "hq", "h"))
        out = core.store_sem("r_out")
        nd, md = sem("r_nd"), sem("r_md")
        block = c.enter_context(nc.Block())
        halves = [slice(0, DH), slice(DH, P)]

        @block.sync
        def _(sp):
            sp.dma_start(z[:], core.zm_s).then_inc(z_in, 16)
            with nc.allow_non_contiguous_dma(reason="64 gates"):
                sp.dma_start(gt[:, 0, :], core.if_s[0].rearrange("h b -> b h")).then_inc(g_in, 16)
                sp.dma_start(gt[:, 1, :], core.if_s[1].rearrange("h b -> b h")).then_inc(g_in, 16)
                sp.dma_start(om[:], core.om_s.rearrange("k p b -> p k b")).then_inc(g_in, 16)
            sp.dma_start(gt[:, 2, :], t["state_mlstm_m"]).then_inc(g_in, 16)
            sp.dma_start(nn[:], t["state_mlstm_n"].rearrange("b h d -> b (h d)")).then_inc(g_in, 16)
            for b in range(NB):
                sp.dma_start(st[:, b], t["state_mlstm_C"][b].rearrange("(j two) d e -> (two d) j e", two=2)).then_inc(s_in, 16)
            core.load_weights(core.taken + 8)
            sp.wait_ge(md, 1)
            sp.dma_start(o[13], mt[:]).then_inc(out, 16)
            sp.wait_ge(nd, 1)
            sp.dma_start(o[12].rearrange("b h d -> b (h d)"), nn[:]).then_inc(out, 16)
            sp.wait_ge(hd, 1)
            sp.dma_start(core.hm_t[:, :, S:T].rearrange("k p b -> p k b"), ht[:]).then_inc(out, 16)
            for b in range(NB):
                sp.wait_ge(std, 4 * b + 4)
                sp.dma_start(o[11][b].rearrange("(j two) d e -> (two d) j e", two=2), st[:, b]).then_inc(out, 16)
            sp.wait_ge(out, 16 * (3 + NB))

        @block.tensor
        def _(pe):
            pe.wait_ge(z_in, 16)
            for j in range(4):
                nc.tensor.transpose(ps[:, 0, j * NB:(j + 1) * NB], z[:, j * P:(j + 1) * P], ident[0:NB, 0:NB])
            for h in range(H):
                last = nc.tensor.transpose(ps[:, 0, (4 + h) * NB:(5 + h) * NB], z[:, 1024 + h * P:1024 + (h + 1) * P],
                                           ident[0:NB, 0:NB])
            last.then_inc(tr, 1)
            pe.wait_ge(qdd, 2)
            pe.wait_ge(s_in, 16 * NB)
            for b in range(NB):
                for j in range(4):
                    at = (b * 4 + j) * 2
                    last = nc.tensor.matmul(ps[:, 1, at:at + 2], st[:, b, j, :], qd[:, b, j, :], start=True, stop=True)
            last.then_inc(hq, 1)
            pe.wait_ge(dgd, 1)
            nc.tensor.matmul(ps[:, 2, 0:NB * 3 * H], core.ones[0:NB, :], dg[:].rearrange("a b x h -> a (b x h)"),
                             start=True, stop=True).then_inc(cbp, 1)
            pe.wait_ge(kmd, 1)
            for b in range(NB):
                if b >= 2:
                    pe.wait_ge(std, 4 * b - 4)
                for h in range(H):
                    rows = halves[h % 2]
                    last = nc.tensor.matmul(ps[rows, 4 + b % 2, (h // 2) * DV:(h // 2 + 1) * DV],
                                            km[:, b, h * DH:(h + 1) * DH], z[:, 1024 + h * DV:1024 + (h + 1) * DV],
                                            start=True, stop=True)
                last.then_inc(up, 1)

        @block.scalar
        def _(act):
            act.wait_ge(gsub, 3)
            nc.scalar.activation(e3[:], e3[:], ACT.Exp).then_inc(gexp, 1)

        @block.vector
        def _(dve):
            ch = core.dve
            h3 = lambda a: a.rearrange("b (h c) -> b h c", h=H)
            ch.mark(nc.vector.memset(qd[:], 0.0))
            dve.wait_ge(g_in, 80)
            ch.link(nc.vector.tensor_tensor(gt[:, 1, :], gt[:, 1, :], gt[:, 2, :], ALU.add))
            nc.vector.tensor_tensor(mt[:], gt[:, 0, :], gt[:, 1, :], ALU.max).then_inc(md, 1)
            dve.wait_ge(md, 1)
            nc.vector.tensor_tensor(e3[:, 0, :], gt[:, 1, :], mt[:], ALU.subtract).then_inc(gsub, 1)
            nc.vector.tensor_tensor(e3[:, 1, :], gt[:, 0, :], mt[:], ALU.subtract).then_inc(gsub, 1)
            nc.vector.tensor_scalar(e3[:, 2, :], mt[:], -1.0, None, ALU.mult).then_inc(gsub, 1)
            dve.wait_ge(z_in, 16)
            ch.link(nc.vector.tensor_tensor(tmp[:], z[:, 0:512], z[:, 512:1024], ALU.mult))
            ch.link(nc.vector.tensor_reduce(qk[:], h3(tmp[:]), AX.X, ALU.add))
            ch.link(nc.vector.tensor_tensor(tmp[:], z[:, 0:512], nn[:], ALU.mult))
            ch.link(nc.vector.tensor_reduce(qn[:], h3(tmp[:]), AX.X, ALU.add))
            dve.wait_ge(tr, 1)
            q4 = ps[:, 0, 0:4 * NB].rearrange("p (j b) -> p b j", j=4)
            nc.vector.tensor_copy(qd[halves[0], :, :, 0], q4[halves[0]]).then_inc(qdd, 1)
            nc.vector.tensor_copy(qd[halves[1], :, :, 1], q4[halves[1]]).then_inc(qdd, 1)
            ch.link(nc.vector.tensor_copy(vt[:].rearrange("p h b -> p (h b)"), ps[:, 0, 4 * NB:12 * NB]))
            dve.wait_ge(gexp, 1)
            ch.link(nc.vector.tensor_tensor(qk[:], qk[:], e3[:, 1, :], ALU.mult))
            ch.link(nc.vector.tensor_tensor(qn[:], qn[:], e3[:, 0, :], ALU.mult))
            ch.link(nc.vector.tensor_tensor(qn[:], qn[:], qk[:], ALU.add))
            ch.link(nc.vector.scalar_tensor_tensor(qn[:], qn[:], -1.0, qn[:], ALU.mult, ALU.max))
            ch.link(nc.vector.tensor_tensor(qn[:], qn[:], e3[:, 2, :], ALU.max))
            ch.link(nc.vector.reciprocal(qn[:], qn[:]))
            ch.mark(nc.vector.tensor_copy(co[:, 0, :], e3[:, 0, :]))
            ch.mark(nc.vector.tensor_tensor(co[:, 1, :], e3[:, 0, :], qn[:], ALU.mult))
            ch.link(nc.vector.tensor_tensor(co[:, 2, :], qk[:], qn[:], ALU.mult))
            nc.vector.tensor_tensor(dg[:].rearrange("a b x h -> a b (x h)"),
                                    co[:].rearrange("a x h -> a (x h)").unsqueeze(1).to_broadcast([NB, NB, 3 * H]),
                                    bc(ident[0:NB, 0:NB], [NB, NB, 3 * H]), ALU.mult).then_inc(dgd, 1)
            ch.link(nc.vector.tensor_tensor(h3(kw[:]), h3(z[:, 512:1024]), bc(e3[:, 1, :], [NB, H, DH]), ALU.mult))
            nc.vector.tensor_tensor(km[:], kw[:].unsqueeze(1).to_broadcast([NB, NB, 512]),
                                    bc(ident[0:NB, 0:NB], [NB, NB, 512]), ALU.mult).then_inc(kmd, 1)
            ch.link(nc.vector.tensor_tensor(h3(nn[:]), h3(nn[:]), bc(e3[:, 0, :], [NB, H, DH]), ALU.mult))
            nc.vector.tensor_tensor(nn[:], nn[:], kw[:], ALU.add).then_inc(nd, 1)
            dve.wait_ge(cbp, 1)
            ch.link(nc.vector.tensor_copy(cb[:].rearrange("p b x h -> p (b x h)"), ps[:, 2, 0:NB * 3 * H]))
            ch.mark(nc.vector.tensor_copy(d2[halves[0]], cb[halves[0], :, 0, 0::2]))
            ch.mark(nc.vector.tensor_copy(d2[halves[1]], cb[halves[1], :, 0, 1::2]))
            dve.wait_ge(hq, 1)
            ch.mark(nc.vector.tensor_tensor(ht[:], cb[:, :, 1, :].rearrange("p b h -> p h b"),
                                            ps[:, 1, 0:NB * H].rearrange("p (b h) -> p h b", b=NB), ALU.mult))
            ch.link(nc.vector.tensor_tensor(vt[:], vt[:], cb[:, :, 2, :].rearrange("p b h -> p h b"), ALU.mult))
            ch.link(nc.vector.tensor_tensor(ht[:], ht[:], vt[:], ALU.add))
            nc.vector.tensor_tensor(ht[:], ht[:], om[:], ALU.mult).then_inc(hd, 1)
            for b in range(NB):
                dve.wait_ge(up, b + 1)
                for j in range(4):
                    nc.vector.scalar_tensor_tensor(st[:, b, j, :], st[:, b, j, :], d2[:, b, j:j + 1],
                                                   ps[:, 4 + b % 2, j * DV:(j + 1) * DV], ALU.mult,
                                                   ALU.add).then_inc(std, 1)


def project_across(core, nk, p0, cols, rhs, bank, release):
    nc, ps = core.nc, core.ps
    hi, lo = rhs
    m = cols.stop - cols.start
    for k in range(nk):
        w_hi, w_lo = core.weight(p0 + k, cols)
        for i, (w, x) in enumerate(((w_hi, hi), (w_hi, lo), (w_lo, hi))):
            for s in range(3):
                last = nc.tensor.matmul(ps[0:m, bank + s, 0:SEG], w, x[:, k, s * SEG:(s + 1) * SEG],
                                        start=(k == 0 and i == 0), stop=(k == nk - 1 and i == 2))
        if release:
            last.then_inc(core.w_used, 1)
    return last


class Groups:

    def __init__(self, core, name, groups, nk):
        self.core, self.nk, self.per, self.n = core, nk, CW // P, groups * (CW // P)
        self.p0 = core.taken
        core.taken += groups * nk
        self.mm = core.sem(name)

    def product(self, pe, u, rhs):
        g, m = divmod(u, self.per)
        if m == 0:
            pe.wait_ge(self.core.w_lo, self.p0 + (g + 1) * self.nk)
        end = m == self.per - 1
        last = project_across(self.core, self.nk, self.p0 + g * self.nk, slice(m * P, (m + 1) * P), rhs,
                              3 * (u % 2), end)
        if not end:
            last.then_inc(self.mm, 1)

    def wait(self, eng, u):
        if u % self.per == self.per - 1:
            eng.wait_ge(self.core.w_used, self.p0 + (u // self.per + 1) * self.nk)
        else:
            eng.wait_ge(self.mm, u + 1 - (u + 1) // self.per)


def banks(core, u):
    return core.ps[:, 3 * (u % 2):3 * (u % 2) + 3, 0:SEG]


def gate_projections(core):
    nc, sem, sb, ps = core.nc, core.sem, core.sb, core.ps
    U = 3 * KD
    PER = 6
    p0 = core.taken
    core.taken += 6 * KD
    with ExitStack() as c:
        chunks = Chunks(core, c)
        sg = sb("e_sg", [P, 2, T], ctx=c)
        hm = sb("e_hm", [P, 2, S], ctx=c)
        mm, ev, mul = sem("e_mm"), sem("e_ev"), sem("e_mul")
        h_in = [sem(f"e_hin{i}") for i in range(2)]
        out = [sem(f"e_out{i}") for i in range(2)]
        om_out = sem("e_omout")
        block = c.enter_context(nc.Block())

        def step(i):
            n, r = divmod(i, PER)
            if n >= NT or r == 1:
                return None
            return n * chunks.STEPS + max(r - 1, 0)

        @block.sync
        def _(sp):
            core.load_weights(core.taken + 8)

        @block.gpsimd
        def _(pool):
            core.split_weights(core.taken + 8)

        @block.tensor
        def _(pe):
            for i in range(3 * U):
                u, s = divmod(i, 3)
                g, m = divmod(u, 4)
                if m == 0 and s == 0:
                    pe.wait_ge(core.w_lo, p0 + (g + 1) * KD)
                if i >= 2:
                    pe.wait_ge(ev, i - 1)
                seg = slice(s * SEG, (s + 1) * SEG)
                frees = m == 3 and s == 2
                for k in range(KD):
                    last = products(nc, ps[:, i % 2, 0:SEG], core.weight(p0 + g * KD + k, slice(m * P, (m + 1) * P)),
                                    (core.hhi[:, k, seg], core.hlo[:, k, seg]), k == 0, k == KD - 1)
                    if frees:
                        last.then_inc(core.w_used, 1)
                if not frees:
                    last.then_inc(mm, 1)
                if step(i) is not None:
                    chunks.pe(step(i))

        @block.scalar
        def _(act):
            chunks.act_init()
            for i in range(3 * U):
                u, s = divmod(i, 3)
                if s == 0 and u >= 2:
                    act.wait_ge(out[u % 2], 16 * (u // 2))
                if i % 12 == 11:
                    act.wait_ge(core.w_used, p0 + (i // 12 + 1) * KD)
                else:
                    act.wait_ge(mm, i + 1 - (i + 1) // 12)
                act.activation(sg[:, u % 2, s * SEG:(s + 1) * SEG], ps[:, i % 2, 0:SEG], ACT.Sigmoid).then_inc(ev, 1)
                if s == 2 and u < 2 * KD:
                    act.wait_ge(ev, i + 1)
                    act.dma_start(core.gates[u], sg[:, u % 2, :]).then_inc(out[u % 2], 16)
                elif s == 2:
                    h = u - 2 * KD
                    act.wait_ge(mul, h + 1)
                    act.dma_start(core.om_s[h], sg[:, u % 2, S:T]).then_inc(om_out, 16)
                    act.dma_start(core.hm_t[h, :, 0:S], hm[:, h % 2, :]).then_inc(out[u % 2], 16)
                    act.wait_ge(om_out, 16 * (h + 1))
                if s == 2 and u >= 2 * KD and u - 2 * KD + 2 < KD:
                    h = u - 2 * KD
                    act.wait_ge(out[u % 2], 16 * (u // 2 + 1))
                    act.dma_start(hm[:, h % 2, :], core.h_mem[h + 2, :, 0:S]).then_inc(h_in[h % 2], 16)
                if step(i) is not None:
                    chunks.act(step(i))
                if i == 6 * KD - 1:
                    chunks.store_state()
                    for h in range(2):
                        act.dma_start(hm[:, h, :], core.h_mem[h, :, 0:S]).then_inc(h_in[h], 16)
            for i in range(2):
                act.wait_ge(out[i], 16 * U // 2)

        @block.vector
        def _(dve):
            chunks.dve_init()
            for i in range(3 * U):
                if step(i) is not None:
                    chunks.dve(step(i))
                u, s = divmod(i, 3)
                if s == 2 and u >= 2 * KD:
                    h = u - 2 * KD
                    dve.wait_ge(ev, i + 1)
                    dve.wait_ge(h_in[h % 2], 16 * (h // 2 + 1))
                    nc.vector.tensor_tensor(hm[:, h % 2, :], hm[:, h % 2, :], sg[:, u % 2, 0:S],
                                            ALU.mult).then_inc(mul, 1)


def merge_product(core, tag, src, nk, gate0):
    nc, sem, sb, acc = core.nc, core.sem, core.sb, core.acc
    with ExitStack() as c:
        hi = sb(f"{tag}_hi", [P, nk, T], F32R, c)
        lo = sb(f"{tag}_lo", [P, nk, T], F32R, c)
        rw = sb(f"{tag}_rw", [P, 2, T], ctx=c)
        units = Groups(core, f"{tag}_mm", 2, nk)
        his, los, ev, add = sem(f"{tag}_his"), sem(f"{tag}_los"), sem(f"{tag}_ev"), sem(f"{tag}_add")
        r_in = [sem(f"{tag}_in{i}") for i in range(2)]
        block = c.enter_context(nc.Block())

        @block.sync
        def _(sp):
            for k in range(nk):
                if k >= 2:
                    sp.wait_ge(los, k - 1)
                sp.dma_start(rw[:, k % 2, :], src[k]).then_inc(r_in[k % 2], 16)
            core.load_weights(core.taken + 8)

        @block.gpsimd
        def _(pool):
            core.split_weights(core.taken + 8)

        @block.scalar
        def _(act):
            for k in range(nk):
                act.wait_ge(r_in[k % 2], 16 * (k // 2 + 1))
                nc.scalar.activation(hi[:, k, :], rw[:, k % 2, :], ACT.Copy).then_inc(his, 1)
            for u in range(KD):
                if u < 2:
                    act.wait_ge(los, nk - 1 + u)
                else:
                    act.wait_ge(ev, u - 1)
                act.dma_start(rw[:, u % 2, :], core.gates[gate0 + u]).then_inc(r_in[u % 2], 16)

        @block.vector
        def _(dve):
            for k in range(nk):
                dve.wait_ge(his, k + 1)
                nc.vector.tensor_tensor(lo[:, k, :], rw[:, k % 2, :], hi[:, k, :].bitcast(F32),
                                        ALU.subtract).then_inc(los, 1)
            for u in range(KD):
                units.wait(dve, u)
                dve.wait_ge(r_in[u % 2], 16 * (nk // 2 + u // 2 + 1))
                if gate0 == 0:
                    nc.vector.tensor_tensor(seg3(acc[:, u, :]), banks(core, u), seg3(rw[:, u % 2, :]),
                                            ALU.mult).then_inc(ev, 1)
                else:
                    nc.vector.tensor_tensor(seg3(rw[:, u % 2, :]), banks(core, u), seg3(rw[:, u % 2, :]),
                                            ALU.mult).then_inc(add, 1)
                    dve.wait_ge(add, u + 1)
                    nc.vector.tensor_tensor(acc[:, u, :], acc[:, u, :], rw[:, u % 2, :], ALU.add).then_inc(ev, 1)

        @block.tensor
        def _(pe):
            pe.wait_ge(los, nk)
            for u in range(KD):
                if u >= 2:
                    pe.wait_ge(ev, u - 1)
                units.product(pe, u, (hi, lo))


def output_projection(core):
    nc, t, sem, sb, acc, ident, ps = core.nc, core.t, core.sem, core.sb, core.acc, core.ident, core.ps
    with ExitStack() as c:
        hi = sb("o_hi", [P, KD, T], F32R, c)
        lo = sb("o_lo", [P, KD, T], F32R, c)
        xr = sb("o_x", [P, 2, D], ctx=c)
        units = Groups(core, "o_mm", 2, KD)
        his, los, tr, xt, ev = (sem(f"o_{x}") for x in ("his", "los", "tr", "xt", "ev"))
        x_in = [sem(f"o_xin{i}") for i in range(2)]
        block = c.enter_context(nc.Block())

        @block.sync
        def _(sp):
            for n in range(NT + 1):
                if n >= 2:
                    sp.wait_ge(tr, 2 * n - 2)
                if n < NT:
                    sp.dma_start(xr[:, n % 2, :], t["x_prompt"][0, n * P:(n + 1) * P, :]).then_inc(x_in[n % 2], 16)
                else:
                    sp.dma_start(xr[0:NB, n % 2, :], t["x_sample"].rearrange("b s d -> (b s) d")).then_inc(x_in[n % 2], 16)
            core.load_weights(core.taken + 8)

        @block.gpsimd
        def _(pool):
            core.split_weights(core.taken + 8)

        @block.scalar
        def _(act):
            for k in range(KD):
                nc.scalar.activation(hi[:, k, :], acc[:, k, :], ACT.Copy).then_inc(his, 1)
            act.wait_ge(los, KD)
            for v in range(2 * (NT + 1)):
                n, kk = divmod(v, 2)
                cols = P if n < NT else NB
                act.wait_ge(tr, v + 1)
                nc.scalar.activation(acc[:, 4 * kk:4 * kk + 4, n * P:n * P + cols],
                                     ps[:, 6 + v % 2, :].rearrange("p (k c) -> p k c", k=4)[:, :, 0:cols],
                                     ACT.Copy).then_inc(xt, 1)

        @block.vector
        def _(dve):
            for k in range(KD):
                dve.wait_ge(his, k + 1)
                nc.vector.tensor_tensor(lo[:, k, :], acc[:, k, :], hi[:, k, :].bitcast(F32), ALU.subtract).then_inc(los, 1)
            dve.wait_ge(xt, 2 * (NT + 1))
            for u in range(KD):
                units.wait(dve, u)
                nc.vector.tensor_tensor(seg3(acc[:, u, :]), seg3(acc[:, u, :]), banks(core, u), ALU.add).then_inc(ev, 1)

        @block.tensor
        def _(pe):
            for v in range(2 * (NT + 1)):
                n, kk = divmod(v, 2)
                rows = P if n < NT else NB
                pe.wait_ge(x_in[n % 2], 16 * (n // 2 + 1))
                if v >= 2:
                    pe.wait_ge(xt, v - 1)
                for k in range(4):
                    last = nc.tensor.transpose(ps[:, 6 + v % 2, k * P:k * P + rows],
                                               xr[0:rows, n % 2, (4 * kk + k) * P:(4 * kk + k + 1) * P],
                                               ident[0:rows, 0:rows])
                last.then_inc(tr, 1)
            for u in range(KD):
                if u >= 2:
                    pe.wait_ge(ev, u - 1)
                units.product(pe, u, (hi, lo))


def norm_ffn_input(core):
    nc, t, sem, sb, acc, ps = core.nc, core.t, core.sem, core.sb, core.acc, core.ps
    hi, lo = core.h2hi, core.h2lo
    with ExitStack() as c:
        g2 = sb("n_g", [P, KD], ctx=c)
        sq = sb("n_sq", [P, 2, T], ctx=c)
        rs = sb("n_rs", [P, T], ctx=c)
        g_in, sqd, mm, var, std, scl, his, los = (sem(f"n_{x}") for x in
                                                  ("gin", "sq", "mm", "var", "std", "scl", "hi", "lo"))
        block = c.enter_context(nc.Block())

        @block.sync
        def _(sp):
            with nc.allow_non_contiguous_dma(reason="1024 gains"):
                sp.dma_start(g2[:], t["norm2_g"].rearrange("(k p) -> p k", p=P)).then_inc(g_in, 16)
            core.load_weights(core.taken + 8)
            sp.wait_ge(g_in, 16)

        @block.tensor
        def _(pe):
            for k in range(KD):
                pe.wait_ge(sqd, k + 1)
                for s in range(3):
                    last = nc.tensor.matmul(ps[:, s, 0:SEG], core.ones[:], sq[:, k % 2, s * SEG:(s + 1) * SEG],
                                            start=(k == 0), stop=(k == KD - 1))
                last.then_inc(mm, 1)

        @block.scalar
        def _(act):
            for k in range(KD):
                if k >= 2:
                    act.wait_ge(mm, k - 1)
                nc.scalar.activation(sq[:, k % 2, :], acc[:, k, :], ACT.Square).then_inc(sqd, 1)
            act.wait_ge(var, 1)
            nc.scalar.activation(rs[:], rs[:], ACT.Sqrt).then_inc(std, 1)
            for k in range(KD):
                act.wait_ge(scl, k + 1)
                nc.scalar.activation(hi[:, k, :], sq[:, k % 2, :], ACT.Copy).then_inc(his, 1)

        @block.vector
        def _(dve):
            ch = core.dve
            dve.wait_ge(mm, KD)
            nc.vector.tensor_scalar(seg3(rs[:]), ps[:, 0:3, 0:SEG], 1.0 / D, EPS, ALU.mult, ALU.add).then_inc(var, 1)
            dve.wait_ge(std, 1)
            ch.link(nc.vector.reciprocal(rs[:], rs[:]))
            dve.wait_ge(g_in, 16)
            for k in range(KD):
                if k >= 2:
                    dve.wait_ge(los, k - 1)
                nc.vector.scalar_tensor_tensor(sq[:, k % 2, :], acc[:, k, :], g2[:, k:k + 1], rs[:], ALU.mult,
                                               ALU.mult).then_inc(scl, 1)
                dve.wait_ge(his, k + 1)
                nc.vector.tensor_tensor(lo[:, k, :], sq[:, k % 2, :], hi[:, k, :].bitcast(F32),
                                        ALU.subtract).then_inc(los, 1)


def ffn(core):
    nc, sem, sb, acc = core.nc, core.sem, core.sb, core.acc
    J = DFF // 256
    p0 = core.taken
    core.taken += J * (KD + 4)
    with ExitStack() as c:
        sg = sb("ff_sg", [P, T], ctx=c)
        fh = sb("ff_hi", [P, 2, 2, T], F32R, c)
        fl = sb("ff_lo", [P, 2, 2, T], F32R, c)
        mm, sil, mul, his, los, add = (sem(f"ff_{x}") for x in ("mm", "sil", "mul", "hi", "lo", "add"))
        block = c.enter_context(nc.Block())

        def first(j):
            return p0 + j * (KD + 4) - (4 if j else 0)

        def first_down(j):
            return first(j + 1) + KD if j < J - 1 else p0 + J * (KD + 4) - 4

        order = []
        for j in range(J + 1):
            if j < J:
                order += [("gu", j, m) for m in range(4)]
            if j >= 1:
                order += [("dn", j - 1, m) for m in range(KD)]
        index = {x: i for i, x in enumerate(order)}
        ends = {}
        n = 0
        for i, (kind, j, m) in enumerate(order):
            frees = (kind == "gu" and m == 3) or (kind == "dn" and m in (3, 7))
            if not frees:
                n += 1
            ends[i] = (frees, n)

        def complete(eng, x):
            kind, j, m = x
            frees, count = ends[index[x]]
            if not frees:
                eng.wait_ge(mm, count)
            elif kind == "gu":
                eng.wait_ge(core.w_used, first(j) + KD)
            else:
                eng.wait_ge(core.w_used, first_down(j) + (2 if m == 3 else 4))

        def taken(eng, i):
            kind, j, m = order[i]
            if kind == "dn":
                eng.wait_ge(add, KD * j + m + 1)
            elif m % 2 == 0:
                eng.wait_ge(sil, 2 * j + m // 2 + 1)
            else:
                eng.wait_ge(mul, 2 * j + m // 2 + 1)

        def res(i):
            return core.ps[:, 3 * (i % 2):3 * (i % 2) + 3, 0:SEG]

        @block.sync
        def _(sp):
            core.load_weights(core.taken + 8)

        @block.gpsimd
        def _(pool):
            core.split_weights(core.taken + 8)

        @block.tensor
        def _(pe):
            for i, (kind, j, m) in enumerate(order):
                if i >= 2:
                    taken(pe, i - 2)
                frees = ends[i][0]
                if kind == "gu":
                    if m == 0:
                        pe.wait_ge(core.w_lo, first(j) + KD)
                    tile, up = divmod(m, 2)
                    at = 256 * up + P * tile
                    last = project_across(core, KD, first(j), slice(at, at + P), (core.h2hi, core.h2lo), 3 * (i % 2), frees)
                else:
                    p = first_down(j) + (0 if m < 4 else 2)
                    if m % 4 == 0:
                        pe.wait_ge(core.w_lo, p + 2)
                    if m == 0:
                        pe.wait_ge(los, 2 * j + 2)
                    last = project_across(core, 2, p, slice(P * (m % 4), P * (m % 4) + P),
                                          (fh[:, j % 2], fl[:, j % 2]), 3 * (i % 2), frees)
                if not frees:
                    last.then_inc(mm, 1)

        @block.scalar
        def _(act):
            for j in range(J):
                for tile in range(2):
                    v = 2 * j + tile
                    x = ("gu", j, 2 * tile)
                    complete(act, x)
                    if v >= 1:
                        act.wait_ge(los, v)
                    nc.scalar.activation(seg3(sg[:]), res(index[x]), ACT.Silu).then_inc(sil, 1)
                    act.wait_ge(mul, v + 1)
                    if j >= 2:
                        complete(act, ("dn", j - 2, 7))
                    nc.scalar.activation(fh[:, j % 2, tile, :], sg[:], ACT.Copy).then_inc(his, 1)

        @block.vector
        def _(dve):
            def split(v):
                j, tile = divmod(v, 2)
                x = ("gu", j, 2 * tile + 1)
                complete(dve, x)
                dve.wait_ge(sil, v + 1)
                nc.vector.tensor_tensor(seg3(sg[:]), seg3(sg[:]), res(index[x]), ALU.mult).then_inc(mul, 1)
                dve.wait_ge(his, v + 1)
                nc.vector.tensor_tensor(fl[:, j % 2, tile, :], sg[:], fh[:, j % 2, tile, :].bitcast(F32),
                                        ALU.subtract).then_inc(los, 1)

            for j in range(J + 1):
                if j < J:
                    split(2 * j)
                    split(2 * j + 1)
                if j >= 1:
                    for m in range(KD):
                        x = ("dn", j - 1, m)
                        complete(dve, x)
                        if j >= 2:
                            dve.wait_ge(add, KD * (j - 2) + m + 1)
                        nc.vector.tensor_tensor(seg3(acc[:, m, :]), seg3(acc[:, m, :]), res(index[x]),
                                                ALU.add).then_inc(add, 1)


def store_output(core):
    nc, o, sem, sb, acc, ps = core.nc, core.o, core.sem, core.sb, core.acc, core.ps
    with ExitStack() as c:
        yt = sb("y_t", [P, 2, D], ctx=c)
        tr, ea, ev = sem("y_tr"), sem("y_ea"), sem("y_ev")
        out = [core.store_sem(f"y_out{i}") for i in range(2)]
        block = c.enter_context(nc.Block())

        @block.tensor
        def _(pe):
            for n in range(NT + 1):
                cols = P if n < NT else NB
                if n >= 2:
                    pe.wait_ge(ea, n - 1)
                    pe.wait_ge(ev, n - 1)
                for k in range(KD):
                    last = nc.tensor.transpose(ps[0:cols, 2 * (n % 2) + k // 4, (k % 4) * P:(k % 4 + 1) * P],
                                               acc[:, k, n * P:n * P + cols], core.ident[:])
                last.then_inc(tr, 1)

        def half(n, k):
            rows = P if n < NT else NB
            return yt[0:rows, n % 2, k * 512:(k + 1) * 512], ps[0:rows, 2 * (n % 2) + k, :]

        @block.scalar
        def _(act):
            for n in range(NT + 1):
                act.wait_ge(tr, n + 1)
                if n >= 2:
                    act.wait_ge(out[n % 2], 16 * (n // 2))
                nc.scalar.activation(*half(n, 0), ACT.Copy).then_inc(ea, 1)

        @block.vector
        def _(dve):
            for n in range(NT + 1):
                dve.wait_ge(tr, n + 1)
                if n >= 2:
                    dve.wait_ge(out[n % 2], 16 * (n // 2))
                nc.vector.tensor_copy(*half(n, 1)).then_inc(ev, 1)

        @block.sync
        def _(sp):
            for n in range(NT + 1):
                sp.wait_ge(ea, n + 1)
                sp.wait_ge(ev, n + 1)
                dst = o[0][0, n * P:(n + 1) * P, :] if n < NT else o[1].rearrange("b s d -> (b s) d")
                rows = P if n < NT else NB
                sp.dma_start(dst, yt[0:rows, n % 2, :]).then_inc(out[n % 2], 16)
            for i in range(2):
                sp.wait_ge(out[i], 16 * (NT // 2 + (i == 0)))
            sp.wait_ge(core.cache_out, 16 * len(core.copies))


def program(nc, t, o):
    with ExitStack() as top:
        core = Core(nc, t, o, top)
        with ExitStack() as ch:
            core.hhi = core.sb("hhi", [P, KD, T], F32R, ch)
            core.hlo = core.sb("hlo", [P, KD, T], F32R, ch)
            core.phase = []
            norm_input(core)
            core.bands = core.sb("bands", [P, S], ctx=ch)
            core.neg_m = core.sb("neg_m", [8, S], ctx=ch)
            project(core, 0, None, True)
            core.clear_phase()
            project(core, 1, 0, False)
            core.clear_phase()
            project(core, 2, 1, False)
            core.clear_phase()
            project(core, None, 2, False)
            core.clear_phase()
            gate_projections(core)
            core.clear_phase()
        merge_groups(core)
        core.clear_phase()
        sample_attention(core)
        core.clear_phase()
        sample_mlstm(core)
        core.clear_phase()
        with ExitStack() as ca:
            core.acc = core.sb("acc", [P, KD, T], ctx=ca)
            merge_product(core, "f", core.att_t, 4, 0)
            merge_product(core, "m", core.hm_t, KD, KD)
            core.clear_phase()
            output_projection(core)
            core.clear_phase()
            core.h2hi = core.sb("h2hi", [P, KD, T], F32R, ca)
            core.h2lo = core.sb("h2lo", [P, KD, T], F32R, ca)
            norm_ffn_input(core)
            ffn(core)
            core.clear_phase()
            store_output(core)


def rope_tables():
    import numpy as np
    half = DH // 8
    pos = np.concatenate([np.arange(S), [PAST]]).astype(np.float32)
    freq = np.exp(np.float32(-math.log(500000.0)) * np.arange(0, 2 * half, 2, dtype=np.float32) / np.float32(2 * half))
    ang = pos[:, None] * freq[None, :].astype(np.float32)
    c, s = np.cos(ang), np.sin(ang)
    return np.concatenate([c, c, -s, s], axis=1).astype(np.float32)


def alternate_mask():
    import numpy as np
    q, k = np.arange(P)[:, None], np.arange(P)[None, :]
    return np.where((q >= k) & ((q - k) % 2 == 0), 0.0, NEG).astype(np.float32)


_INS = ["x_prompt", "x_sample", "cache_kv_w128", "cache_kv_w512", "cache_kv_w2048", "state_mlstm_C", "state_mlstm_n",
        "state_mlstm_m", "norm1_g", "w_in", "b_if", "q_norm_g", "k_norm_g", "w_att_out", "w_m_out", "w_o", "norm2_g",
        "w_gate", "w_up", "w_down"]
_OUTS = [(1, S, D), (NB, 1, D)] + [(1, min(w, S), 2, H, DH) for w in WINDOWS] + \
    [(1, H, DH, DV), (1, H, DH), (1, H)] + [(NB, w, 2, H, DH) for w in WINDOWS] + \
    [(NB, H, DH, DV), (NB, H, DH), (NB, H)]


def kernel(**inputs):
    import numpy as _np
    import concourse.bacc as _bacc
    from concourse.bass_utils import run_bass_kernel_spmd as _run

    nc = _bacc.Bacc("TRN2", target_bir_lowering=False, num_devices=1)
    arrays = {f"in_{n}": _np.ascontiguousarray(inputs[n]) for n in _INS}
    arrays["in_rope_table"], arrays["in_mask_halves"] = rope_tables(), alternate_mask()
    t = {n[3:]: nc.dram_tensor(n, a.shape, mybir.dt.from_np(a.dtype), kind="ExternalInput").ap()
         for n, a in arrays.items()}
    o = [nc.dram_tensor(f"out_{i}", s, F32, kind="ExternalOutput").ap() for i, s in enumerate(_OUTS)]
    program(nc, t, o)
    r = _run(nc, [arrays], core_ids=[0])
    return tuple(r.results[0][f"out_{i}"] for i in range(len(_OUTS)))
```

```python
import math
from contextlib import ExitStack

import concourse.bass as bass
from concourse import mybir

F32 = mybir.dt.float32
F32R = mybir.dt.float32r
ALU = mybir.AluOpType
ACT = mybir.ActivationFunctionType
AX = mybir.AxisListType

P = 128
D = 1024
S = 1024
NB = 8
T = S + NB
SEG = T // 3
KD = D // P
NT = S // P
H = 8
DH = 64
DV = 128
G = 3
WINDOWS = (128, 512, 2048)
DILS = (1, 4, 16)
AW = G * H * DH
DFF = 2816
EPS = 1e-6
NEG = -1e30
SCALE = DH ** -0.5
CQM, CKM, CVM, COM = 3 * AW, 3 * AW + 512, 3 * AW + 1024, 3 * AW + 2048
CIF = COM + 1024
CGA, CGB = CIF + 16, CIF + 16 + 1024
CW = 512
RAW = 3
RING = 15
PAST = 2048


def bc(ap, shape):
    return ap.unsqueeze(len(shape) - 1).to_broadcast(shape)


STEPS = tuple(min(d, S // P) for d in DILS)


def residues(ap, g, n):
    length = S // STEPS[g]
    r, i = n * P // length, n * P % length
    if len(ap.shape) == 2:
        return ap.rearrange("p (i d) -> p d i", d=STEPS[g])[:, r, i:i + P]
    return ap.rearrange("p k (i d) -> p k d i", d=STEPS[g])[:, :, r, i:i + P]


def token_rows(ap, g, n):
    length = S // STEPS[g]
    return ap.rearrange("(i d) c -> d i c", d=STEPS[g])[n * P // length, n * P % length:n * P % length + P, :]


def by_tile(tiles, nat, g):
    if g == 0:
        return [(tiles, nat.rearrange("(n p) h -> p n h", p=P))]
    d, per = STEPS[g], NT // STEPS[g]
    return [(tiles.rearrange("p (d j) h -> p d j h", j=per)[:, :, j, :],
             nat.rearrange("(j p d) h -> p j d h", p=P, d=d)[:, j]) for j in range(per)]


def has_prev(g, n):
    return n * P % (S // STEPS[g]) != 0


class Chain:

    def __init__(self, eng, sem):
        self.eng, self.sem, self.n = eng, sem, 0

    def mark(self, ins):
        self.n += 1
        ins.then_inc(self.sem, 1)
        return self.n

    def wait(self, n=None):
        self.eng.wait_ge(self.sem, self.n if n is None else n)

    def link(self, ins):
        self.mark(ins)
        self.wait()


def weight_pieces(t):
    w_in = t["w_in"]
    cols = [x * AW + g * 512 for g in range(G) for x in range(3)] + [CQM, CKM, CVM, CVM + 512]
    cols += [CGA, CGA + 512, CGB, CGB + 512, COM, COM + 512]
    out = [[(w_in[k * P:(k + 1) * P, c:c + CW], 0)] for c in cols for k in range(KD)]
    for name, nk in (("w_att_out", 4), ("w_m_out", KD), ("w_o", KD)):
        out += [[(t[name][k * P:(k + 1) * P, c:c + CW], 0)] for c in (0, CW) for k in range(nk)]
    down = []
    for j in range(DFF // 256):
        out += [[(t["w_gate"][k * P:(k + 1) * P, j * 256:(j + 1) * 256], 0),
                 (t["w_up"][k * P:(k + 1) * P, j * 256:(j + 1) * 256], 256)] for k in range(KD)]
        out += down
        down = [[(t["w_down"][(2 * j + k) * P:(2 * j + k + 1) * P, c:c + CW], 0)] for c in (0, CW) for k in range(2)]
    out += down
    return out


def cache_copies(t, o):
    out = []
    for g, w in enumerate(WINDOWS):
        cache = t[f"cache_kv_w{w}"].rearrange("b w a h c -> b (w a h c)")
        new = o[8 + g].rearrange("b w a h c -> b (w a h c)")
        row = 2 * H * DH
        for b in range(NB):
            for r in range(0, w - 1, P):
                n = min(P, w - 1 - r) * row
                src = cache[b, (r + 1) * row:(r + 1) * row + n].rearrange("(a c) -> a c", a=16)
                out.append((new[b, r * row:r * row + n].rearrange("(a c) -> a c", a=16), src))
    return out


class Core:

    def __init__(self, nc, t, o, top):
        self.nc, self.t, self.o, self.top = nc, t, o, top
        self.phase = None
        self.stale, self.cleared = [], []
        self.pending, self.open = [], []
        sb, sem, dram = self.sb, self.sem, self.dram
        self.ps = top.enter_context(nc.psum_tensor("ps", [P, 8, 512], F32))

        self.pieces = weight_pieces(t)
        self.raw = sb("raw", [P, RAW, CW])
        self.whi = sb("whi", [P, RING, CW], F32R)
        self.wlo = sb("wlo", [P, RING, CW], F32R)
        self.raw_in = [sem(f"raw_in{i}") for i in range(RAW)]
        self.w_hi, self.w_lo, self.w_used = sem("w_hi"), sem("w_lo"), sem("w_used")
        self.landed, at = [], [0] * RAW
        for p, parts in enumerate(self.pieces):
            at[p % RAW] += 16 * len(parts)
            self.landed.append(at[p % RAW])
        self.loaded = self.split = self.taken = 0
        self.copies = cache_copies(t, o)
        self.copied = 0
        self.cache_out = sem("cache_out")

        names = [f"b_zout{g}_{i}" for g in (*range(G), "m") for i in range(4)]
        names += ["g_mout", "c_out", "s_rows", "r_out", *(f"y_out{i}" for i in range(4)), "o_gin"]
        self.stores = {name: sem(name) for name in names}

        self.ident = sb("ident", [P, P])
        self.ones = sb("ones", [P, P])

        self.z_s = dram("z_s", (G, 3, NB, 512))
        self.m_tok = dram("m_tok", (NT, P, 3, 512))
        self.m_tr = dram("m_tr", (2, NT, P, 512))
        self.zm_s = dram("zm_s", (NB, 2048))
        self.neg_all = dram("neg_all", (NT, H, P))
        self.if_s = dram("if_s", (2, H, NB))
        self.om_s = dram("om_s", (KD, P, NB))
        self.a_tr = dram("a_tr", (G, 2, NT, P, 512))
        self.a_v = dram("a_v", (G, NT, P, 512))
        self.o_grp = dram("o_grp", (G, NT, P, 512))
        self.ml_nat = dram("ml_nat", (G, 2, S, H))
        self.cf_nat = dram("cf_nat", (G, S, 8))
        self.h_mem = dram("h_mem", (KD, P, T))
        self.gates = dram("gates", (2 * KD, P, T))
        self.att_t = dram("att_t", (4, P, T))
        self.hm_t = dram("hm_t", (KD, P, T))

        self.dve = Chain(nc.vector, sem("dve_c"))
        self.act = Chain(nc.scalar, sem("act_c"))
        self.pool = Chain(nc.gpsimd, sem("pool_c"))

    def front(self, ctx):
        sb = self.sb
        self.hhi = sb("hhi", [P, KD, T], F32R, ctx)
        self.hlo = sb("hlo", [P, KD, T], F32R, ctx)
        self.mask_pair = sb("mask_pair", [P, 2 * P], ctx=ctx)
        self.mask_halves = sb("mask_halves", [P, P], ctx=ctx)
        self.mask_later = sb("mask_later", [P, P], ctx=ctx)
        self.hs = sb("hs", [P, KD, 40], F32R, ctx)
        self.gq = sb("gq", [P, DH], ctx=ctx)
        self.gk = sb("gk", [P, DH], ctx=ctx)
        self.rope = sb("rope", [P, G, NT + 1, 32], ctx=ctx)
        self.mstat = sb("mstat", [P, G, 2, NT, H], ctx=ctx)

    def sem(self, name):
        handle = self.nc.alloc_semaphore(name=name)
        if self.phase is not None:
            self.phase.append(handle)
        return handle

    def store_sem(self, name):
        return self.stores[name]

    def end_phase(self):
        for handle in self.cleared:
            self.nc.release_semaphore(handle)
        held = [sem for sem, _ in self.pending]
        self.cleared, phase = [], self.phase or []
        self.stale = [x for x in phase if x not in held]
        self.phase = [x for x in phase if x in held]
        self.open, self.pending = self.pending, []

    def defer(self, sem, value):
        self.pending.append((sem, value))

    def settle(self, eng):
        for sem, value in self.open:
            eng.wait_ge(sem, value)

    def clear_stale(self):
        for handle in self.stale:
            self.nc.gpsimd.sem_clear(handle)
        self.cleared, self.stale = self.stale, []

    def sb(self, name, shape, dt=F32, ctx=None):
        return (ctx or self.top).enter_context(self.nc.sbuf_tensor(name, shape, dt))

    def dram(self, name, shape):
        return self.nc.dram_tensor(name, shape, F32, kind="Internal").ap()

    def load_weights(self, until):
        sp = self.nc.sync
        for p in range(self.loaded, min(until + RAW, len(self.pieces))):
            if p >= RAW:
                sp.wait_ge(self.w_lo, p - RAW + 1)
            for src, c in self.pieces[p]:
                sp.dma_start(self.raw[:, p % RAW, c:c + src.shape[1]], src).then_inc(self.raw_in[p % RAW], 16)
            self.loaded = p + 1
            while self.copied < len(self.copies) * (p + 1) // len(self.pieces):
                dst, src = self.copies[self.copied]
                sp.dma_start(dst, src).then_inc(self.cache_out, 16)
                self.copied += 1

    def split_weights(self, until):
        pool = self.nc.gpsimd
        self.clear_stale()
        for p in range(self.split, min(until, len(self.pieces))):
            pool.wait_ge(self.raw_in[p % RAW], self.landed[p])
            if p >= RING:
                pool.wait_ge(self.w_used, p - RING + 1)
            pool.tensor_copy(self.whi[:, p % RING, :], self.raw[:, p % RAW, :]).then_inc(self.w_hi, 1)
            pool.wait_ge(self.w_hi, p + 1)
            pool.tensor_tensor(self.wlo[:, p % RING, :], self.raw[:, p % RAW, :],
                               self.whi[:, p % RING, :].bitcast(F32), ALU.subtract).then_inc(self.w_lo, 1)
            self.split = p + 1

    def weight(self, p, cols):
        return self.whi[:, p % RING, cols], self.wlo[:, p % RING, cols]


def products(nc, out, lhs, rhs, start, stop):
    nc.tensor.matmul(out, lhs[0], rhs[0], start=start, stop=False)
    nc.tensor.matmul(out, lhs[0], rhs[1], start=False, stop=False)
    return nc.tensor.matmul(out, lhs[1], rhs[0], start=False, stop=stop)


def norm_input(core):
    nc, t, ps, sem, sb = core.nc, core.t, core.ps, core.sem, core.sb
    ident, hhi, hlo = core.ident, core.hhi, core.hlo
    with ExitStack() as c:
        x_sb = sb("x_sb", [P, NT + 1, D], ctx=c)
        g1 = sb("g1", [P, D], ctx=c)
        sq_a = sb("sq_a", [P, 2, D], ctx=c)
        ssq = sb("ssq", [P, NT + 1], ctx=c)
        a_in = [sem(f"a_in{n}") for n in range(NT + 1)]
        batches = [range(0, 2), range(2, 4), range(4, 6), range(6, NT + 1)]
        a_g, a_const, a_ssq, a_var, a_std, a_xn = (sem(x) for x in ("a_g", "a_const", "a_ssq", "a_var", "a_std", "a_xn"))
        a_tr, a_hi, a_lo, a_zero, a_hs = (sem(x) for x in ("a_tr", "a_hi", "a_lo", "a_zero", "a_hs"))
        core.c_in, core.constants = sem("c_in"), 3 * 16
        c_in = core.c_in
        block = c.enter_context(nc.Block())

        @block.sync
        def _(sp):
            core.load_weights(0)
            sp.dma_start(core.gq[:], t["q_norm_g"].rearrange("(a d) -> a d", a=1).to_broadcast([P, DH])).then_inc(c_in, 16)
            sp.dma_start(core.mask_halves[:], t["mask_halves"]).then_inc(c_in, 16)
            sp.dma_start(core.gk[:], t["k_norm_g"].rearrange("(a d) -> a d", a=1).to_broadcast([P, DH])).then_inc(c_in, 16)
            for g in range(G):
                for dst, src in by_tile(core.rope[:, g, 0:NT, :], t["rope_table"][0:S, :], g):
                    sp.dma_start(dst, src).then_inc(c_in, 16)
                    core.constants += 16
                sp.dma_start(core.rope[0:NB, g, NT, :], t["rope_table"][S:S + 1, :].to_broadcast([NB, 32])).then_inc(c_in, 16)
                core.constants += 16
            core.load_weights(8)

        @block.gpsimd
        def _(pool):
            ch = core.pool
            ch.link(pool.memset(ident[:], 0.0))
            ch.link(pool.affine_select(out=ident[:], in_=ident[:], compare_op=ALU.not_equal, fill=1.0, base=0,
                                       pattern=[[-1, P]], channel_multiplier=1))
            pool.memset(core.ones[:], 1.0).then_inc(a_const, 1)
            for m in (core.mask_pair, core.mask_later):
                ch.mark(pool.memset(m[:], 0.0))
            ch.wait()
            ch.mark(pool.affine_select(out=core.mask_pair[:, 0:P], in_=core.mask_pair[:, 0:P], compare_op=ALU.is_ge, fill=NEG,
                                       base=0, pattern=[[1, P]], channel_multiplier=-1))
            ch.mark(pool.affine_select(out=core.mask_pair[:, P:2 * P], in_=core.mask_pair[:, P:2 * P], compare_op=ALU.is_ge,
                                       fill=NEG, base=0, pattern=[[-1, P]], channel_multiplier=1))
            ch.mark(pool.affine_select(out=core.mask_later[:], in_=core.mask_later[:], compare_op=ALU.is_ge, fill=NEG,
                                       base=0, pattern=[[1, P]], channel_multiplier=-1))
            ch.wait()
            pool.memset(core.mstat[:], 0.0).then_inc(a_const, 1)
            core.split_weights(8)

        @block.scalar
        def _(act):
            ch = core.act
            def take(n):
                cols = P if n < NT else NB
                for u in (2 * n, 2 * n + 1):
                    act.wait_ge(a_tr, u + 1)
                    nc.scalar.activation(hhi[:, 4 * (u % 2):4 * (u % 2) + 4, n * P:n * P + cols],
                                         ps[:, u % 4, :].rearrange("p (k c) -> p k c", k=4)[:, :, 0:cols],
                                         ACT.Copy).then_inc(a_hi, 1)

            for n in range(NT):
                act.dma_start(x_sb[:, n, :], t["x_prompt"][0, n * P:(n + 1) * P, :]).then_inc(a_in[n], 16)
                if n == 1:
                    act.dma_start(g1[:], t["norm1_g"].rearrange("(a d) -> a d", a=1).to_broadcast([P, D])).then_inc(a_g, 16)
            act.dma_start(x_sb[0:NB, NT, :], t["x_sample"].rearrange("b s d -> (b s) d")).then_inc(a_in[NT], 16)
            act.wait_ge(a_var, 1)
            for i, batch in enumerate(batches):
                for n in batch:
                    rows = P if n < NT else NB
                    act.wait_ge(a_in[n], 16)
                    if n >= 2:
                        act.wait_ge(a_ssq, n - 1)
                    nc.scalar.activation(sq_a[0:rows, n % 2, :], x_sb[0:rows, n, :], ACT.Square,
                                         accum_out=ssq[0:rows, n:n + 1]).then_inc(a_ssq, 1)
                act.wait_ge(a_var, i + 2)
                cols = slice(batch[0], batch[-1] + 1)
                nc.scalar.activation(ssq[:, cols], ssq[:, cols], ACT.Sqrt).then_inc(a_std, 1)
                for n in batches[i - 1] if i else ():
                    take(n)
            for n in batches[-1]:
                take(n)
            act.wait_ge(a_zero, 1)
            act.wait_ge(a_hi, 2 * (NT + 1))
            nc.scalar.activation(core.hs[:, :, 0:NB], hhi[:, :, S:T], ACT.Copy).then_inc(a_hs, 1)

        @block.vector
        def _(dve):
            ch = core.dve
            nc.vector.memset(ssq[:], 1.0).then_inc(a_var, 1)
            nc.vector.memset(core.hs[:].bitcast(F32), 0.0).then_inc(a_zero, 1)

            def take(n):
                cols = P if n < NT else NB
                for u in (2 * n, 2 * n + 1):
                    dve.wait_ge(a_hi, u + 1)
                    part = slice(4 * (u % 2), 4 * (u % 2) + 4), slice(n * P, n * P + cols)
                    nc.vector.tensor_tensor(hlo[:, part[0], part[1]],
                                            ps[:, u % 4, :].rearrange("p (k c) -> p k c", k=4)[:, :, 0:cols],
                                            hhi[:, part[0], part[1]].bitcast(F32), ALU.subtract).then_inc(a_lo, 1)

            for i, batch in enumerate(batches):
                cols = slice(batch[0], batch[-1] + 1)
                dve.wait_ge(a_ssq, batch[-1] + 1)
                nc.vector.tensor_scalar(ssq[:, cols], ssq[:, cols], 1.0 / D, EPS, ALU.mult, ALU.add).then_inc(a_var, 1)
                dve.wait_ge(a_std, i + 1)
                ch.link(nc.vector.reciprocal(ssq[:, cols], ssq[:, cols]))
                dve.wait_ge(a_g, 16)
                for n in batch:
                    rows = P if n < NT else NB
                    nc.vector.scalar_tensor_tensor(x_sb[0:rows, n, :], x_sb[0:rows, n, :], ssq[0:rows, n:n + 1],
                                                   g1[0:rows, :], ALU.mult, ALU.mult).then_inc(a_xn, 1)
                for n in batches[i - 1] if i else ():
                    take(n)
            for n in batches[-1]:
                take(n)
            dve.wait_ge(a_lo, 2 * (NT + 1))
            dve.wait_ge(a_zero, 1)
            nc.vector.tensor_copy(core.hs[:, :, 32:32 + NB], hlo[:, :, S:T]).then_inc(a_hs, 1)

        @block.tensor
        def _(pe):
            pe.wait_ge(a_const, 1)
            for u in range(2 * (NT + 1)):
                n, kk = divmod(u, 2)
                rows = P if n < NT else NB
                pe.wait_ge(a_xn, n + 1)
                if u >= 4:
                    pe.wait_ge(a_lo, u - 3)
                for k in range(4):
                    last = nc.tensor.transpose(ps[:, u % 4, k * P:k * P + rows],
                                               x_sb[0:rows, n, (4 * kk + k) * P:(4 * kk + k + 1) * P],
                                               ident[0:rows, 0:rows])
                last.then_inc(a_tr, 1)



class Projection:

    Z = 4

    def __init__(self, core, c, g):
        self.core, self.g = core, g
        sb, sem, Z = core.sb, core.sem, self.Z
        self.groups = 3 if g is not None else 4
        self.units = self.groups * (NT + 1)
        self.nq = 2 * (NT + 1)
        self.steps = self.units + 2
        self.p0 = core.taken
        core.taken += self.groups * KD
        tag = "m" if g is None else g
        self.zt = sb(f"zt{tag}", [P, Z, 512], ctx=c)
        self.tt = sb(f"tt{tag}", [P, 2, 512], ctx=c)
        if g is not None:
            self.sq = sb(f"sq{g}", [P, 512], ctx=c)
            self.st = sb(f"st{g}", [P, Z, H], ctx=c)
            self.rt = sb(f"rt{g}", [P, 2, H, 16], ctx=c)
        self.half = sb(f"zh{tag}", [NB, 512], ctx=c)
        (self.mm, self.ev, self.hlf, self.var, self.std, self.nrm, self.tr, self.tre) = (
            sem(f"b_{x}{tag}") for x in ("mm", "ev", "hlf", "var", "std", "nrm", "tr", "tre"))
        self.zout = [core.store_sem(f"b_zout{tag}_{i}") for i in range(Z)]
        self.tout = [sem(f"b_tout{tag}_{i}") for i in range(2)]
        self.n_out, self.done_at = [0] * Z, {}
        for u in range(self.units):
            self.n_out[u % Z] += 16 * len(self.stores(u))
            self.done_at[u] = self.n_out[u % Z]

    def stores(self, u):
        core, g = self.core, self.g
        x, n = divmod(u, NT + 1)
        if g is None:
            if n == NT:
                return [core.zm_s[:, x * 512:(x + 1) * 512]]
            return [core.m_tok[n, :, x - 1, :]] if x else []
        if n == NT:
            return [core.z_s[g, x]]
        out = [core.a_v[g, n]] if x == 2 else []
        keep, length = min(WINDOWS[g], S), S // STEPS[g]
        if x and (keep == S or (n + 1) * P % length == 0):
            rows = core.o[2 + g][0][:, x - 1].rearrange("(i d) h c -> d i (h c)", d=STEPS[g])
            out.append(rows[n * P // length])
        return out

    def wait_turned(self, eng, u):
        m = min(u + 1, self.nq)
        eng.wait_ge(self.tr, m - m // (NT + 1))

    def wait_whole(self, eng, u):
        if self.g is not None and u < self.nq:
            eng.wait_ge(self.nrm, u + 1)
        else:
            eng.wait_ge(self.ev, u + 1)

    def pe(self, u):
        core, nc, ps, g = self.core, self.core.nc, self.core.ps, self.g
        pe = nc.tensor
        if u < self.units:
            x, n = divmod(u, NT + 1)
            if u >= 2:
                pe.wait_ge(self.ev, u - 1)
            for k in range(KD):
                w = core.weight(self.p0 + x * KD + k, slice(0, CW))
                if n == NT:
                    pe.matmul(ps[0:40, u % 2, :], core.hs[:, k, :], w[0], start=(k == 0), stop=False)
                    pe.matmul(ps[0:40, u % 2, :], core.hs[:, k, :], w[1], start=False,
                              stop=(k == KD - 1)).then_inc(core.w_used, 1)
                    continue
                lhs = [residues(a[:, k, 0:S], g or 0, n) for a in (core.hhi, core.hlo)]
                if n == 0:
                    pe.wait_ge(core.w_lo, self.p0 + x * KD + k + 1)
                last = products(nc, ps[:, u % 2, :], lhs, w, k == 0, k == KD - 1)
            if n < NT:
                last.then_inc(self.mm, 1)
        v = u - 2
        if 0 <= v < self.nq and v % (NT + 1) < NT:
            self.wait_whole(pe, v)
            t = v - v // (NT + 1)
            if t >= 1:
                pe.wait_ge(self.tre, t)
            for j in range(4):
                last = pe.transpose(ps[:, 2, j * P:(j + 1) * P], self.zt[:, v % self.Z, j * P:(j + 1) * P],
                                    core.ident[:])
            last.then_inc(self.tr, 1)

    def act(self, u):
        core, nc, ps, g, Z = self.core, self.core.nc, self.core.ps, self.g, self.Z
        act = nc.scalar
        if u < self.units:
            x, n = divmod(u, NT + 1)
            rows = P if n < NT else NB
            if n == 0 and u:
                act.wait_ge(self.ev, u)
            if n < NT:
                act.wait_ge(self.mm, u + 1 - (u + 1) // (NT + 1))
            else:
                act.wait_ge(core.w_used, self.p0 + (x + 1) * KD)
            if u >= Z:
                self.wait_turned(act, u - Z)
                if self.done_at[u - Z]:
                    act.wait_ge(self.zout[u % Z], self.done_at[u - Z])
            scale = SCALE if g is None and x == 0 else 1.0
            if n < NT:
                act.activation(self.zt[:, u % Z, :], ps[:, u % 2, :], ACT.Copy, scale=scale).then_inc(self.ev, 1)
            else:
                act.activation(self.half[:], ps[32:32 + NB, u % 2, :], ACT.Copy, scale=scale).then_inc(self.hlf, 1)
        v = u - 1
        if g is not None and 0 <= v < self.nq:
            rows = P if v % (NT + 1) < NT else NB
            act.wait_ge(self.var, v + 1)
            act.activation(self.st[0:rows, v % Z, :], self.st[0:rows, v % Z, :], ACT.Sqrt).then_inc(self.std, 1)
        v = u - 2
        if v < 0:
            return
        x, n = divmod(v, NT + 1)
        if v < self.nq and n < NT:
            t = v - v // (NT + 1)
            act.wait_ge(self.tr, t + 1)
            if t >= 2:
                act.wait_ge(self.tout[t % 2], 16 * (t // 2))
            act.activation(self.tt[:, t % 2, :], ps[:, 2, :], ACT.Copy).then_inc(self.tre, 1)
            act.wait_ge(self.tre, t + 1)
            dst = core.m_tr[x, n] if g is None else core.a_tr[g, x, n]
            act.dma_start(dst, self.tt[:, t % 2, :]).then_inc(self.tout[t % 2], 16)
        for dst in self.stores(v):
            self.wait_whole(act, v)
            act.dma_start(dst, self.zt[0:NB if n == NT else P, v % Z, :]).then_inc(self.zout[v % Z], 16)

    def act_end(self):
        for i in range(self.Z):
            self.core.defer(self.zout[i], self.n_out[i])
        for i in range(2):
            self.core.defer(self.tout[i], 16 * NT)

    def dve(self, u):
        core, nc, Z, ch, g = self.core, self.core.nc, self.Z, self.core.dve, self.g
        dve = nc.vector
        if u < self.units and u % (NT + 1) == NT:
            dve.wait_ge(self.hlf, u // (NT + 1) + 1)
            dve.scalar_tensor_tensor(self.zt[0:NB, u % Z, :], core.ps[0:NB, u % 2, :],
                                     SCALE if g is None and u < NT + 1 else 1.0, self.half[:], ALU.mult,
                                     ALU.add).then_inc(self.ev, 1)
        if g is None:
            return
        if u == 0 and g == 0:
            dve.wait_ge(core.c_in, core.constants)
        if u < self.nq:
            rows = P if u % (NT + 1) < NT else NB
            z, st = self.zt[0:rows, u % Z, :], self.st[0:rows, u % Z, :]
            dve.wait_ge(self.ev, u + 1)
            ch.link(dve.tensor_tensor(self.sq[0:rows, :], z, z, ALU.mult))
            ch.link(dve.tensor_reduce(st, self.sq[0:rows, :].rearrange("p (h c) -> p h c", h=H), AX.X, ALU.add))
            dve.tensor_scalar(st, st, 1.0 / DH, EPS, ALU.mult, ALU.add).then_inc(self.var, 1)
        v = u - 1
        if 0 <= v < self.nq:
            x, n = divmod(v, NT + 1)
            rows = P if n < NT else NB
            z = self.zt[0:rows, v % Z, :].rearrange("p (h c) -> p h c", h=H)
            st, r = self.st[0:rows, v % Z, :], self.rt[0:rows]
            gain = (core.gq, core.gk)[x][0:rows, :].unsqueeze(1).to_broadcast([rows, H, DH])
            tab = core.rope[0:rows, g, n, :].unsqueeze(1).to_broadcast([rows, H, 32])
            dve.wait_ge(self.std, v + 1)
            ch.link(dve.reciprocal(st, st))
            ch.link(dve.tensor_tensor(z, z, bc(st, [rows, H, DH]), ALU.mult))
            ch.link(dve.tensor_tensor(z, z, gain, ALU.mult))
            ch.mark(dve.tensor_tensor(r[:, 0], z[:, :, 0:16], tab[:, :, 0:16], ALU.mult))
            ch.mark(dve.tensor_tensor(r[:, 1, :, 0:8], z[:, :, 8:16], tab[:, :, 16:24], ALU.mult))
            ch.link(dve.tensor_tensor(r[:, 1, :, 8:16], z[:, :, 0:8], tab[:, :, 24:32], ALU.mult))
            dve.tensor_tensor(z[:, :, 0:16], r[:, 0], r[:, 1], ALU.add).then_inc(self.nrm, 1)


class Attention:

    def __init__(self, core, c, g):
        self.core, self.g = core, g
        sb, sem = core.sb, core.sem
        self.items = [(n, hh) for n in range(NT) for hh in range(2)]
        self.steps = len(self.items) + 2
        self.q = sb(f"aq{g}", [P, 2, 4, P], ctx=c)
        self.k = sb(f"ak{g}", [P, 3, 4, P], ctx=c)
        self.v = sb(f"av{g}", [P, 4, 512], ctx=c)
        self.sc = sb(f"sc{g}", [P, 2, 4, 2 * P], ctx=c)
        self.pt = sb(f"pt{g}", [P, 4, 2 * P], ctx=c)
        self.nm = sb(f"nm{g}", [P, 2, 4], ctx=c)
        self.ot = sb(f"ot{g}", [P, 2, 512], ctx=c)
        (self.qk, self.msk, self.neg, self.prb, self.ptr, self.pte_a, self.pte_v, self.pv, self.oev) = (
            sem(f"t_{x}{g}") for x in ("qk", "msk", "neg", "prb", "ptr", "pte_a", "pte_v", "pv", "oev"))
        self.o_out = [sem(f"t_out{g}_{i}") for i in range(2)]
        self.t_in = [sem(f"t_in{g}_{i}") for i in range(2)]
        self.ml_out = sem(f"t_ml{g}")

    def blocks(self, n):
        return [n - 1, n] if has_prev(self.g, n) else [n]

    def heads(self, hh):
        return [(4 * hh + 2 * i + par, par, i) for i in range(2) for par in range(2)]

    def load(self, n):
        act, core, g = self.core.nc.scalar, self.core, self.g
        for dst, src in ((self.q[:, n % 2], core.a_tr[g, 0, n].rearrange("p (j c) -> p j c", j=4)),
                         (self.k[:, n % 3], core.a_tr[g, 1, n].rearrange("p (j c) -> p j c", j=4)),
                         (self.v[:, n % 4, :], core.a_v[g, n])):
            act.dma_start(dst, src).then_inc(self.t_in[n % 2], 16)

    def pe(self, i):
        core, ps = self.core, self.core.ps
        pe = core.nc.tensor
        if i < len(self.items):
            n, hh = self.items[i]
            tiles = self.blocks(n)
            if hh == 0:
                pe.wait_ge(self.t_in[n % 2], 48 * (n // 2 + 1))
            if i >= 1:
                pe.wait_ge(self.msk, i)
            for h, par, j in self.heads(hh):
                rows = slice(DH * par, DH * par + DH)
                for b, m in enumerate(tiles):
                    at = (2 * j + b) * P
                    last = pe.matmul(ps[:, 3 + par, at:at + P], self.q[rows, n % 2, h // 2, :],
                                     self.k[rows, m % 3, h // 2, :], start=True, stop=True)
            last.then_inc(self.qk, 1)
        w = i - 2
        if w >= 0:
            n, hh = self.items[w]
            tiles = self.blocks(n)
            pe.wait_ge(self.pte_a, w + 1)
            pe.wait_ge(self.pte_v, w + 1)
            if hh == 0 and n >= 1:
                pe.wait_ge(self.oev, n)
            for h, par, j in self.heads(hh):
                for b, m in enumerate(tiles):
                    last = pe.matmul(ps[:, 7, h * DH:(h + 1) * DH], self.pt[:, 2 * par + j, b * P:(b + 1) * P],
                                     self.v[:, m % 4, h * DH:(h + 1) * DH], start=(b == 0),
                                     stop=(b == len(tiles) - 1))
            last.then_inc(self.pv, 1)
        w = i - 1
        if 0 <= w < len(self.items):
            n, hh = self.items[w]
            pe.wait_ge(self.prb, w + 1)
            if w >= 1:
                pe.wait_ge(self.pte_a, w)
                pe.wait_ge(self.pte_v, w)
            for h, par, j in self.heads(hh):
                for b in range(len(self.blocks(n))):
                    at = (2 * j + b) * P
                    last = pe.transpose(ps[:, 5 + par, at:at + P], self.sc[:, w % 2, 2 * par + j, b * P:(b + 1) * P],
                                        core.ident[:])
            last.then_inc(self.ptr, 1)

    def dve_first(self, i):
        core, ps, g, ch = self.core, self.core.ps, self.g, self.core.dve
        dve = core.nc.vector
        w = i - 1
        if not 0 <= w < len(self.items):
            return
        n, hh = self.items[w]
        span = P * len(self.blocks(n))
        mask = core.mask_halves[:] if g == 2 else core.mask_pair[:, 2 * P - span:]
        dve.wait_ge(self.qk, w + 1)
        if w >= 2:
            dve.wait_ge(self.ptr, w - 1)
            dve.wait_ge(self.prb, w - 1)
        for h, par, j in self.heads(hh):
            ins = dve.tensor_tensor_reduce(self.sc[:, w % 2, 2 * par + j, 0:span],
                                           ps[:, 3 + par, 2 * j * P:2 * j * P + span], mask, SCALE, 3 * NEG,
                                           ALU.add, ALU.max, core.mstat[:, g, 0, n, h:h + 1])
            if (par, j) == (1, 1):
                ins.then_inc(self.msk, 1)
            else:
                ch.mark(ins)
        ch.wait()
        dve.wait_ge(self.msk, w + 1)
        dve.tensor_scalar(self.nm[:, w % 2, :], core.mstat[:, g, 0, n, 4 * hh:4 * hh + 4], -1.0, None,
                          ALU.mult).then_inc(self.neg, 1)

    def act_first(self, i):
        core, g, ch = self.core, self.g, self.core.act
        act = core.nc.scalar
        if i == 0:
            self.load(0)
            self.load(1)
        elif i % 2 == 0 and 2 <= i // 2 + 1 < NT:
            act.wait_ge(self.qk, i)
            if i >= 4:
                act.wait_ge(self.pv, i - 3)
            self.load(i // 2 + 1)
        w = i - 1
        if not 0 <= w < len(self.items):
            return
        n, hh = self.items[w]
        span = P * len(self.blocks(n))
        act.wait_ge(self.neg, w + 1)
        for h, par, j in self.heads(hh):
            row = self.sc[:, w % 2, 2 * par + j, 0:span]
            ins = act.activation(row, row, ACT.Exp, bias=self.nm[:, w % 2, h - 4 * hh:h - 4 * hh + 1],
                                 accum_out=core.mstat[:, g, 1, n, h:h + 1])
            if (par, j) == (1, 1):
                ins.then_inc(self.prb, 1)
            else:
                ch.mark(ins)

    def take(self, eng, copy, par, w, sem):
        eng.wait_ge(self.ptr, w + 1)
        if w >= 1:
            eng.wait_ge(self.pv, w)
        span = P * len(self.blocks(self.items[w][0]))
        copy(self.pt[:, 2 * par:2 * par + 2, 0:span],
             self.core.ps[:, 5 + par, :].rearrange("p (i c) -> p i c", i=2)[:, :, 0:span]).then_inc(sem, 1)

    def dve_last(self, i):
        dve, ps = self.core.nc.vector, self.core.ps
        if 1 <= i <= len(self.items):
            self.take(dve, dve.tensor_copy, 1, i - 1, self.pte_v)
        if i >= 3 and i % 2 == 1:
            n = (i - 3) // 2
            dve.wait_ge(self.pv, 2 * n + 2)
            if n >= 2:
                dve.wait_ge(self.o_out[n % 2], 16 * (n // 2))
            dve.tensor_copy(self.ot[:, n % 2, :], ps[:, 7, :]).then_inc(self.oev, 1)

    def act_last(self, i):
        act = self.core.nc.scalar
        if 1 <= i <= len(self.items):
            self.take(act, act.copy, 0, i - 1, self.pte_a)
        if i >= 3 and i % 2 == 1:
            n = (i - 3) // 2
            act.wait_ge(self.oev, n + 1)
            act.dma_start(self.core.o_grp[self.g, n], self.ot[:, n % 2, :]).then_inc(self.o_out[n % 2], 16)
        if i == self.steps - 1:
            act.wait_ge(self.prb, len(self.items))
            self.core.act.wait()
            for src, dst in self.statistics():
                act.dma_start(dst, src).then_inc(self.ml_out, 16)

    def statistics(self):
        core, g = self.core, self.g
        return [pair for x in range(2) for pair in by_tile(core.mstat[:, g, x], core.ml_nat[g, x], g)]

    def act_end(self):
        act = self.core.nc.scalar
        for i in range(2):
            act.wait_ge(self.o_out[i], 16 * NT // 2)
        act.wait_ge(self.ml_out, 16 * len(self.statistics()))


class SampleScores:

    def __init__(self, core, c):
        self.core = core
        sb, sem = core.sb, core.sem
        self.units = [(b, g) for b in range(NB) for g in range(G)] + [(None, g) for g in range(G)]
        self.steps = len(self.units) + 1
        self.kc = sb("k_kc", [P, 2, 512], ctx=c)
        self.qb = sb("k_qb", [P, 2, 512], ctx=c)
        self.k_in = [sem(f"k_in{i}") for i in range(2)]
        self.sc = sem("k_sc")

    def act(self, i):
        core, act = self.core, self.core.nc.scalar
        if i >= len(self.units):
            return
        b, g = self.units[i]
        if i >= 2:
            act.wait_ge(self.sc, i - 1)
        if b is None:
            rows, key, query = slice(0, NB), core.z_s[g, 1], core.z_s[g, 0]
        else:
            rows, key = slice(0, P), cached_rows(core, g, b, 0)
            query = core.z_s[g, 0, b:b + 1, :].to_broadcast([P, 512])
        act.dma_start(self.kc[rows, i % 2, :], key).then_inc(self.k_in[i % 2], 16)
        act.dma_start(self.qb[rows, i % 2, :], query).then_inc(self.k_in[i % 2], 16)

    def dve(self, i):
        core, ch, v = self.core, self.core.dve, i - 1
        dve = core.nc.vector
        if v < 0:
            return
        b, g = self.units[v]
        rows = slice(0, P if b is not None else NB)
        kc, qb = self.kc[rows, v % 2, :], self.qb[rows, v % 2, :]
        dve.wait_ge(self.k_in[v % 2], 32 * (v // 2 + 1))
        ch.link(dve.tensor_tensor(kc, kc, qb, ALU.mult))
        dst = core.ss[:, b, g, :] if b is not None else core.sn[:, g, :]
        dve.tensor_reduce(dst, kc.rearrange("p (h c) -> p h c", h=H), AX.X, ALU.add).then_inc(self.sc, 1)


def cached_rows(core, g, b, which):
    cache = core.t[f"cache_kv_w{WINDOWS[g]}"]
    return cache[b].rearrange("(j d) a h c -> d j a (h c)", d=DILS[g])[0, :, which]


def project(core, g, att_g):
    nc = core.nc
    with ExitStack() as c:
        proj = Projection(core, c, g)
        att = Attention(core, c, att_g) if att_g is not None else None
        gates = Gates(core, c) if g == 0 else None
        sample = SampleScores(core, c) if g is None else None
        steps = range(max(proj.steps, att.steps if att else 0))
        block = c.enter_context(nc.Block())

        @block.sync
        def _(sp):
            if gates:
                gates.load()
            core.load_weights(core.taken + 8)
            if gates:
                gates.store_m()

        @block.gpsimd
        def _(pool):
            core.split_weights(core.taken + 8)

        @block.tensor
        def _(pe):
            for i in steps:
                if i < proj.steps:
                    proj.pe(i)
                if gates and i == proj.nq - 3:
                    gates.pe()
                if att and i < att.steps:
                    att.pe(i)

        @block.scalar
        def _(act):
            core.settle(act)
            for i in steps:
                if sample and i < sample.steps:
                    sample.act(i)
                if att and i < att.steps:
                    att.act_first(i)
                if i < proj.steps:
                    proj.act(i)
                if gates and i == proj.nq + 1:
                    gates.act_first()
                if gates and i == proj.nq + 3:
                    gates.act_last()
                if att and i < att.steps:
                    att.act_last(i)
            if gates:
                gates.act_end()
            proj.act_end()
            if att:
                att.act_end()

        @block.vector
        def _(dve):
            for i in steps:
                if att and i < att.steps:
                    att.dve_first(i)
                if i < proj.steps:
                    proj.dve(i)
                if gates and i == proj.nq - 5:
                    gates.dve_first()
                if gates and i == proj.nq:
                    gates.dve_last()
                if att and i < att.steps:
                    att.dve_last(i)
                if sample and i < sample.steps:
                    sample.dve(i)


class GroupMerge:

    FIRST = 6

    def __init__(self, core, c):
        self.core = core
        sb, sem = core.sb, core.sem
        self.ml = sb("ml", [P, G, 2, NT, H], ctx=c)
        self.mx = sb("mx", [P, NT, H], ctx=c)
        self.cf = sb("cf", [P, G, NT, H], ctx=c)
        self.cr = sb("cr", [P, G, NT, H], ctx=c)
        self.og = sb("og", [P, 4, 512], ctx=c)
        self.at = sb("at", [P, 4, S], ctx=c)
        (self.m_in, self.e_sub, self.e_exp, self.c_done, self.c_out, self.c_in, self.scaled, self.tr, self.added,
         self.a_out) = (sem(f"m_{x}") for x in ("in", "sub", "exp", "done", "cout", "cin", "scaled", "tr", "added", "aout"))
        self.o_in = [sem(f"m_oin{i}") for i in range(4)]
        self.tiles = [(g, n) for g in range(G) for n in range(NT)]
        self.last = self.FIRST + len(self.tiles) // 2

    def pair(self, i):
        v = 2 * (i - self.FIRST)
        return range(v, v + 2) if 0 <= v < len(self.tiles) else range(0)

    def load(self, u):
        g, n = self.tiles[u]
        self.core.nc.scalar.dma_start(self.og[:, u % 4, :], self.core.o_grp[g, n]).then_inc(self.o_in[u % 4], 16)

    def act(self, i):
        core, act = self.core, self.core.nc.scalar
        if i == 0:
            for g in range(G):
                for x in range(2):
                    act.dma_start(self.ml[:, g, x], core.ml_nat[g, x].rearrange("(n p) h -> p n h", p=P)).then_inc(self.m_in, 16)
            for u in range(4):
                self.load(u)
        elif i == 2:
            act.wait_ge(self.e_sub, 1)
            act.activation(self.cf[:], self.cf[:], ACT.Exp).then_inc(self.e_exp, 1)
        elif i == 4:
            act.wait_ge(self.c_done, 1)
            for g in range(G):
                act.dma_start(core.cf_nat[g].rearrange("(n p) c -> p n c", p=P), self.cf[:, g]).then_inc(self.c_out, 16)
        elif i == 5:
            act.wait_ge(self.c_out, 16 * G)
            for g in range(G):
                for dst, src in by_tile(self.cr[:, g], core.cf_nat[g], g):
                    act.dma_start(dst, src).then_inc(self.c_in, 16)
        elif i == self.last + 1:
            act.wait_ge(self.added, len(self.tiles))
            act.dma_start(core.att_t[:, :, 0:S].rearrange("k p t -> p k t"), self.at[:]).then_inc(self.a_out, 16)
        if i > self.FIRST:
            for u in self.pair(i + 1):
                act.wait_ge(self.tr, u - 3)
                self.load(u)

    def act_end(self):
        self.core.nc.scalar.wait_ge(self.a_out, 16)

    def dve(self, i):
        core, ch, ps = self.core, self.core.dve, self.core.ps
        dve, ml, mx, cf = core.nc.vector, self.ml, self.mx, self.cf
        if i == 1:
            dve.wait_ge(self.m_in, 16 * 2 * G)
            ch.link(dve.tensor_tensor(mx[:], ml[:, 0, 0], ml[:, 1, 0], ALU.max))
            ch.link(dve.tensor_tensor(mx[:], mx[:], ml[:, 2, 0], ALU.max))
            dve.tensor_tensor(cf[:], ml[:, :, 0], mx[:].unsqueeze(1).to_broadcast([P, G, NT, H]),
                              ALU.subtract).then_inc(self.e_sub, 1)
        elif i == 3:
            dve.wait_ge(self.e_exp, 1)
            ch.link(dve.tensor_tensor(ml[:, :, 1], ml[:, :, 1], cf[:], ALU.mult))
            ch.link(dve.tensor_tensor(mx[:], ml[:, 0, 1], ml[:, 1, 1], ALU.add))
            ch.link(dve.tensor_tensor(mx[:], mx[:], ml[:, 2, 1], ALU.add))
            ch.link(dve.reciprocal(mx[:], mx[:]))
            dve.tensor_tensor(cf[:], cf[:], mx[:].unsqueeze(1).to_broadcast([P, G, NT, H]),
                              ALU.mult).then_inc(self.c_done, 1)
        elif i == self.FIRST:
            dve.wait_ge(self.c_in, 16 * sum(len(by_tile(self.cr[:, g], core.cf_nat[g], g)) for g in range(G)))
        for u in self.pair(i):
            g, n = self.tiles[u]
            dve.wait_ge(self.o_in[u % 4], 16 * (u // 4 + 1))
            v = self.og[:, u % 4, :].rearrange("p (h c) -> p h c", h=H)
            dve.tensor_tensor(v, v, bc(self.cr[:, g, n, :], [P, H, DH]), ALU.mult).then_inc(self.scaled, 1)
        for u in self.pair(i - 1):
            g, n = self.tiles[u]
            dve.wait_ge(self.tr, u + 1)
            dst = residues(self.at[:], g, n)
            src = ps[:, 2 + u % 2, :].rearrange("p (k c) -> p k c", k=4)
            if g == 0:
                dve.tensor_copy(dst, src).then_inc(self.added, 1)
            else:
                dve.wait_ge(self.added, g * NT)
                dve.tensor_tensor(dst, dst, src, ALU.add).then_inc(self.added, 1)

    def pe(self, i):
        pe, ps = self.core.nc.tensor, self.core.ps
        for u in self.pair(i):
            pe.wait_ge(self.scaled, u + 1)
            if u >= 2:
                pe.wait_ge(self.added, u - 1)
            for j in range(4):
                last = pe.transpose(ps[:, 2 + u % 2, j * P:(j + 1) * P], self.og[:, u % 4, j * P:(j + 1) * P],
                                    self.core.ident[:])
            last.then_inc(self.tr, 1)


class Gates:

    def __init__(self, core, c):
        self.core = core
        sb, sem = core.sb, core.sem
        self.w = sb("wif", [P, KD, 16], ctx=c)
        self.hi = sb("wif_hi", [P, KD, 40], F32R, c)
        self.lo = sb("wif_lo", [P, KD, 40], F32R, c)
        self.bias = sb("bif", [40, 1], ctx=c)
        self.yy = sb("yif", [40, T], ctx=c)
        self.ab = sb("aif", [40, T], ctx=c)
        self.ig = sb("igf", [8, T], ctx=c)
        self.lf = sb("lfg", [8, T], ctx=c)
        self.bb = sb("g_b", [8, S], ctx=c)
        self.mx = sb("g_m", [8, S], ctx=c)
        self.zero = sb("g_zero", [8, P], ctx=c)
        self.m_run = sb("g_run", [8, NT + 1], ctx=c)
        (self.w_in, self.w_hi, self.w_lo, self.mm, self.ab_set, self.ln, self.done, self.out, self.end) = (
            sem(f"g_{x}") for x in ("w_in", "w_hi", "w_lo", "mm", "ab_set", "ln", "done", "out", "end"))
        self.m_out = core.store_sem("g_mout")

    def load(self):
        t, sp = self.core.t, self.core.nc.sync
        sp.dma_start(self.w[:], t["w_in"].rearrange("(k p) c -> p k c", p=P)[:, :, CIF:CIF + 16]).then_inc(self.w_in, 16)
        for rows, at in ((slice(0, 8), 0), (slice(32, 40), 8)):
            sp.dma_start(self.bias[rows, :], t["b_if"].rearrange("(h a) -> h a", a=1)[at:at + 8, :]).then_inc(self.w_in, 16)

    def store_m(self):
        sp = self.core.nc.sync
        sp.wait_ge(self.end, 1)
        sp.dma_start(self.core.o[7].rearrange("a h -> h a"), self.m_run[:, NT:NT + 1]).then_inc(self.m_out, 16)
        self.core.defer(self.m_out, 16)

    def pe(self):
        core, nc = self.core, self.core.nc
        nc.tensor.wait_ge(self.w_lo, 2)
        for s in range(3):
            seg = slice(s * SEG, (s + 1) * SEG)
            for k in range(KD):
                last = products(nc, core.ps[0:40, 5 + s, 0:SEG], (self.hi[:, k, :], self.lo[:, k, :]),
                                (core.hhi[:, k, seg], core.hlo[:, k, seg]), k == 0, k == KD - 1)
        last.then_inc(self.mm, 1)

    def act_first(self):
        act, ab = self.core.nc.scalar, self.ab[32:40, :]
        act.wait_ge(self.ab_set, 1)
        act.activation(ab, ab, ACT.Exp, scale=-1.0).then_inc(self.ln, 1)
        act.wait_ge(self.ln, 1)
        act.activation(ab, ab, ACT.Ln, bias=1.0).then_inc(self.ln, 1)

    def act_last(self):
        act, core = self.core.nc.scalar, self.core
        act.wait_ge(self.done, 1)
        act.dma_start(core.if_s[0], self.ig[0:8, S:T]).then_inc(self.out, 16)
        act.dma_start(core.if_s[1], self.lf[0:8, S:T]).then_inc(self.out, 16)

    def act_end(self):
        act, core = self.core.nc.scalar, self.core
        act.wait_ge(self.end, 1)
        act.dma_start(core.neg_all.rearrange("n h t -> h n t"), core.neg_m[:].rearrange("h (n t) -> h n t", n=NT)).then_inc(
            self.out, 16)
        core.defer(self.out, 48)

    def dve_first(self):
        core, ch, dve = self.core, self.core.dve, self.core.nc.vector
        bands, zero, m_run = core.bands, self.zero, self.m_run
        for w in (self.hi, self.lo):
            ch.mark(dve.memset(w[:].bitcast(F32), 0.0))
        ch.mark(dve.memset(zero[:], 0.0))
        ch.mark(dve.memset(m_run[:], 0.0))
        ch.mark(dve.memset(bands[:], 0.0))
        dve.wait_ge(self.w_in, 48)
        ch.wait()
        for at, frm in ((0, 0), (32, 8)):
            dve.tensor_copy(self.hi[:, :, at:at + 8], self.w[:, :, frm:frm + 8]).then_inc(self.w_hi, 1)
        dve.wait_ge(self.w_hi, 2)
        for at, frm in ((0, 0), (32, 8)):
            dve.tensor_tensor(self.lo[:, :, at:at + 8], self.w[:, :, frm:frm + 8],
                              self.hi[:, :, at:at + 8].bitcast(F32), ALU.subtract).then_inc(self.w_lo, 1)

    def dve_last(self):
        core, ch = self.core, self.core.dve
        dve, bands, neg_m = core.nc.vector, core.bands, core.neg_m
        ig, lf, bb, mx, zero, m_run = self.ig, self.lf, self.bb, self.mx, self.zero, self.m_run
        yy, ab = self.yy[32:40, :], self.ab[32:40, :]
        dve.wait_ge(self.mm, 1)
        src = core.ps[:, 5:8, 0:SEG]
        ch.mark(dve.tensor_scalar(seg3(ig[0:8, :]), src[0:8], self.bias[0:8, :], None, ALU.add))
        ch.link(dve.tensor_scalar(seg3(yy), src[32:40], self.bias[32:40, :], None, ALU.add))
        dve.scalar_tensor_tensor(ab, yy, -1.0, yy, ALU.mult, ALU.max).then_inc(self.ab_set, 1)
        dve.wait_ge(self.ab_set, 1)
        ch.link(dve.tensor_scalar(yy, yy, 0.0, None, ALU.min))
        dve.wait_ge(self.ln, 2)
        dve.tensor_tensor(lf[0:8, :], yy, ab, ALU.subtract).then_inc(self.done, 1)
        dve.wait_ge(self.done, 1)
        for n in range(NT):
            cols = slice(n * P, (n + 1) * P)
            ch.mark(dve.tensor_tensor_scan(bb[:, cols], lf[0:8, cols], zero[:], 0.0, ALU.add, ALU.add))
        ch.wait()
        ch.link(dve.tensor_tensor(bands[0:8, :], ig[0:8, 0:S], bb[:], ALU.subtract))
        for n in range(NT):
            cols = slice(n * P, (n + 1) * P)
            end = slice(n * P + P - 1, n * P + P)
            ch.link(dve.tensor_tensor_scan(mx[:, cols], zero[:], bands[0:8, cols], m_run[:, n:n + 1], ALU.add, ALU.max))
            ch.mark(dve.tensor_tensor(m_run[:, n + 1:n + 2], bb[:, end], mx[:, end], ALU.add))
            ch.mark(dve.tensor_scalar(bands[32:40, cols], mx[:, cols], -1.0, m_run[:, n:n + 1], ALU.mult, ALU.add))
            ch.link(dve.tensor_scalar(bands[96:104, cols], bands[0:8, cols], mx[:, end], None, ALU.subtract))
        ch.mark(dve.scalar_tensor_tensor(bands[64:72, :], mx[:], -1.0, bb[:], ALU.mult, ALU.subtract))
        ch.link(dve.tensor_scalar(neg_m[:], mx[:], -1.0, None, ALU.mult))
        dve.tensor_copy(m_run[:, 0:1], zero[:, 0:1]).then_inc(self.end, 1)


class Chunks:

    STEPS = 5

    def __init__(self, core, c):
        self.core = core
        sb, sem = core.sb, core.sem
        self.E = E = DV + 1
        self.q = sb("c_q", [P, 2, 4, P], ctx=c)
        self.k = sb("c_k", [P, 2, 4, P], ctx=c)
        self.kk = sb("c_kk", [P, 2, H, DH], ctx=c)
        self.v = sb("c_v", [P, 2, H, E], ctx=c)
        self.mb = sb("c_mb", [P, 2, H, P], ctx=c)
        self.st = sb("c_state", [P, 4, E], ctx=c)
        self.xt = sb("c_xt", [P, P], ctx=c)
        self.xe = sb("c_xe", [P, 3, H], ctx=c)
        self.ww = sb("c_w", [P, H, P], ctx=c)
        self.num = sb("c_num", [P, H, E], ctx=c)
        self.den = sb("c_den", [P, H], ctx=c)
        self.ht = sb("c_ht", [P, H, P], ctx=c)
        self.kw = sb("c_kw", [P, H, DH], ctx=c)
        self.dec = sb("c_dec", [P, 4], ctx=c)
        (self.one, self.st0, self.xtp, self.xts, self.xex, self.kq, self.wm, self.wex, self.wqk,
         self.inter, self.nsc, self.intra, self.num_set, self.dstp, self.kwd, self.up, self.std, self.hbd,
         self.htp, self.hts, self.hts2, self.h_out) = (
            sem(f"c_{x}") for x in ("one", "st0", "xtp", "xts", "xex", "kq", "wm", "wex", "wqk", "inter",
                "nsc", "intra", "num_set", "dstp", "kwd", "up", "std", "hbd", "htp", "hts", "hts2", "h_out"))
        self.c_in = [sem(f"c_in{i}") for i in range(2)]
        self.c_out = core.store_sem("c_out")

    def at(self, h):
        return 4 * (h % 2) + h // 2

    def rows(self, h):
        return slice(DH * (h % 2), DH * (h % 2) + DH)

    def inter_at(self, h):
        i, E = h // 2, self.E
        return (2 if i < 3 else 6) + h % 2, slice((i % 3) * E, (i % 3 + 1) * E)

    def intra_at(self, h):
        E = self.E
        return 4 + h // 3, slice((h % 3) * E, (h % 3 + 1) * E)

    def update_at(self, h):
        i, E = h // 2, self.E
        return (2, slice(i * E, (i + 1) * E)) if i < 3 else (3, slice(P, P + E))

    def load(self, n):
        act, core, b = self.core.nc.scalar, self.core, n % 2
        for two in range(2):
            act.dma_start(self.mb[:, b, 4 * two:4 * two + 4, :],
                          core.neg_all[n, two::2].unsqueeze(0).to_broadcast([P, 4, P])).then_inc(self.c_in[b], 16)
        for dst, src in ((self.q[:, b], core.m_tr[0, n].rearrange("p (j c) -> p j c", j=4)),
                         (self.k[:, b], core.m_tr[1, n].rearrange("p (j c) -> p j c", j=4)),
                         (self.kk[:, b], core.m_tok[n, :, 0, :].rearrange("p (h c) -> p h c", h=H)),
                         (self.v[:, b, :, 0:DV], core.m_tok[n, :, 1:3, :].rearrange("p x (h c) -> p (x h) c", c=DV))):
            act.dma_start(dst, src).then_inc(self.c_in[b], 16)

    def pe(self, i):
        core, ps = self.core, self.core.ps
        pe = core.nc.tensor
        n, step = divmod(i, self.STEPS)
        b, cols = n % 2, slice(n * P, (n + 1) * P)
        if step == 0:
            if n >= 1:
                pe.wait_ge(self.std, n + 1)
                pe.wait_ge(self.hts, n)
                pe.wait_ge(self.hts2, n)
            pe.transpose(ps[:, 7, 0:P], core.bands[:, cols], core.ident[:]).then_inc(self.xtp, 1)
            pe.wait_ge(self.c_in[b], 96 * (n // 2 + 1))
            for h in range(H):
                last = pe.matmul(ps[:, 4 + h % 2, (h // 2) * P:(h // 2 + 1) * P], self.k[self.rows(h), b, h // 2, :],
                                 self.q[self.rows(h), b, h // 2, :], start=True, stop=True)
            last.then_inc(self.kq, 1)
        elif step == 1:
            if n == 0:
                pe.wait_ge(self.st0, 1)
            pe.wait_ge(self.xts, n + 1)
            for h in range(H):
                bank, at = self.inter_at(h)
                last = pe.matmul(ps[:, bank, at], self.q[self.rows(h), b, h // 2, :], self.st[self.rows(h), h // 2, :],
                                 start=True, stop=True)
            last.then_inc(self.inter, 1)
        elif step == 2:
            pe.wait_ge(self.wqk, 2 * n + 2)
            pe.wait_ge(self.nsc, n + 1)
            for h in range(H):
                bank, at = self.intra_at(h)
                last = pe.matmul(ps[:, bank, at], self.ww[:, self.at(h), :], self.v[:, b, h, :], start=True, stop=True)
            last.then_inc(self.intra, 1)
        elif step == 3:
            pe.wait_ge(self.nsc, n + 1)
            pe.matmul(ps[:, 3, 0:H], core.ident[:, P - 1:P].to_broadcast([P, P]), self.xe[:, 0, :],
                      start=True, stop=True).then_inc(self.dstp, 1)
            pe.wait_ge(self.kwd, n + 1)
            for h in range(H):
                bank, at = self.update_at(h)
                last = pe.matmul(ps[self.rows(h), bank, at], self.kw[:, h, :], self.v[:, b, h, :], start=True, stop=True)
            last.then_inc(self.up, 1)
        else:
            pe.wait_ge(self.hbd, n + 1)
            for h in range(H):
                last = pe.transpose(ps[:, 4 + h // 4, (h % 4) * P:(h % 4 + 1) * P], self.num[:, h, 0:DV], core.ident[:])
            last.then_inc(self.htp, 1)

    def dve_init(self):
        dve = self.core.nc.vector
        dve.memset(self.v[:], 1.0).then_inc(self.one, 1)
        dve.memset(self.st[:], 0.0).then_inc(self.st0, 1)
        dve.memset(self.dec[:], 0.0).then_inc(self.std, 1)

    def dve(self, i):
        core, ps, ch, E = self.core, self.core.ps, self.core.dve, self.E
        dve = core.nc.vector
        n, step = divmod(i, self.STEPS)
        b = n % 2
        quad = lambda a: a.rearrange("p (i c) -> p i c", i=4)
        if step == 0:
            dve.wait_ge(self.xtp, n + 1)
            if n >= 1:
                dve.wait_ge(self.wex, n)
            dve.tensor_copy(self.xt[:], ps[:, 7, 0:P]).then_inc(self.xts, 1)
            dve.wait_ge(self.c_in[b], 96 * (n // 2 + 1))
            if n >= 1:
                dve.wait_ge(self.intra, n)
            mask = core.mask_later[:].unsqueeze(1).to_broadcast([P, 4, P])
            for q in range(2):
                dve.tensor_tensor(self.ww[:, 4 * q:4 * q + 4, :], self.mb[:, b, 4 * q:4 * q + 4, :], mask,
                                  ALU.add).then_inc(self.wm, 1)
            dve.wait_ge(self.xex, n + 1)
            if n >= 1:
                dve.wait_ge(self.up, n)
            dve.tensor_tensor(self.kw[:], self.kk[:, b], bc(self.xe[:, 2, :], [P, H, DH]), ALU.mult).then_inc(self.kwd, 1)
            dve.wait_ge(self.kq, n + 1)
            for q in range(2):
                dve.wait_ge(self.wex, 2 * n + q + 1)
                part = self.ww[:, 4 * q:4 * q + 4, :]
                dve.tensor_tensor(part, part, quad(ps[:, 4 + q, :]), ALU.mult).then_inc(self.wqk, 1)
        elif step == 2:
            dve.wait_ge(self.intra, n + 1)
            dve.wait_ge(self.nsc, n + 1)
            for q, k in ((0, 3), (1, 3), (2, 2)):
                part = self.num[:, 3 * q:3 * q + k, :]
                ins = dve.tensor_tensor(part, part, ps[:, 4 + q, 0:k * E].rearrange("p (i c) -> p i c", i=k), ALU.add)
                if q == 2:
                    ins.then_inc(self.num_set, 1)
                else:
                    ch.mark(ins)
            ch.wait()
            dve.wait_ge(self.num_set, n + 1)
            den, col = self.den[:], self.num[:, :, DV]
            ch.link(dve.scalar_tensor_tensor(den, col, -1.0, col, ALU.mult, ALU.max))
            ch.link(dve.tensor_tensor(den, den, self.xe[:, 1, :], ALU.max))
            ch.link(dve.reciprocal(den, den))
            part = self.num[:, :, 0:DV]
            dve.tensor_tensor(part, part, bc(den, [P, H, DV]), ALU.mult).then_inc(self.hbd, 1)
        elif step == 3:
            dve.wait_ge(self.dstp, n + 1)
            dve.wait_ge(self.up, n + 1)
            dve.wait_ge(self.std, n + 1)
            ch.mark(dve.tensor_copy(self.dec[0:DH, :], ps[0:DH, 3, 0:H:2]))
            ch.link(dve.tensor_copy(self.dec[DH:P, :], ps[DH:P, 3, 1:H:2]))
            for j in range(4):
                bank, at = self.update_at(2 * j)
                ins = dve.scalar_tensor_tensor(self.st[:, j, :], self.st[:, j, :], self.dec[:, j:j + 1],
                                               ps[:, bank, at], ALU.mult, ALU.add)
                if j == 3:
                    ch.wait()
                    ins.then_inc(self.std, 1)
                else:
                    ch.mark(ins)
        elif step == 4:
            dve.wait_ge(self.htp, n + 1)
            if n >= 1:
                dve.wait_ge(self.h_out, 16 * n)
            dve.tensor_copy(self.ht[:, 0:4, :], quad(ps[:, 4, :])).then_inc(self.hts, 1)

    def act(self, i):
        core, ps, ch = self.core, self.core.ps, self.core.act
        act = core.nc.scalar
        n, step = divmod(i, self.STEPS)
        if step == 0:
            act.wait_ge(self.xts, n + 1)
            if n >= 1:
                act.wait_ge(self.dstp, n)
                act.wait_ge(self.hbd, n)
                act.wait_ge(self.kwd, n)
            act.activation(self.xe[:], self.xt[:].rearrange("p (b c) -> p b c", b=4)[:, 1:4, 0:H],
                           ACT.Exp).then_inc(self.xex, 1)
            for h in [0, 2, 4, 6, 1, 3, 5, 7]:
                if h < 2:
                    act.wait_ge(self.wm, 2 * n + h + 1)
                row = self.ww[:, self.at(h), :]
                ins = act.activation(row, row, ACT.Exp, bias=self.xt[:, h:h + 1])
                if h >= 6:
                    ch.wait()
                    ins.then_inc(self.wex, 1)
                else:
                    ch.mark(ins)
        elif step == 1:
            act.wait_ge(self.inter, n + 1)
            act.wait_ge(self.xex, n + 1)
            if n >= 1:
                act.wait_ge(self.htp, n)
            for h in range(H):
                bank, at = self.inter_at(h)
                ins = act.activation(self.num[:, h, :], ps[:, bank, at], ACT.Copy, scale=self.xe[:, 0, h:h + 1])
                if h == H - 1:
                    ch.wait()
                    ins.then_inc(self.nsc, 1)
                else:
                    ch.mark(ins)
        elif step == 3:
            if n + 2 < NT:
                act.wait_ge(self.up, n + 1)
                act.wait_ge(self.wm, 2 * n + 2)
                self.load(n + 2)
        elif step == 4:
            act.wait_ge(self.htp, n + 1)
            if n >= 1:
                act.wait_ge(self.h_out, 16 * n)
            act.activation(self.ht[:, 4:8, :], ps[:, 5, :].rearrange("p (i c) -> p i c", i=4),
                           ACT.Copy).then_inc(self.hts2, 1)
            act.wait_ge(self.hts, n + 1)
            act.wait_ge(self.hts2, n + 1)
            act.dma_start(core.h_mem[:, :, n * P:(n + 1) * P].rearrange("k p t -> p k t"), self.ht[:]).then_inc(self.h_out, 16)

    def act_init(self):
        self.core.nc.scalar.wait_ge(self.one, 1)
        self.load(0)
        self.load(1)

    def store_state(self):
        nc, o, st = self.core.nc, self.core.o, self.st
        act = nc.scalar
        act.wait_ge(self.std, NT + 1)
        dst = o[5][0].rearrange("(j two) d e -> two d j e", two=2)
        dstn = o[6][0].rearrange("(j two) d -> two d j", two=2)
        with nc.allow_non_contiguous_dma(reason="the normaliser's column"):
            for two in range(2):
                rows = slice(DH * two, DH * two + DH)
                act.dma_start(dst[two], st[rows, :, 0:DV]).then_inc(self.c_out, 16)
                act.dma_start(dstn[two], st[rows, :, DV]).then_inc(self.c_out, 16)
        self.core.defer(self.c_out, 64)
        self.core.defer(self.h_out, 16 * NT)


def seg3(ap):
    return ap.rearrange("p (s c) -> p s c", s=3)


class SampleSoftmax:

    C = NB * G * H
    END = 4 + NB

    def __init__(self, core, c):
        self.core = core
        sb, sem = core.sb, core.sem
        self.zs = sb("s_z", [NB, G, 512], ctx=c)
        self.dg = sb("s_dg", [NB, NB, G * H], ctx=c)
        self.vc = sb("s_vc", [P, 2, G, 512], ctx=c)
        self.sa = sb("s_sa", [P, NB, G, H], ctx=c)
        self.nw = sb("s_nw", [P, NB, G, H], ctx=c)
        self.mx = sb("s_mx", [P, NB, H], ctx=c)
        self.ll = sb("s_ll", [P, NB, H], ctx=c)
        self.vt = sb("s_vt", [P, G, 4, NB], ctx=c)
        self.pn = sb("s_pn", [P, G, 4, NB], ctx=c)
        self.rl = sb("s_rl", [P, 4, NB], ctx=c)
        self.ot = sb("s_ot", [P, 4, NB], ctx=c)
        (self.z_in, self.dgd, self.bcp, self.amx, self.sub, self.ex, self.vtp, self.lp, self.pv, self.done,
         self.out) = (sem(f"s_{x}") for x in ("zin", "dg", "bcp", "amx", "sub", "ex", "vtp", "lp", "pv", "done", "out"))
        self.v_in = [sem(f"s_vin{i}") for i in range(2)]
        self.rows_out = core.store_sem("s_rows")

    def load(self, b):
        for g in range(G):
            self.core.nc.scalar.dma_start(self.vc[:, b % 2, g, :], cached_rows(self.core, g, b, 1)).then_inc(
                self.v_in[b % 2], 16)

    def act(self, i):
        core, act, ss, nw = self.core, self.core.nc.scalar, self.core.ss, self.nw
        if i == 0:
            act.dma_start(self.zs[:], core.z_s[:, 2].rearrange("g b c -> b g c")).then_inc(self.z_in, 16)
            self.load(0)
            self.load(1)
            for g in range(G):
                act.dma_start(core.o[8 + g][:, -1 + WINDOWS[g]].rearrange("b a h c -> a b (h c)"),
                              core.z_s[g, 1:3]).then_inc(self.rows_out, 16)
        elif i == 2:
            act.wait_ge(self.sub, 2)
            act.activation(ss[:], ss[:], ACT.Exp, scale=SCALE).then_inc(self.ex, 1)
            act.activation(nw[:], nw[:], ACT.Exp, scale=SCALE).then_inc(self.ex, 1)
        elif 5 <= i and i - 3 < NB:
            act.wait_ge(self.pv, i - 4)
            self.load(i - 3)
        elif i == self.END + 1:
            act.wait_ge(self.done, 1)
            act.dma_start(core.att_t[:, :, S:T].rearrange("k p b -> p k b"), self.ot[:]).then_inc(self.out, 16)

    def act_end(self):
        self.core.nc.scalar.wait_ge(self.out, 16)
        self.core.nc.scalar.wait_ge(self.rows_out, 16 * G)

    def pool(self):
        flat = lambda a: a[:].rearrange("p b g h -> p (b g h)")
        self.core.nc.gpsimd.partition_all_reduce(flat(self.sa), flat(self.core.ss), P,
                                                 bass.bass_isa.ReduceOp.max).then_inc(self.amx, 1)

    def dve(self, i):
        core, ch, ps, C = self.core, self.core.dve, self.core.ps, self.C
        dve, ident, ss, sa, nw, mx, ll, vt = core.nc.vector, core.ident, core.ss, self.sa, self.nw, self.mx, self.ll, self.vt
        flat = lambda a: a[:].rearrange("p b g h -> p (b g h)")
        if i == 0:
            sn = core.sn[:].rearrange("b g h -> b (g h)")
            dve.tensor_tensor(self.dg[:], sn.unsqueeze(1).to_broadcast([NB, NB, G * H]),
                              bc(ident[0:NB, 0:NB], [NB, NB, G * H]), ALU.mult).then_inc(self.dgd, 1)
        elif i == 1:
            dve.wait_ge(self.bcp, 1)
            ch.link(dve.tensor_copy(flat(nw), ps[:, 4, 0:C]))
            dve.wait_ge(self.amx, 1)
            ch.link(dve.tensor_tensor(sa[:], sa[:], nw[:], ALU.max))
            ch.link(dve.tensor_reduce(mx[:], sa[:].rearrange("p b g h -> p b h g"), AX.X, ALU.max))
            m4 = mx[:].unsqueeze(2).to_broadcast([P, NB, G, H])
            dve.tensor_tensor(ss[:], ss[:], m4, ALU.subtract).then_inc(self.sub, 1)
            dve.tensor_tensor(nw[:], nw[:], m4, ALU.subtract).then_inc(self.sub, 1)
            dve.wait_ge(self.vtp, 1)
            ch.mark(dve.tensor_copy(vt[:].rearrange("p g j b -> p (g j b)"), ps[:, 5, 0:G * 4 * NB]))
        elif i == 4:
            dve.wait_ge(self.ex, 2)
            dve.wait_ge(self.lp, 1)
            ch.link(dve.tensor_tensor(flat(sa), ps[:, 6, 0:C], flat(nw), ALU.add))
            ch.link(dve.tensor_reduce(ll[:], sa[:].rearrange("p b g h -> p b h g"), AX.X, ALU.add))
            ch.link(dve.reciprocal(ll[:], ll[:]))
            for two in range(2):
                rows = slice(DH * two, DH * two + DH)
                for g in range(G):
                    ch.mark(dve.tensor_copy(self.pn[rows, g], nw[rows, :, g, two::2].rearrange("p b j -> p j b")))
                ch.mark(dve.tensor_copy(self.rl[rows], ll[rows, :, two::2].rearrange("p b j -> p j b")))
            ch.wait()
            ch.link(dve.tensor_tensor(vt[:], vt[:], self.pn[:], ALU.mult))
            ch.link(dve.tensor_tensor(vt[:, 0], vt[:, 0], vt[:, 1], ALU.add))
            ch.link(dve.tensor_tensor(vt[:, 0], vt[:, 0], vt[:, 2], ALU.add))
        elif i == self.END:
            ot = self.ot
            dve.wait_ge(self.pv, NB)
            for two in range(2):
                rows = slice(DH * two, DH * two + DH)
                src = ps[rows, 7, 0:NB * H].rearrange("p (b j two) -> p two j b", two=2, j=4)[:, two]
                ch.mark(dve.tensor_tensor(ot[rows], vt[rows, 0], src, ALU.add))
            ch.wait()
            dve.tensor_tensor(ot[:], ot[:], self.rl[:], ALU.mult).then_inc(self.done, 1)

    def pe(self, i):
        core, ps, ident, C = self.core, self.core.ps, self.core.ident, self.C
        pe, ss = core.nc.tensor, core.ss
        if i == 0:
            pe.wait_ge(self.dgd, 1)
            pe.matmul(ps[:, 4, 0:C], core.ones[0:NB, :], self.dg[:].rearrange("a b c -> a (b c)"),
                      start=True, stop=True).then_inc(self.bcp, 1)
            pe.wait_ge(self.z_in, 16)
            for g in range(G):
                for j in range(4):
                    at = (4 * g + j) * NB
                    last = pe.transpose(ps[:, 5, at:at + NB], self.zs[:, g, j * P:(j + 1) * P], ident[0:NB, 0:NB])
            last.then_inc(self.vtp, 1)
        elif i == 3:
            pe.wait_ge(self.ex, 2)
            pe.matmul(ps[:, 6, 0:C], core.ones[:], ss[:].rearrange("p b g h -> p (b g h)"),
                      start=True, stop=True).then_inc(self.lp, 1)
        elif 4 <= i and i - 4 < NB:
            b = i - 4
            pe.wait_ge(self.v_in[b % 2], 48 * (b // 2 + 1))
            for j in range(4):
                for g in range(G):
                    at = (b * 4 + j) * 2
                    last = pe.matmul(ps[:, 7, at:at + 2], self.vc[:, b % 2, g, j * P:(j + 1) * P],
                                     ss[:, b, g, 2 * j:2 * j + 2], start=(g == 0), stop=(g == G - 1))
            last.then_inc(self.pv, 1)


class SampleMlstm:

    def __init__(self, core, c):
        self.core = core
        sb, sem = core.sb, core.sem
        self.z = sb("r_z", [NB, 2048], ctx=c)
        self.nn = sb("r_n", [NB, 512], ctx=c)
        self.gt = sb("r_g", [NB, 3, H], ctx=c)
        self.tmp = sb("r_t", [NB, 512], ctx=c)
        self.kw = sb("r_kw", [NB, 512], ctx=c)
        self.km = sb("r_km", [NB, NB, 512], ctx=c)
        self.mt = sb("r_m", [NB, H], ctx=c)
        self.e3 = sb("r_e", [NB, 3, H], ctx=c)
        self.qk = sb("r_qk", [NB, H], ctx=c)
        self.qn = sb("r_qn", [NB, H], ctx=c)
        self.co = sb("r_co", [NB, 3, H], ctx=c)
        self.dg = sb("r_dg", [NB, NB, 3, H], ctx=c)
        self.cb = sb("r_cb", [P, NB, 3, H], ctx=c)
        self.d2 = sb("r_d2", [P, NB, 4], ctx=c)
        self.qd = sb("r_qd", [P, NB, 4, 2], ctx=c)
        self.vt = sb("r_vt", [P, H, NB], ctx=c)
        self.ht = sb("r_ht", [P, H, NB], ctx=c)
        self.om = sb("r_om", [P, H, NB], ctx=c)
        self.st = sb("r_c", [P, NB, 4, DV], ctx=c)
        (self.z_in, self.g_in, self.s_in, self.tr, self.qdd, self.gsub, self.gexp, self.dgd, self.cbp, self.kmd,
         self.up, self.std, self.hq, self.hd, self.nd, self.md) = (sem(f"r_{x}") for x in
            ("zin", "gin", "sin", "tr", "qd", "gsub", "gexp", "dg", "cbp", "km", "up", "st", "hq", "h", "nd", "md"))
        self.out, self.h_out = core.store_sem("r_out"), sem("r_hout")
        self.halves = [slice(0, DH), slice(DH, P)]

    def rows(self, u):
        return range(2 * (u - 4), 2 * (u - 4) + 2) if 4 <= u < 4 + NB // 2 else range(0)

    def load(self):
        core, t = self.core, self.core.t
        sp, gt = core.nc.sync, self.gt
        sp.dma_start(self.z[:], core.zm_s).then_inc(self.z_in, 16)
        with core.nc.allow_non_contiguous_dma(reason="64 gates"):
            sp.dma_start(gt[:, 0, :], core.if_s[0].rearrange("h b -> b h")).then_inc(self.g_in, 16)
            sp.dma_start(gt[:, 1, :], core.if_s[1].rearrange("h b -> b h")).then_inc(self.g_in, 16)
            sp.dma_start(self.om[:], core.om_s.rearrange("k p b -> p k b")).then_inc(self.g_in, 16)
        sp.dma_start(gt[:, 2, :], t["state_mlstm_m"]).then_inc(self.g_in, 16)
        sp.dma_start(self.nn[:], t["state_mlstm_n"].rearrange("b h d -> b (h d)")).then_inc(self.g_in, 16)
        for b in range(NB):
            sp.dma_start(self.st[:, b], t["state_mlstm_C"][b].rearrange("(j two) d e -> (two d) j e", two=2)).then_inc(
                self.s_in, 16)

    def pe_first(self):
        pe, ps, z, ident = self.core.nc.tensor, self.core.ps, self.z, self.core.ident
        pe.wait_ge(self.z_in, 16)
        for j in range(4):
            pe.transpose(ps[:, 6, j * NB:(j + 1) * NB], z[:, j * P:(j + 1) * P], ident[0:NB, 0:NB])
        for h in range(H):
            last = pe.transpose(ps[:, 6, (4 + h) * NB:(5 + h) * NB], z[:, 1024 + h * P:1024 + (h + 1) * P],
                                ident[0:NB, 0:NB])
        last.then_inc(self.tr, 1)

    def pe(self, u):
        pe, ps, core = self.core.nc.tensor, self.core.ps, self.core
        if u == 3:
            pe.wait_ge(self.qdd, 2)
            pe.wait_ge(self.s_in, 16 * NB)
            for b in range(NB):
                for j in range(4):
                    at = (b * 4 + j) * 2
                    last = pe.matmul(ps[:, 7, at:at + 2], self.st[:, b, j, :], self.qd[:, b, j, :], start=True, stop=True)
            last.then_inc(self.hq, 1)
            pe.wait_ge(self.dgd, 1)
            pe.matmul(ps[:, 7, 64:64 + NB * 3 * H], core.ones[0:NB, :], self.dg[:].rearrange("a b x h -> a (b x h)"),
                      start=True, stop=True).then_inc(self.cbp, 1)
        for b in self.rows(u):
            if b == 0:
                pe.wait_ge(self.kmd, 1)
                pe.wait_ge(self.hd, 1)
            if b >= 2:
                pe.wait_ge(self.std, 4 * b - 4)
            for h in range(H):
                last = pe.matmul(ps[self.halves[h % 2], 6 + b % 2, (h // 2) * DV:(h // 2 + 1) * DV],
                                 self.km[:, b, h * DH:(h + 1) * DH], self.z[:, 1024 + h * DV:1024 + (h + 1) * DV],
                                 start=True, stop=True)
            last.then_inc(self.up, 1)

    def act_first(self):
        act = self.core.nc.scalar
        act.wait_ge(self.gsub, 3)
        act.activation(self.e3[:], self.e3[:], ACT.Exp).then_inc(self.gexp, 1)

    def act(self, u):
        act, core, o = self.core.nc.scalar, self.core, self.core.o
        if u == 4:
            act.wait_ge(self.md, 1)
            act.dma_start(o[13], self.mt[:]).then_inc(self.out, 16)
            act.wait_ge(self.nd, 1)
            act.dma_start(o[12].rearrange("b h d -> b (h d)"), self.nn[:]).then_inc(self.out, 16)
            act.wait_ge(self.hd, 1)
            act.dma_start(core.hm_t[:, :, S:T].rearrange("k p b -> p k b"), self.ht[:]).then_inc(self.h_out, 16)
        for b in self.rows(u):
            act.wait_ge(self.std, 4 * b + 4)
            act.dma_start(o[11][b].rearrange("(j two) d e -> (two d) j e", two=2), self.st[:, b]).then_inc(self.out, 16)

    def act_end(self):
        self.core.nc.scalar.wait_ge(self.h_out, 16)
        self.core.defer(self.out, 16 * (2 + NB))

    def dve_first(self):
        core, ch, ps, halves = self.core, self.core.dve, self.core.ps, self.halves
        dve, z, nn, gt, tmp, mt, e3, qk, qn = (core.nc.vector, self.z, self.nn, self.gt, self.tmp, self.mt, self.e3,
                                               self.qk, self.qn)
        h3 = lambda a: a.rearrange("b (h c) -> b h c", h=H)
        ch.mark(dve.memset(self.qd[:], 0.0))
        dve.wait_ge(self.g_in, 80)
        ch.link(dve.tensor_tensor(gt[:, 1, :], gt[:, 1, :], gt[:, 2, :], ALU.add))
        dve.tensor_tensor(mt[:], gt[:, 0, :], gt[:, 1, :], ALU.max).then_inc(self.md, 1)
        dve.wait_ge(self.md, 1)
        dve.tensor_tensor(e3[:, 0, :], gt[:, 1, :], mt[:], ALU.subtract).then_inc(self.gsub, 1)
        dve.tensor_tensor(e3[:, 1, :], gt[:, 0, :], mt[:], ALU.subtract).then_inc(self.gsub, 1)
        dve.tensor_scalar(e3[:, 2, :], mt[:], -1.0, None, ALU.mult).then_inc(self.gsub, 1)
        dve.wait_ge(self.z_in, 16)
        ch.link(dve.tensor_tensor(tmp[:], z[:, 0:512], z[:, 512:1024], ALU.mult))
        ch.link(dve.tensor_reduce(qk[:], h3(tmp[:]), AX.X, ALU.add))
        ch.link(dve.tensor_tensor(tmp[:], z[:, 0:512], nn[:], ALU.mult))
        ch.link(dve.tensor_reduce(qn[:], h3(tmp[:]), AX.X, ALU.add))
        dve.wait_ge(self.tr, 1)
        q4 = ps[:, 6, 0:4 * NB].rearrange("p (j b) -> p b j", j=4)
        dve.tensor_copy(self.qd[halves[0], :, :, 0], q4[halves[0]]).then_inc(self.qdd, 1)
        dve.tensor_copy(self.qd[halves[1], :, :, 1], q4[halves[1]]).then_inc(self.qdd, 1)
        ch.link(dve.tensor_copy(self.vt[:].rearrange("p h b -> p (h b)"), ps[:, 6, 4 * NB:12 * NB]))

    def dve_second(self):
        core, ch, ident = self.core, self.core.dve, self.core.ident
        dve, z, nn, kw, e3, qk, qn, co = (core.nc.vector, self.z, self.nn, self.kw, self.e3, self.qk, self.qn, self.co)
        h3 = lambda a: a.rearrange("b (h c) -> b h c", h=H)
        dve.wait_ge(self.gexp, 1)
        ch.link(dve.tensor_tensor(qk[:], qk[:], e3[:, 1, :], ALU.mult))
        ch.link(dve.tensor_tensor(qn[:], qn[:], e3[:, 0, :], ALU.mult))
        ch.link(dve.tensor_tensor(qn[:], qn[:], qk[:], ALU.add))
        ch.link(dve.scalar_tensor_tensor(qn[:], qn[:], -1.0, qn[:], ALU.mult, ALU.max))
        ch.link(dve.tensor_tensor(qn[:], qn[:], e3[:, 2, :], ALU.max))
        ch.link(dve.reciprocal(qn[:], qn[:]))
        ch.mark(dve.tensor_copy(co[:, 0, :], e3[:, 0, :]))
        ch.mark(dve.tensor_tensor(co[:, 1, :], e3[:, 0, :], qn[:], ALU.mult))
        ch.link(dve.tensor_tensor(co[:, 2, :], qk[:], qn[:], ALU.mult))
        dve.tensor_tensor(self.dg[:].rearrange("a b x h -> a b (x h)"),
                          co[:].rearrange("a x h -> a (x h)").unsqueeze(1).to_broadcast([NB, NB, 3 * H]),
                          bc(ident[0:NB, 0:NB], [NB, NB, 3 * H]), ALU.mult).then_inc(self.dgd, 1)
        ch.link(dve.tensor_tensor(h3(kw[:]), h3(z[:, 512:1024]), bc(e3[:, 1, :], [NB, H, DH]), ALU.mult))
        dve.tensor_tensor(self.km[:], kw[:].unsqueeze(1).to_broadcast([NB, NB, 512]),
                          bc(ident[0:NB, 0:NB], [NB, NB, 512]), ALU.mult).then_inc(self.kmd, 1)
        ch.link(dve.tensor_tensor(h3(nn[:]), h3(nn[:]), bc(e3[:, 0, :], [NB, H, DH]), ALU.mult))
        dve.tensor_tensor(nn[:], nn[:], kw[:], ALU.add).then_inc(self.nd, 1)

    def dve(self, u):
        core, ch, ps, halves = self.core, self.core.dve, self.core.ps, self.halves
        dve, cb, d2, ht, vt, st = core.nc.vector, self.cb, self.d2, self.ht, self.vt, self.st
        if u == 1:
            self.dve_first()
        elif u == 2:
            self.dve_second()
        elif u == 3:
            dve.wait_ge(self.cbp, 1)
            ch.link(dve.tensor_copy(cb[:].rearrange("p b x h -> p (b x h)"), ps[:, 7, 64:64 + NB * 3 * H]))
            ch.mark(dve.tensor_copy(d2[halves[0]], cb[halves[0], :, 0, 0::2]))
            ch.mark(dve.tensor_copy(d2[halves[1]], cb[halves[1], :, 0, 1::2]))
            dve.wait_ge(self.hq, 1)
            ch.mark(dve.tensor_tensor(ht[:], cb[:, :, 1, :].rearrange("p b h -> p h b"),
                                      ps[:, 7, 0:NB * H].rearrange("p (b h) -> p h b", b=NB), ALU.mult))
            ch.link(dve.tensor_tensor(vt[:], vt[:], cb[:, :, 2, :].rearrange("p b h -> p h b"), ALU.mult))
            ch.link(dve.tensor_tensor(ht[:], ht[:], vt[:], ALU.add))
            dve.tensor_tensor(ht[:], ht[:], self.om[:], ALU.mult).then_inc(self.hd, 1)
        for b in self.rows(u):
            dve.wait_ge(self.up, b + 1)
            for j in range(4):
                dve.scalar_tensor_tensor(st[:, b, j, :], st[:, b, j, :], d2[:, b, j:j + 1],
                                         ps[:, 6 + b % 2, j * DV:(j + 1) * DV], ALU.mult,
                                         ALU.add).then_inc(self.std, 1)


def project_across(core, nk, p0, cols, rhs, bank, release, waits=()):
    nc, ps = core.nc, core.ps
    hi, lo = rhs
    m = cols.stop - cols.start
    for k in range(nk):
        for sem, value in waits:
            nc.tensor.wait_ge(sem, value + k)
        w_hi, w_lo = core.weight(p0 + k, cols)
        for i, (w, x) in enumerate(((w_hi, hi), (w_hi, lo), (w_lo, hi))):
            for s in range(3):
                last = nc.tensor.matmul(ps[0:m, bank + s, 0:SEG], w, x[:, k, s * SEG:(s + 1) * SEG],
                                        start=(k == 0 and i == 0), stop=(k == nk - 1 and i == 2))
        if release:
            last.then_inc(core.w_used, 1)
    return last


class Groups:

    def __init__(self, core, name, groups, nk):
        self.core, self.nk, self.per, self.n = core, nk, CW // P, groups * (CW // P)
        self.p0 = core.taken
        core.taken += groups * nk
        self.mm = core.sem(name)

    def product(self, pe, u, rhs, ready):
        g, m = divmod(u, self.per)
        waits = [(self.core.w_lo, self.p0 + g * self.nk + 1)] if m == 0 else []
        if u == 0:
            waits.append((ready, 1))
        end = m == self.per - 1
        last = project_across(self.core, self.nk, self.p0 + g * self.nk, slice(m * P, (m + 1) * P), rhs,
                              3 * (u % 2), end, waits)
        if not end:
            last.then_inc(self.mm, 1)

    def wait(self, eng, u):
        if u % self.per == self.per - 1:
            eng.wait_ge(self.core.w_used, self.p0 + (u // self.per + 1) * self.nk)
        else:
            eng.wait_ge(self.mm, u + 1 - (u + 1) // self.per)


def banks(core, u):
    return core.ps[:, 3 * (u % 2):3 * (u % 2) + 3, 0:SEG]


def segment_product(core, i, p0, ev, mm):
    nc, pe, ps = core.nc, core.nc.tensor, core.ps
    u, s = divmod(i, 3)
    g, m = divmod(u, 4)
    if i >= 2:
        pe.wait_ge(ev, i - 1)
    seg = slice(s * SEG, (s + 1) * SEG)
    frees = m == 3 and s == 2
    for k in range(KD):
        if m == 0 and s == 0:
            pe.wait_ge(core.w_lo, p0 + g * KD + k + 1)
        last = products(nc, ps[:, i % 2, 0:SEG], core.weight(p0 + g * KD + k, slice(m * P, (m + 1) * P)),
                        (core.hhi[:, k, seg], core.hlo[:, k, seg]), k == 0, k == KD - 1)
        if frees:
            last.then_inc(core.w_used, 1)
    if not frees:
        last.then_inc(mm, 1)


def wait_segment(core, eng, i, p0, mm):
    if i % 12 == 11:
        eng.wait_ge(core.w_used, p0 + (i // 12 + 1) * KD)
    else:
        eng.wait_ge(mm, i + 1 - (i + 1) // 12)


def gate_projections(core):
    sem, sb, ps = core.sem, core.sb, core.ps
    U = 2 * KD
    PER = 6
    p0 = core.taken
    core.taken += 4 * KD
    with ExitStack() as c:
        chunks = Chunks(core, c)
        sg = sb("e_sg", [P, 2, T], ctx=c)
        mm, ev = sem("e_mm"), sem("e_ev")
        out = [sem(f"e_out{i}") for i in range(2)]
        block = c.enter_context(core.nc.Block())

        def step(i):
            n, r = divmod(i - 1, PER)
            if n == NT - 1:
                return n * chunks.STEPS + r if r < chunks.STEPS else None
            return None if r == 1 or n < 0 else n * chunks.STEPS + max(r - 1, 0)

        @block.sync
        def _(sp):
            core.load_weights(core.taken + 8)

        @block.gpsimd
        def _(pool):
            core.split_weights(core.taken + 8)

        @block.tensor
        def _(pe):
            for i in range(3 * U):
                segment_product(core, i, p0, ev, mm)
                if step(i) is not None:
                    chunks.pe(step(i))

        @block.scalar
        def _(act):
            core.settle(act)
            chunks.act_init()
            for i in range(3 * U):
                u, s = divmod(i, 3)
                if s == 0 and u >= 2:
                    act.wait_ge(out[u % 2], 16 * (u // 2))
                wait_segment(core, act, i, p0, mm)
                act.activation(sg[:, u % 2, s * SEG:(s + 1) * SEG], ps[:, i % 2, 0:SEG], ACT.Sigmoid).then_inc(ev, 1)
                if s == 2:
                    act.wait_ge(ev, i + 1)
                    act.dma_start(core.gates[u], sg[:, u % 2, :]).then_inc(out[u % 2], 16)
                if step(i) is not None:
                    chunks.act(step(i))
            chunks.store_state()
            for i in range(2):
                core.defer(out[i], 16 * U // 2)

        @block.vector
        def _(dve):
            chunks.dve_init()
            for i in range(3 * U):
                if step(i) is not None:
                    chunks.dve(step(i))


def output_gates(core):
    sem, sb, ps = core.sem, core.sb, core.ps
    p0 = core.taken
    core.taken += 2 * KD
    with ExitStack() as c:
        parts = [GroupMerge(core, c), SampleSoftmax(core, c)]
        sg = sb("v_sg", [P, 3, SEG], ctx=c)
        hm = sb("v_hm", [P, 2, S], ctx=c)
        mm, ev, mul, om_out = sem("v_mm"), sem("v_ev"), sem("v_mul"), sem("v_omout")
        h_in = [sem(f"v_hin{i}") for i in range(2)]
        out = [sem(f"v_out{i}") for i in range(2)]
        block = c.enter_context(core.nc.Block())

        def load_h(u):
            core.nc.scalar.dma_start(hm[:, u % 2, :], core.h_mem[u, :, 0:S]).then_inc(h_in[u % 2], 16)

        @block.sync
        def _(sp):
            core.load_weights(core.taken + 8)

        @block.gpsimd
        def _(pool):
            parts[1].pool()
            core.split_weights(core.taken + 8)

        @block.tensor
        def _(pe):
            for i in range(3 * KD):
                segment_product(core, i, p0, ev, mm)
                for part in parts:
                    part.pe(i)

        @block.scalar
        def _(act):
            core.settle(act)
            load_h(0)
            for i in range(3 * KD):
                u, s = divmod(i, 3)
                for part in parts:
                    part.act(i)
                if s == 1 and u + 1 < KD:
                    if u >= 1:
                        act.wait_ge(out[(u + 1) % 2], 16 * ((u + 1) // 2))
                    load_h(u + 1)
                wait_segment(core, act, i, p0, mm)
                if i >= 3:
                    act.wait_ge(mul, i - 2)
                if s == 2 and u >= 1:
                    act.wait_ge(om_out, 16 * u)
                act.activation(sg[:, s, :], ps[:, i % 2, 0:SEG], ACT.Sigmoid).then_inc(ev, 1)
                if s == 2:
                    act.wait_ge(ev, i + 1)
                    act.dma_start(core.om_s[u], sg[:, 2, SEG - NB:SEG]).then_inc(om_out, 16)
                    act.wait_ge(mul, i + 1)
                    act.dma_start(core.hm_t[u, :, 0:S], hm[:, u % 2, :]).then_inc(out[u % 2], 16)
            for part in parts:
                part.act_end()
            core.defer(om_out, 16 * KD)
            for i in range(2):
                core.defer(out[i], 16 * KD // 2)

        @block.vector
        def _(dve):
            for i in range(3 * KD):
                u, s = divmod(i, 3)
                for part in parts:
                    part.dve(i)
                cols = slice(s * SEG, min((s + 1) * SEG, S))
                dve.wait_ge(ev, i + 1)
                dve.wait_ge(h_in[u % 2], 16 * (u // 2 + 1))
                dve.tensor_tensor(hm[:, u % 2, cols], hm[:, u % 2, cols], sg[:, s, 0:cols.stop - cols.start],
                                  ALU.mult).then_inc(mul, 1)


def merge_product(core, tag, src, nk, gate0):
    nc, sem, sb, acc = core.nc, core.sem, core.sb, core.acc
    R = 4
    with ExitStack() as c:
        hi = sb(f"{tag}_hi", [P, nk, T], F32R, c)
        lo = sb(f"{tag}_lo", [P, nk, T], F32R, c)
        rw = sb(f"{tag}_rw", [P, R, T], ctx=c)
        units = Groups(core, f"{tag}_mm", 2, nk)
        his, los, ev, add = sem(f"{tag}_his"), sem(f"{tag}_los"), sem(f"{tag}_ev"), sem(f"{tag}_add")
        r_in = [sem(f"{tag}_in{i}") for i in range(R)]
        sample = SampleMlstm(core, c) if gate0 == 0 else None
        block = c.enter_context(nc.Block())

        @block.sync
        def _(sp):
            for k in range(nk):
                if k >= R:
                    sp.wait_ge(los, k - R + 1)
                sp.dma_start(rw[:, k % R, :], src[k]).then_inc(r_in[k % R], 16)
            if sample:
                core.settle(sp)
                sample.load()
            core.load_weights(core.taken + 8)

        @block.gpsimd
        def _(pool):
            core.split_weights(core.taken + 8)

        @block.scalar
        def _(act):
            def load_gate(u):
                act.dma_start(rw[:, u % R, :], core.gates[gate0 + u]).then_inc(r_in[u % R], 16)

            for k in range(nk):
                act.wait_ge(r_in[k % R], 16 * (k // R + 1))
                nc.scalar.activation(hi[:, k, :], rw[:, k % R, :], ACT.Copy).then_inc(his, 1)
            for u in range(R):
                act.wait_ge(los, nk - R + u + 1)
                load_gate(u)
            if sample:
                sample.act_first()
            for u in range(KD):
                act.wait_ge(ev, u + 1)
                if u + R < KD:
                    load_gate(u + R)
                if sample:
                    sample.act(u)
            if sample:
                sample.act_end()
            else:
                core.settle(act)

        @block.vector
        def _(dve):
            for k in range(nk):
                dve.wait_ge(his, k + 1)
                nc.vector.tensor_tensor(lo[:, k, :], rw[:, k % R, :], hi[:, k, :].bitcast(F32),
                                        ALU.subtract).then_inc(los, 1)
            for u in range(KD):
                units.wait(dve, u)
                dve.wait_ge(r_in[u % R], 16 * (nk // R + u // R + 1))
                if gate0 == 0:
                    nc.vector.tensor_tensor(seg3(acc[:, u, :]), banks(core, u), seg3(rw[:, u % R, :]),
                                            ALU.mult).then_inc(ev, 1)
                else:
                    nc.vector.tensor_tensor(seg3(rw[:, u % R, :]), banks(core, u), seg3(rw[:, u % R, :]),
                                            ALU.mult).then_inc(add, 1)
                    dve.wait_ge(add, u + 1)
                    nc.vector.tensor_tensor(acc[:, u, :], acc[:, u, :], rw[:, u % R, :], ALU.add).then_inc(ev, 1)
                if sample:
                    sample.dve(u)

        @block.tensor
        def _(pe):
            for u in range(KD):
                if u >= 2:
                    pe.wait_ge(ev, u - 1)
                units.product(pe, u, (hi, lo), los)
                if sample and u == 0:
                    sample.pe_first()
                if sample:
                    sample.pe(u)


def output_projection(core):
    nc, t, sem, sb, acc, ident, ps = core.nc, core.t, core.sem, core.sb, core.acc, core.ident, core.ps
    with ExitStack() as c:
        hi = sb("o_hi", [P, KD, T], F32R, c)
        lo = sb("o_lo", [P, KD, T], F32R, c)
        xr = sb("o_x", [P, 4, 512], ctx=c)
        sq = sb("o_sq", [P, T], ctx=c)
        units = Groups(core, "o_mm", 2, KD)
        his, los, tr, xt, ev, sqd, sum_sq = (sem(f"o_{x}") for x in ("his", "los", "tr", "xt", "ev", "sq", "sum"))
        x_in = [sem(f"o_xin{i}") for i in range(4)]
        g_in = core.store_sem("o_gin")
        block = c.enter_context(nc.Block())
        HALF = NT + 1

        @block.sync
        def _(sp):
            with nc.allow_non_contiguous_dma(reason="1024 gains"):
                sp.dma_start(core.g2[:], t["norm2_g"].rearrange("(k p) -> p k", p=P)).then_inc(g_in, 16)
            for v in range(2 * HALF):
                kk, n = divmod(v, HALF)
                cols = slice(512 * kk, 512 * kk + 512)
                if v >= 4:
                    sp.wait_ge(tr, v - 3)
                if n < NT:
                    sp.dma_start(xr[:, v % 4, :], t["x_prompt"][0, n * P:(n + 1) * P, cols]).then_inc(x_in[v % 4], 16)
                else:
                    sp.dma_start(xr[0:NB, v % 4, :], t["x_sample"].rearrange("b s d -> (b s) d")[:, cols]).then_inc(
                        x_in[v % 4], 16)
            core.load_weights(core.taken + 8)
            sp.wait_ge(g_in, 16)

        @block.gpsimd
        def _(pool):
            core.split_weights(core.taken + 8)

        @block.scalar
        def _(act):
            for k in range(KD):
                nc.scalar.activation(hi[:, k, :], acc[:, k, :], ACT.Copy).then_inc(his, 1)
            act.wait_ge(los, KD)
            for v in range(2 * HALF):
                kk, n = divmod(v, HALF)
                cols = P if n < NT else NB
                act.wait_ge(tr, v + 1)
                nc.scalar.activation(acc[:, 4 * kk:4 * kk + 4, n * P:n * P + cols],
                                     ps[:, 6 + v % 2, :].rearrange("p (k c) -> p k c", k=4)[:, :, 0:cols],
                                     ACT.Copy).then_inc(xt, 1)
            for u in range(KD):
                act.wait_ge(ev, u + 1)
                if u >= 2:
                    act.wait_ge(sum_sq, u - 1)
                nc.scalar.activation(sq[:] if u else core.ssq[:], acc[:, u, :], ACT.Square).then_inc(sqd, 1)

        @block.vector
        def _(dve):
            def add_squares(u):
                dve.wait_ge(sqd, u + 1)
                if u >= 2:
                    dve.wait_ge(sum_sq, u - 1)
                nc.vector.tensor_tensor(core.ssq[:], core.ssq[:], sq[:], ALU.add).then_inc(sum_sq, 1)

            for k in range(KD):
                dve.wait_ge(his, k + 1)
                nc.vector.tensor_tensor(lo[:, k, :], acc[:, k, :], hi[:, k, :].bitcast(F32), ALU.subtract).then_inc(los, 1)
            for u in range(KD):
                units.wait(dve, u)
                dve.wait_ge(xt, HALF if u < 4 else 2 * HALF)
                nc.vector.tensor_tensor(seg3(acc[:, u, :]), seg3(acc[:, u, :]), banks(core, u), ALU.add).then_inc(ev, 1)
                if u >= 2:
                    add_squares(u - 1)
            add_squares(KD - 1)

        @block.tensor
        def _(pe):
            for u in range(KD):
                if u >= 2:
                    pe.wait_ge(ev, u - 1)
                units.product(pe, u, (hi, lo), los)
                for v in range(u * HALF, (u + 1) * HALF) if u < 2 else ():
                    n = v % HALF
                    rows = P if n < NT else NB
                    pe.wait_ge(x_in[v % 4], 16 * (v // 4 + 1))
                    if v >= 2:
                        pe.wait_ge(xt, v - 1)
                    for k in range(4):
                        last = nc.tensor.transpose(ps[:, 6 + v % 2, k * P:k * P + rows],
                                                   xr[0:rows, v % 4, k * P:(k + 1) * P], ident[0:rows, 0:rows])
                    last.then_inc(tr, 1)


def ffn(core):
    nc, sem, sb, acc, ps = core.nc, core.sem, core.sb, core.acc, core.ps
    hi, lo, rs = core.h2hi, core.h2lo, core.ssq
    J = DFF // 256
    p0 = core.taken
    core.taken += J * (KD + 4)
    with ExitStack() as c:
        sg = sb("ff_sg", [P, T], ctx=c)
        fh = sb("ff_hi", [P, 2, 2, T], F32R, c)
        fl = sb("ff_lo", [P, 2, 2, T], F32R, c)
        mm, scl, sil, mul, his, los, add = (sem(f"ff_{x}") for x in ("mm", "scl", "sil", "mul", "hi", "lo", "add"))
        nhi, nlo, tot, var, std = (sem(f"ff_n{x}") for x in ("hi", "lo", "tot", "var", "std"))
        block = c.enter_context(nc.Block())

        def first(j):
            return p0 + j * (KD + 4) - (4 if j else 0)

        def first_down(j):
            return first(j + 1) + KD if j < J - 1 else p0 + J * (KD + 4) - 4

        order = []
        for j in range(J + 1):
            if j < J:
                order += [("gu", j, m) for m in range(4)]
            if j >= 1:
                order += [("dn", j - 1, m) for m in range(KD)]
        index = {x: i for i, x in enumerate(order)}
        ends = {}
        n = 0
        for i, (kind, j, m) in enumerate(order):
            frees = (kind == "gu" and m == 3) or (kind == "dn" and m in (3, 7))
            if not frees:
                n += 1
            ends[i] = (frees, n)

        def complete(eng, x):
            kind, j, m = x
            frees, count = ends[index[x]]
            if not frees:
                eng.wait_ge(mm, count)
            elif kind == "gu":
                eng.wait_ge(core.w_used, first(j) + KD)
            else:
                eng.wait_ge(core.w_used, first_down(j) + (2 if m == 3 else 4))

        def taken(eng, i):
            kind, j, m = order[i]
            if kind == "dn":
                eng.wait_ge(add, KD * j + m + 1)
            elif m % 2 == 0:
                eng.wait_ge(scl, 2 * j + m // 2 + 1)
            else:
                eng.wait_ge(mul, 2 * j + m // 2 + 1)

        def res(i):
            return ps[:, 3 * (i % 2):3 * (i % 2) + 3, 0:SEG]

        @block.sync
        def _(sp):
            core.load_weights(core.taken + 8)

        @block.gpsimd
        def _(pool):
            core.split_weights(core.taken + 8)

        @block.tensor
        def _(pe):
            for s in range(3):
                last = nc.tensor.matmul(ps[:, 3 + s, 0:SEG], core.ones[:], rs[:, s * SEG:(s + 1) * SEG],
                                        start=True, stop=True)
            last.then_inc(tot, 1)
            for i, (kind, j, m) in enumerate(order):
                if i == 1:
                    pe.wait_ge(var, 1)
                if i >= 2:
                    taken(pe, i - 2)
                frees = ends[i][0]
                if kind == "gu":
                    waits = [(core.w_lo, first(j) + 1)] if m == 0 else []
                    if i == 0:
                        waits.append((nlo, 1))
                    tile, up = divmod(m, 2)
                    at = 256 * up + P * tile
                    last = project_across(core, KD, first(j), slice(at, at + P), (hi, lo), 3 * (i % 2), frees, waits)
                else:
                    p = first_down(j) + (0 if m < 4 else 2)
                    waits = [(core.w_lo, p + 1)] if m % 4 == 0 else []
                    if m == 0:
                        waits.append((los, 2 * j + 1))
                    last = project_across(core, 2, p, slice(P * (m % 4), P * (m % 4) + P),
                                          (fh[:, j % 2], fl[:, j % 2]), 3 * (i % 2), frees, waits)
                if not frees:
                    last.then_inc(mm, 1)

        @block.scalar
        def _(act):
            for k in range(KD):
                nc.scalar.activation(hi[:, k, :], acc[:, k, :], ACT.Copy, scale=core.g2[:, k:k + 1]).then_inc(nhi, 1)
            act.wait_ge(var, 1)
            nc.scalar.activation(rs[:], rs[:], ACT.Sqrt).then_inc(std, 1)
            for j in range(J):
                for tile in range(2):
                    v = 2 * j + tile
                    act.wait_ge(scl, v + 1)
                    nc.scalar.activation(sg[:], sg[:], ACT.Silu).then_inc(sil, 1)
                    act.wait_ge(mul, v + 1)
                    if j >= 2:
                        complete(act, ("dn", j - 2, 7))
                    nc.scalar.activation(fh[:, j % 2, tile, :], sg[:], ACT.Copy).then_inc(his, 1)

        @block.vector
        def _(dve):
            ch = core.dve

            def split(v):
                j, tile = divmod(v, 2)
                gate, up = ("gu", j, 2 * tile), ("gu", j, 2 * tile + 1)
                complete(dve, gate)
                if v >= 1:
                    dve.wait_ge(los, v)
                nc.vector.tensor_tensor(seg3(sg[:]), seg3(rs[:]), res(index[gate]), ALU.mult).then_inc(scl, 1)
                dve.wait_ge(sil, v + 1)
                ch.link(nc.vector.tensor_tensor(sg[:], sg[:], rs[:], ALU.mult))
                complete(dve, up)
                nc.vector.tensor_tensor(seg3(sg[:]), seg3(sg[:]), res(index[up]), ALU.mult).then_inc(mul, 1)
                dve.wait_ge(his, v + 1)
                nc.vector.tensor_tensor(fl[:, j % 2, tile, :], sg[:], fh[:, j % 2, tile, :].bitcast(F32),
                                        ALU.subtract).then_inc(los, 1)

            dve.wait_ge(tot, 1)
            nc.vector.tensor_scalar(seg3(rs[:]), ps[:, 3:6, 0:SEG], 1.0 / D, EPS, ALU.mult, ALU.add).then_inc(var, 1)
            for k in range(KD):
                dve.wait_ge(nhi, k + 1)
                nc.vector.scalar_tensor_tensor(lo[:, k, :], acc[:, k, :], core.g2[:, k:k + 1], hi[:, k, :].bitcast(F32),
                                               ALU.mult, ALU.subtract).then_inc(nlo, 1)
            dve.wait_ge(std, 1)
            ch.link(nc.vector.reciprocal(rs[:], rs[:]))
            for j in range(J + 1):
                if j < J:
                    split(2 * j)
                    split(2 * j + 1)
                if j >= 1:
                    for m in range(KD):
                        x = ("dn", j - 1, m)
                        complete(dve, x)
                        if j >= 2:
                            dve.wait_ge(add, KD * (j - 2) + m + 1)
                        nc.vector.tensor_tensor(seg3(acc[:, m, :]), seg3(acc[:, m, :]), res(index[x]),
                                                ALU.add).then_inc(add, 1)


def store_output(core):
    nc, o, sem, sb, acc, ps = core.nc, core.o, core.sem, core.sb, core.acc, core.ps
    with ExitStack() as c:
        yt = sb("y_t", [P, 4, D], ctx=c)
        tr, ea, ev = sem("y_tr"), sem("y_ea"), sem("y_ev")
        out = [core.store_sem(f"y_out{i}") for i in range(4)]
        block = c.enter_context(nc.Block())

        @block.tensor
        def _(pe):
            for n in range(NT + 1):
                cols = P if n < NT else NB
                if n >= 2:
                    pe.wait_ge(ea, n - 1)
                    pe.wait_ge(ev, n - 1)
                for k in range(KD):
                    last = nc.tensor.transpose(ps[0:cols, 2 * (n % 2) + k // 4, (k % 4) * P:(k % 4 + 1) * P],
                                               acc[:, k, n * P:n * P + cols], core.ident[:])
                last.then_inc(tr, 1)

        def half(n, k):
            rows = P if n < NT else NB
            return yt[0:rows, n % 4, k * 512:(k + 1) * 512], ps[0:rows, 2 * (n % 2) + k, :]

        @block.scalar
        def _(act):
            for n in range(NT + 1):
                act.wait_ge(tr, n + 1)
                if n >= 4:
                    act.wait_ge(out[n % 4], 16 * (n // 4))
                nc.scalar.activation(*half(n, 0), ACT.Copy).then_inc(ea, 1)

        @block.vector
        def _(dve):
            for n in range(NT + 1):
                dve.wait_ge(tr, n + 1)
                if n >= 4:
                    dve.wait_ge(out[n % 4], 16 * (n // 4))
                nc.vector.tensor_copy(*half(n, 1)).then_inc(ev, 1)

        @block.sync
        def _(sp):
            for n in range(NT + 1):
                sp.wait_ge(ea, n + 1)
                sp.wait_ge(ev, n + 1)
                dst = o[0][0, n * P:(n + 1) * P, :] if n < NT else o[1].rearrange("b s d -> (b s) d")
                rows = P if n < NT else NB
                sp.dma_start(dst, yt[0:rows, n % 4, :]).then_inc(out[n % 4], 16)
            for i in range(4):
                sp.wait_ge(out[i], 16 * (NT // 4 + (i == 0)))
            sp.wait_ge(core.cache_out, 16 * len(core.copies))


def program(nc, t, o):
    with ExitStack() as top:
        core = Core(nc, t, o, top)
        with ExitStack() as ch:
            core.front(ch)
            core.ss = core.sb("ss", [P, NB, G, H], ctx=ch)
            core.sn = core.sb("sn", [NB, G, H], ctx=ch)
            core.end_phase()
            norm_input(core)
            with ExitStack() as cm:
                core.bands = core.sb("bands", [P, S], ctx=cm)
                core.neg_m = core.sb("neg_m", [8, S], ctx=cm)
                for g, att_g in ((0, None), (1, 0), (2, 1), (None, 2)):
                    project(core, g, att_g)
                    core.end_phase()
                gate_projections(core)
                core.end_phase()
            output_gates(core)
            core.end_phase()
        with ExitStack() as ca:
            core.acc = core.sb("acc", [P, KD, T], ctx=ca)
            core.g2 = core.sb("g2", [P, KD], ctx=ca)
            merge_product(core, "f", core.att_t, 4, 0)
            core.end_phase()
            merge_product(core, "m", core.hm_t, KD, KD)
            core.end_phase()
            core.ssq = core.sb("sumsq", [P, T], ctx=ca)
            output_projection(core)
            core.end_phase()
            core.h2hi = core.sb("h2hi", [P, KD, T], F32R, ca)
            core.h2lo = core.sb("h2lo", [P, KD, T], F32R, ca)
            ffn(core)
            core.end_phase()
            store_output(core)


def rope_tables():
    import numpy as np
    half = DH // 8
    pos = np.concatenate([np.arange(S), [PAST]]).astype(np.float32)
    freq = np.exp(np.float32(-math.log(500000.0)) * np.arange(0, 2 * half, 2, dtype=np.float32) / np.float32(2 * half))
    ang = pos[:, None] * freq[None, :].astype(np.float32)
    c, s = np.cos(ang), np.sin(ang)
    return np.concatenate([c, c, -s, s], axis=1).astype(np.float32)


def alternate_mask():
    import numpy as np
    q, k = np.arange(P)[:, None], np.arange(P)[None, :]
    return np.where((q >= k) & ((q - k) % 2 == 0), 0.0, NEG).astype(np.float32)


_INS = ["x_prompt", "x_sample", "cache_kv_w128", "cache_kv_w512", "cache_kv_w2048", "state_mlstm_C", "state_mlstm_n",
        "state_mlstm_m", "norm1_g", "w_in", "b_if", "q_norm_g", "k_norm_g", "w_att_out", "w_m_out", "w_o", "norm2_g",
        "w_gate", "w_up", "w_down"]
_OUTS = [(1, S, D), (NB, 1, D)] + [(1, min(w, S), 2, H, DH) for w in WINDOWS] + \
    [(1, H, DH, DV), (1, H, DH), (1, H)] + [(NB, w, 2, H, DH) for w in WINDOWS] + \
    [(NB, H, DH, DV), (NB, H, DH), (NB, H)]


def kernel(**inputs):
    import numpy as _np
    import concourse.bacc as _bacc
    from concourse.bass_utils import run_bass_kernel_spmd as _run

    nc = _bacc.Bacc("TRN2", target_bir_lowering=False, num_devices=1)
    arrays = {f"in_{n}": _np.ascontiguousarray(inputs[n]) for n in _INS}
    arrays["in_rope_table"], arrays["in_mask_halves"] = rope_tables(), alternate_mask()
    t = {n[3:]: nc.dram_tensor(n, a.shape, mybir.dt.from_np(a.dtype), kind="ExternalInput").ap()
         for n, a in arrays.items()}
    o = [nc.dram_tensor(f"out_{i}", s, F32, kind="ExternalOutput").ap() for i, s in enumerate(_OUTS)]
    program(nc, t, o)
    r = _run(nc, [arrays], core_ids=[0])
    return tuple(r.results[0][f"out_{i}"] for i in range(len(_OUTS)))
```
